# Optimizing a Trainium2 kernel written in Bass

```python
import math
import jax, jax.numpy as jnp
from jax import lax
import numpy as np

D_MODEL = 1024
BATCH = 1
SEQ = 512
DEPTH = 2

GRID_W = 64
CTX_LEN = 256
N_MIXERS = 2
N_SSD_LAYERS = (DEPTH + N_MIXERS - 1) // N_MIXERS
N_ATTN_LAYERS = DEPTH // N_MIXERS
EPS = 1e-6
SSD_EXPAND = 2
D_INNER = SSD_EXPAND * D_MODEL
SSD_HEADDIM = 64
SSD_HEADS = D_INNER // SSD_HEADDIM
SSD_GROUPS = 8
SSD_HPG = SSD_HEADS // SSD_GROUPS
D_STATE = 128
CONV_W = 5
SSD_CHUNK = 128
CONV_DIM = D_INNER + 2 * SSD_GROUPS * D_STATE
SSD_IN_DIM = 2 * D_INNER + 2 * SSD_GROUPS * D_STATE + 2 * SSD_HEADS
HEAD_DIM = 64
N_Q_HEADS = D_MODEL // HEAD_DIM
N_KV_HEADS = 4
Q_PER_KV = N_Q_HEADS // N_KV_HEADS
D_ATTN = N_Q_HEADS * HEAD_DIM
QKV_DIM = (N_Q_HEADS + 2 * N_KV_HEADS) * HEAD_DIM
ROPE_AXIS_DIM = HEAD_DIM // 2
ROPE_THETA = 10000.0
Q_BLOCK = 128
N_EXPERTS = 16
D_EXPERT = D_MODEL
EC_CAPACITY = 2


def rmsnorm(x, w):
    xf = x.astype(jnp.float32)
    y = xf * lax.rsqrt(jnp.mean(xf * xf, axis=-1, keepdims=True) + EPS)
    return (y * w.astype(jnp.float32)).astype(x.dtype)

def dwconv_centred(u, w, b):
    out = lax.conv_general_dilated(
        u, w[:, None, :].astype(u.dtype), window_strides=(1,),
        padding=[(CONV_W // 2, CONV_W // 2)],
        dimension_numbers=('NWC', 'WIO', 'NWC'), feature_group_count=u.shape[-1])
    return out + b.astype(u.dtype)

def ssd_chunked(xs, dt, A, Bm, Cm, h0):
    b, L = xs.shape[:2]
    Q = SSD_CHUNK
    nc = L // Q
    x = xs.reshape(b, nc, Q, SSD_GROUPS, SSD_HPG, SSD_HEADDIM)
    dtc = dt.reshape(b, nc, Q, SSD_GROUPS, SSD_HPG)
    Bc = Bm.reshape(b, nc, Q, SSD_GROUPS, D_STATE)
    Cc = Cm.reshape(b, nc, Q, SSD_GROUPS, D_STATE)
    a = jnp.moveaxis(dtc * A.reshape(SSD_GROUPS, SSD_HPG), 2, -1)
    acum = jnp.cumsum(a, axis=-1)
    tri = jnp.tril(jnp.ones((Q, Q), dtype=bool))
    seg = jnp.exp(jnp.where(tri, acum[..., :, None] - acum[..., None, :], -jnp.inf))
    xdt = x * dtc[..., None].astype(x.dtype)
    cb = jnp.einsum('bclgn,bcsgn->bcgls', Cc, Bc)
    y_diag = jnp.einsum('bcgrls,bcsgrp->bclgrp', cb[:, :, :, None] * seg, xdt)
    decay_end = jnp.exp(acum[..., -1:] - acum)
    states = jnp.einsum('bcsgn,bcgrs,bcsgrp->bcgrpn', Bc, decay_end, xdt)
    chunk_decay = jnp.exp(acum[..., -1])

    def step(h, inp):
        dec, st = inp
        return dec[..., None, None] * h + st, h

    h_last, h_prev = lax.scan(step, h0, (jnp.moveaxis(chunk_decay, 1, 0), jnp.moveaxis(states, 1, 0)))
    h_prev = jnp.moveaxis(h_prev, 0, 1)
    y_off = jnp.einsum('bclgn,bcgrpn,bcgrl->bclgrp', Cc, h_prev, jnp.exp(acum))
    y = (y_diag + y_off).reshape(b, L, SSD_HEADS, SSD_HEADDIM)
    return y, h_last

def ssd_mixer(h_ctx, h_lat, in_w, conv_w, conv_b, dt_bias, A_log, D_skip, norm_w, out_w, ctx_out):
    def project(u):
        b, L = u.shape[:2]
        z, xbc, dtr = jnp.split(u @ in_w, [D_INNER, D_INNER + CONV_DIM], axis=-1)
        xbc = jax.nn.silu(dwconv_centred(xbc, conv_w, conv_b))
        xs, Bm, Cm = jnp.split(xbc, [D_INNER, D_INNER + SSD_GROUPS * D_STATE], axis=-1)
        dt = jax.nn.softplus(dtr.astype(jnp.float32).reshape(b, L, 2, SSD_HEADS) + dt_bias)
        return (z, xs.reshape(b, L, SSD_HEADS, SSD_HEADDIM),
                Bm.reshape(b, L, SSD_GROUPS, D_STATE), Cm.reshape(b, L, SSD_GROUPS, D_STATE), dt)

    zc, xc, Bc, Cc, dtc = project(h_ctx)
    zl, xl, Bl, Cl, dtl = project(h_lat)
    A = -jnp.exp(A_log.astype(jnp.float32))
    b = h_lat.shape[0]
    h0 = jnp.zeros((b, SSD_GROUPS, SSD_HPG, SSD_HEADDIM, D_STATE), jnp.float32)
    flip = lambda t: jnp.flip(t, axis=1)
    yc_f, hc_f = ssd_chunked(xc, dtc[:, :, 0], A[0], Bc, Cc, h0)
    yl_f, _ = ssd_chunked(xl, dtl[:, :, 0], A[0], Bl, Cl, hc_f)
    yc_b, hc_b = ssd_chunked(flip(xc), flip(dtc[:, :, 1]), A[1], flip(Bc), flip(Cc), h0)
    yl_b, _ = ssd_chunked(flip(xl), flip(dtl[:, :, 1]), A[1], flip(Bl), flip(Cl), hc_b)

    def finish(y_f, y_b, xs, z):
        bb, L = xs.shape[:2]
        y = y_f + flip(y_b) + D_skip[:, None] * xs
        y = y.reshape(bb, L, D_INNER).astype(z.dtype)
        return rmsnorm(y * jax.nn.silu(z), norm_w) @ out_w

    out_lat = finish(yl_f, yl_b, xl, zl)
    out_ctx = finish(yc_f, yc_b, xc, zc) if ctx_out else None
    return out_ctx, out_lat

def rope_2d(t, cos, sin):
    half = t.shape[-1] // 2
    t1, t2 = t[..., :half], t[..., half:]
    return jnp.concatenate([t1 * cos - t2 * sin, t2 * cos + t1 * sin], axis=-1)

def attn_mixer(h_ctx, h_lat, qkv_w, q_norm_w, k_norm_w, out_w, cos, sin, ctx_out):
    scale = 1.0 / math.sqrt(HEAD_DIM)

    def project(u):
        b, L = u.shape[:2]
        q, k, v = jnp.split(u @ qkv_w, [D_ATTN, D_ATTN + N_KV_HEADS * HEAD_DIM], axis=-1)
        q = rmsnorm(q.reshape(b, L, N_KV_HEADS, Q_PER_KV, HEAD_DIM), q_norm_w)
        k = rmsnorm(k.reshape(b, L, N_KV_HEADS, HEAD_DIM), k_norm_w)
        return q, k, v.reshape(b, L, N_KV_HEADS, HEAD_DIM)

    qc, kc, vc = project(h_ctx)
    ql, kl, vl = project(h_lat)
    cos = cos.astype(ql.dtype)
    sin = sin.astype(ql.dtype)
    ql = rope_2d(ql, cos[:, None, None], sin[:, None, None])
    kl = rope_2d(kl, cos[:, None], sin[:, None])
    k_all = jnp.concatenate([kl, kc], axis=1)
    v_all = jnp.concatenate([vl, vc], axis=1)

    def attend(q_blk, k, v):
        s = jnp.einsum('bqkgd,bskd->bkgqs', q_blk, k, preferred_element_type=jnp.float32) * scale
        p = jax.nn.softmax(s, axis=-1).astype(v.dtype)
        return jnp.einsum('bkgqs,bskd->bqkgd', p, v)

    b, S = h_lat.shape[:2]
    nb = S // Q_BLOCK
    qb = jnp.moveaxis(ql.reshape(b, nb, Q_BLOCK, N_KV_HEADS, Q_PER_KV, HEAD_DIM), 1, 0)
    o = lax.map(lambda q_blk: attend(q_blk, k_all, v_all), qb)
    out_lat = jnp.moveaxis(o, 0, 1).reshape(b, S, D_ATTN) @ out_w
    out_ctx = None
    if ctx_out:
        bc, Lc = h_ctx.shape[:2]
        out_ctx = attend(qc, kc, vc).reshape(bc, Lc, D_ATTN) @ out_w
    return out_ctx, out_lat

def moe_ec(h, router_w, w1, w3, w2):
    b, T, _ = h.shape
    cap = EC_CAPACITY * T // N_EXPERTS
    logits = jnp.einsum('btd,de->bte', h, router_w, preferred_element_type=jnp.float32)
    aff = jax.nn.softmax(logits, axis=-1)
    gate, idx = lax.top_k(jnp.swapaxes(aff, 1, 2), cap)
    bidx = jnp.arange(b)[:, None, None]
    xg = h[bidx, idx]
    a = jnp.einsum('becd,edf->becf', xg, w1)
    g = jnp.einsum('becd,edf->becf', xg, w3)
    y = jnp.einsum('becf,efd->becd', jax.nn.silu(a) * g, w2)
    y = y * gate[..., None].astype(y.dtype)
    return jnp.zeros_like(h).at[bidx, idx].add(y.astype(h.dtype))

def first_inputs(seed: int = 0) -> dict:
    key = jax.random.key(seed)
    ks = jax.random.split(key, 26)
    f32 = jnp.float32
    nrm = lambda k, shape, s: jax.random.normal(k, shape, f32) * s
    dt0 = jnp.exp(jax.random.uniform(ks[11], (N_SSD_LAYERS, 2, SSD_HEADS), f32, math.log(1e-3), math.log(1e-1)))
    return {
        "x": nrm(ks[0], (BATCH, SEQ, D_MODEL), 1.0),
        "c": nrm(ks[1], (BATCH, D_MODEL), 1.0),
        "ctx": nrm(ks[2], (BATCH, CTX_LEN, D_MODEL), 1.0),
        "c_ctx": nrm(ks[3], (D_MODEL,), 1.0),
        "ada_w": nrm(ks[4], (DEPTH, D_MODEL, 6 * D_MODEL), D_MODEL ** -0.5),
        "ada_b": nrm(ks[5], (DEPTH, 6 * D_MODEL), 0.02),
        "norm1_w": 1.0 + nrm(ks[6], (DEPTH, D_MODEL), 0.02),
        "norm2_w": 1.0 + nrm(ks[7], (DEPTH, D_MODEL), 0.02),
        "ssd_in_w": nrm(ks[8], (N_SSD_LAYERS, D_MODEL, SSD_IN_DIM), D_MODEL ** -0.5),
        "ssd_conv_w": nrm(ks[9], (N_SSD_LAYERS, CONV_W, CONV_DIM), CONV_W ** -0.5),
        "ssd_conv_b": nrm(ks[10], (N_SSD_LAYERS, CONV_DIM), 0.02),
        "ssd_dt_bias": dt0 + jnp.log(-jnp.expm1(-dt0)),
        "ssd_A_log": jnp.log(jax.random.uniform(ks[12], (N_SSD_LAYERS, 2, SSD_HEADS), f32, 1.0, 16.0)),
        "ssd_D": 1.0 + nrm(ks[13], (N_SSD_LAYERS, SSD_HEADS), 0.1),
        "ssd_norm_w": 1.0 + nrm(ks[14], (N_SSD_LAYERS, D_INNER), 0.02),
        "ssd_out_w": nrm(ks[15], (N_SSD_LAYERS, D_INNER, D_MODEL), D_INNER ** -0.5),
        "attn_qkv_w": nrm(ks[16], (N_ATTN_LAYERS, D_MODEL, QKV_DIM), D_MODEL ** -0.5),
        "attn_q_norm_w": 1.0 + nrm(ks[17], (N_ATTN_LAYERS, HEAD_DIM), 0.02),
        "attn_k_norm_w": 1.0 + nrm(ks[18], (N_ATTN_LAYERS, HEAD_DIM), 0.02),
        "attn_out_w": nrm(ks[19], (N_ATTN_LAYERS, D_ATTN, D_MODEL), D_ATTN ** -0.5),
        "moe_router_w": nrm(ks[20], (DEPTH, D_MODEL, N_EXPERTS), D_MODEL ** -0.5),
        "moe_w1": nrm(ks[21], (DEPTH, N_EXPERTS, D_MODEL, D_EXPERT), D_MODEL ** -0.5),
        "moe_w3": nrm(ks[22], (DEPTH, N_EXPERTS, D_MODEL, D_EXPERT), D_MODEL ** -0.5),
        "moe_w2": nrm(ks[23], (DEPTH, N_EXPERTS, D_EXPERT, D_MODEL), D_EXPERT ** -0.5),
        "final_norm_w": 1.0 + nrm(ks[24], (D_MODEL,), 0.02),
    }

def first_block(x, c, ctx, c_ctx, ada_w, ada_b, norm1_w, norm2_w, ssd_in_w, ssd_conv_w, ssd_conv_b,
              ssd_dt_bias, ssd_A_log, ssd_D, ssd_norm_w, ssd_out_w, attn_qkv_w, attn_q_norm_w,
              attn_k_norm_w, attn_out_w, moe_router_w, moe_w1, moe_w3, moe_w2, final_norm_w):
    S = x.shape[1]
    rows = S // GRID_W
    row = jnp.repeat(jnp.arange(rows), GRID_W, total_repeat_length=S).astype(jnp.float32)
    col = jnp.tile(jnp.arange(GRID_W), rows).astype(jnp.float32)
    inv_freq = ROPE_THETA ** (-jnp.arange(0, ROPE_AXIS_DIM, 2, dtype=jnp.float32) / ROPE_AXIS_DIM)
    ang = jnp.concatenate([row[:, None] * inv_freq, col[:, None] * inv_freq], axis=-1)
    cos, sin = jnp.cos(ang), jnp.sin(ang)

    silu_c = jax.nn.silu(c)
    silu_cc = jax.nn.silu(c_ctx)
    for i in range(DEPTH):
        last = i == DEPTH - 1
        j = i // N_MIXERS
        sh1l, sc1l, g1l, sh2l, sc2l, g2l = [m[:, None, :] for m in jnp.split(silu_c @ ada_w[i] + ada_b[i], 6, axis=-1)]
        sh1c, sc1c, g1c, sh2c, sc2c, g2c = jnp.split(silu_cc @ ada_w[i] + ada_b[i], 6, axis=-1)
        h_lat = rmsnorm(x, norm1_w[i]) * (1.0 + sc1l) + sh1l
        h_ctx = rmsnorm(ctx, norm1_w[i]) * (1.0 + sc1c) + sh1c
        if i % N_MIXERS == 0:
            o_ctx, o_lat = ssd_mixer(h_ctx, h_lat, ssd_in_w[j], ssd_conv_w[j], ssd_conv_b[j], ssd_dt_bias[j],
                                     ssd_A_log[j], ssd_D[j], ssd_norm_w[j], ssd_out_w[j], not last)
        else:
            o_ctx, o_lat = attn_mixer(h_ctx, h_lat, attn_qkv_w[j], attn_q_norm_w[j], attn_k_norm_w[j],
                                      attn_out_w[j], cos, sin, not last)
        x = x + g1l * o_lat
        x = x + g2l * moe_ec(rmsnorm(x, norm2_w[i]) * (1.0 + sc2l) + sh2l,
                             moe_router_w[i], moe_w1[i], moe_w3[i], moe_w2[i])
        if not last:
            ctx = ctx + g1c * o_ctx
            ctx = ctx + g2c * moe_ec(rmsnorm(ctx, norm2_w[i]) * (1.0 + sc2c) + sh2c,
                                     moe_router_w[i], moe_w1[i], moe_w3[i], moe_w2[i])
    return rmsnorm(x, final_norm_w)


DEPTH_2 = 1

CHUNK = 64
N_MEM = 256
BRANCH_WIDTH = 512
N_BRANCH = 3
LRU_WIDTH = BRANCH_WIDTH
LRU_BLOCKS = 8
LRU_BLOCK = LRU_WIDTH // LRU_BLOCKS
CONV_WIDTH = 4
LRU_C = 8.0
POOL_WIDTH = BRANCH_WIDTH
POOL_WINDOWS = (2, 4, 8, 16)
POOL_GROUPS = len(POOL_WINDOWS)
POOL_GROUP = POOL_WIDTH // POOL_GROUPS
ATT_HEADS = 8
ATT_HEAD_DIM = 64
ATT_WIDTH = ATT_HEADS * ATT_HEAD_DIM
IDX_HEADS = 8
IDX_DIM = 64
MAX_TOPK = 256
MEM_HEADS = 4
MEM_HEAD_DIM = 128
MEM_WIDTH = MEM_HEADS * MEM_HEAD_DIM
D_FF = ((8 * D_MODEL // 3 + 255) // 256) * 256
RMS_EPS = 1e-6

IN_SIZES = (LRU_WIDTH,
            LRU_WIDTH,
            POOL_WIDTH,
            ATT_WIDTH,
            ATT_HEAD_DIM,
            ATT_HEAD_DIM,
            IDX_HEADS * IDX_DIM,
            IDX_DIM,
            IDX_HEADS,
            N_BRANCH * D_MODEL)
D_IN = sum(IN_SIZES)


def rms_norm(x, g):
    xf = x.astype(jnp.float32)
    y = xf * lax.rsqrt(jnp.mean(xf * xf, axis=-1, keepdims=True) + RMS_EPS)
    return (y * g.astype(jnp.float32)).astype(x.dtype)

def split_columns(h, sizes):
    parts, start = [], 0
    for n in sizes:
        parts.append(h[..., start:start + n])
        start += n
    return parts

def causal_depthwise_conv(x, w, b):
    c = x.shape[-1]
    y = lax.conv_general_dilated(x, w[:, None, :].astype(x.dtype), window_strides=(1,),
                                 padding=[(w.shape[0] - 1, 0)],
                                 dimension_numbers=('NWC', 'WIO', 'NWC'),
                                 feature_group_count=c)
    return y + b

def rg_lru(x, w_a, b_a, w_x, b_x, a_param):
    bsz, s, _ = x.shape
    xb = x.reshape(bsz, s, LRU_BLOCKS, LRU_BLOCK)
    r = jax.nn.sigmoid((jnp.einsum('bshi,hij->bshj', xb, w_a).reshape(bsz, s, LRU_WIDTH) + b_a).astype(jnp.float32))
    i = jax.nn.sigmoid((jnp.einsum('bshi,hij->bshj', xb, w_x).reshape(bsz, s, LRU_WIDTH) + b_x).astype(jnp.float32))
    log_a = -LRU_C * r * jax.nn.softplus(-a_param.astype(jnp.float32))
    a = jnp.exp(log_a)
    mult = jnp.sqrt(jnp.maximum(1.0 - jnp.exp(2.0 * log_a), 0.0))
    u = x.astype(jnp.float32) * i * mult

    def combine(left, right):
        return left[0] * right[0], right[0] * left[1] + right[1]

    _, h = lax.associative_scan(combine, (a, u), axis=1)
    return h.astype(x.dtype)

def multiscale_pool(p, w_pool, pool_scale):
    bsz, s, _ = p.shape
    pf = p.astype(jnp.float32).reshape(bsz, s, POOL_GROUPS, POOL_GROUP)
    cs = jnp.pad(jnp.cumsum(pf, axis=1), ((0, 0), (1, 0), (0, 0), (0, 0)))
    t = jnp.arange(s)
    means = []
    for g, w in enumerate(POOL_WINDOWS):
        start = jnp.maximum(t + 1 - w, 0)
        win_sum = cs[:, 1:, g] - cs[:, start, g]
        count = (t + 1 - start).astype(jnp.float32)[None, :, None]
        means.append(win_sum / count)
    pooled = jnp.stack(means, axis=2) - pf
    mixed = jnp.einsum('bsgc,gcd->bsgd', pooled, w_pool.astype(jnp.float32)).reshape(bsz, s, POOL_WIDTH)
    return (mixed * pool_scale.astype(jnp.float32)).astype(p.dtype)

def dsa_attention(q, k, v, q_idx, k_idx, w_idx):
    bsz, s = q.shape[:2]
    top_k = min(MAX_TOPK, s // 4)
    nb = s // Q_BLOCK
    key_chunk = jnp.arange(s) // CHUNK
    k_idx_f = k_idx.astype(jnp.float32)

    def to_blocks(a):
        return jnp.moveaxis(a.reshape(bsz, nb, Q_BLOCK, *a.shape[2:]), 1, 0)

    def one_block(args):
        qb, qib, wb, pos = args
        q_chunk = pos // CHUNK
        admissible = key_chunk[None, :] <= q_chunk[:, None]
        logits = jnp.einsum('bqhd,bsd->bqhs', qib.astype(jnp.float32), k_idx_f) * (IDX_DIM ** -0.5)
        score = jnp.einsum('bqh,bqhs->bqs', wb.astype(jnp.float32) * (IDX_HEADS ** -0.5), jax.nn.relu(logits))
        score = jnp.where(admissible[None], score, -jnp.inf)
        _, sel = lax.top_k(score, top_k)
        kg = jax.vmap(lambda kk, ii: kk[ii])(k, sel)
        vg = jax.vmap(lambda vv, ii: vv[ii])(v, sel)
        valid = key_chunk[sel] <= q_chunk[None, :, None]
        att = jnp.einsum('bqhd,bqkd->bqhk', qb, kg).astype(jnp.float32) * (ATT_HEAD_DIM ** -0.5)
        att = jnp.where(valid[:, :, None, :], att, -jnp.inf)
        prob = jax.nn.softmax(att, axis=-1).astype(vg.dtype)
        return jnp.einsum('bqhk,bqkd->bqhd', prob, vg)

    q_pos = jnp.arange(s).reshape(nb, Q_BLOCK)
    out = lax.map(one_block, (to_blocks(q), to_blocks(q_idx), to_blocks(w_idx), q_pos))
    return jnp.moveaxis(out, 0, 1).reshape(bsz, s, ATT_WIDTH)

def memory_cross_attention(h, m, w_q, w_kv, w_o):
    bsz, s, _ = h.shape
    q = (h @ w_q).reshape(bsz, s, MEM_HEADS, MEM_HEAD_DIM)
    k, v = jnp.split(m @ w_kv, 2, axis=-1)
    k = k.reshape(bsz, -1, MEM_HEADS, MEM_HEAD_DIM)
    v = v.reshape(bsz, -1, MEM_HEADS, MEM_HEAD_DIM)
    att = jnp.einsum('bshd,bmhd->bhsm', q, k).astype(jnp.float32) * (MEM_HEAD_DIM ** -0.5)
    prob = jax.nn.softmax(att, axis=-1).astype(v.dtype)
    o = jnp.einsum('bhsm,bmhd->bshd', prob, v).reshape(bsz, s, MEM_WIDTH)
    return o @ w_o

def second_inputs(seed: int = 0) -> dict:
    key = jax.random.key(seed)
    ks = iter(jax.random.split(key, 40))

    def nrm(shape, scale):
        return jax.random.normal(next(ks), shape, jnp.float32) * scale

    def gain(shape):
        return 1.0 + nrm(shape, 0.02)

    L = DEPTH_2
    u = jax.random.uniform(next(ks), (L, LRU_WIDTH), jnp.float32, 0.9, 0.999)
    a0 = u ** (1.0 / LRU_C)
    lru_a_param = jnp.log(a0) - jnp.log1p(-a0)
    return {
        'x': nrm((BATCH, SEQ, D_MODEL), 1.0),
        'mem': nrm((BATCH, N_MEM, D_MODEL), 1.0),
        'g_mix_pre': gain((L, D_MODEL)),
        'w_in': nrm((L, D_MODEL, D_IN), D_MODEL ** -0.5),
        'conv_w': nrm((L, CONV_WIDTH, LRU_WIDTH), CONV_WIDTH ** -0.5),
        'conv_b': nrm((L, LRU_WIDTH), 0.02),
        'lru_w_a': nrm((L, LRU_BLOCKS, LRU_BLOCK, LRU_BLOCK), LRU_BLOCK ** -0.5),
        'lru_b_a': nrm((L, LRU_WIDTH), 0.02),
        'lru_w_x': nrm((L, LRU_BLOCKS, LRU_BLOCK, LRU_BLOCK), LRU_BLOCK ** -0.5),
        'lru_b_x': nrm((L, LRU_WIDTH), 0.02),
        'lru_a_param': lru_a_param,
        'w_pool': nrm((L, POOL_GROUPS, POOL_GROUP, POOL_GROUP), POOL_GROUP ** -0.5),
        'pool_scale': gain((L, POOL_WIDTH)),
        'w_branch': nrm((L, N_BRANCH, BRANCH_WIDTH, D_MODEL), BRANCH_WIDTH ** -0.5),
        'b_gate': nrm((L, N_BRANCH, D_MODEL), 0.02),
        'w_out': nrm((L, D_MODEL, D_MODEL), D_MODEL ** -0.5),
        'g_mix_post': gain((L, D_MODEL)),
        'g_mem_pre': gain((L, D_MODEL)),
        'g_mem_kv': gain((L, D_MODEL)),
        'w_mem_q': nrm((L, D_MODEL, MEM_WIDTH), D_MODEL ** -0.5),
        'w_mem_kv': nrm((L, D_MODEL, 2 * MEM_WIDTH), D_MODEL ** -0.5),
        'w_mem_o': nrm((L, MEM_WIDTH, D_MODEL), MEM_WIDTH ** -0.5),
        'g_mem_post': gain((L, D_MODEL)),
        'g_ffn_pre': gain((L, D_MODEL)),
        'w_ffn_in': nrm((L, D_MODEL, 2 * D_FF), D_MODEL ** -0.5),
        'w_ffn_out': nrm((L, D_FF, D_MODEL), D_FF ** -0.5),
        'g_ffn_post': gain((L, D_MODEL)),
    }

def second_block(x, mem, g_mix_pre, w_in, conv_w, conv_b, lru_w_a, lru_b_a, lru_w_x, lru_b_x,
              lru_a_param, w_pool, pool_scale, w_branch, b_gate, w_out, g_mix_post,
              g_mem_pre, g_mem_kv, w_mem_q, w_mem_kv, w_mem_o, g_mem_post,
              g_ffn_pre, w_ffn_in, w_ffn_out, g_ffn_post):
    bsz, s, _ = x.shape
    for l in range(DEPTH_2):
        h = rms_norm(x, g_mix_pre[l])
        (lru_x, lru_gate, pool_in, q, k, v, q_idx, k_idx, w_idx,
         gate_logits) = split_columns(h @ w_in[l], IN_SIZES)
        ua = causal_depthwise_conv(lru_x, conv_w[l], conv_b[l])
        ya = rg_lru(ua, lru_w_a[l], lru_b_a[l], lru_w_x[l], lru_b_x[l], lru_a_param[l]) * jax.nn.gelu(lru_gate)
        yb = multiscale_pool(pool_in, w_pool[l], pool_scale[l])
        yc = dsa_attention(q.reshape(bsz, s, ATT_HEADS, ATT_HEAD_DIM), k, v,
                           q_idx.reshape(bsz, s, IDX_HEADS, IDX_DIM), k_idx, w_idx)
        up = jnp.einsum('bsnc,ncd->bsnd', jnp.stack([ya, yb, yc], axis=2), w_branch[l])
        gates = jax.nn.sigmoid(gate_logits.reshape(bsz, s, N_BRANCH, D_MODEL) + b_gate[l])
        merged = jnp.sum(gates * up, axis=2)
        x = x + rms_norm(merged @ w_out[l], g_mix_post[l])
        h = rms_norm(x, g_mem_pre[l])
        m = rms_norm(mem, g_mem_kv[l])
        x = x + rms_norm(memory_cross_attention(h, m, w_mem_q[l], w_mem_kv[l], w_mem_o[l]), g_mem_post[l])
        h = rms_norm(x, g_ffn_pre[l])
        f_gate, f_up = jnp.split(h @ w_ffn_in[l], 2, axis=-1)
        x = x + rms_norm((jax.nn.silu(f_gate) * f_up) @ w_ffn_out[l], g_ffn_post[l])
    return x


def setup_inputs(seed=0):
    out = dict(first_inputs(seed))
    for name, value in second_inputs(seed + 1).items():
        if name != "x":
            out[name + "_2"] = value
    return out


def reference(
    x, c, ctx, c_ctx, ada_w, ada_b, norm1_w, norm2_w, ssd_in_w, ssd_conv_w, ssd_conv_b,
    ssd_dt_bias, ssd_A_log, ssd_D, ssd_norm_w, ssd_out_w, attn_qkv_w, attn_q_norm_w,
    attn_k_norm_w, attn_out_w, moe_router_w, moe_w1, moe_w3, moe_w2, final_norm_w, mem_2,
    g_mix_pre_2, w_in_2, conv_w_2, conv_b_2, lru_w_a_2, lru_b_a_2, lru_w_x_2, lru_b_x_2,
    lru_a_param_2, w_pool_2, pool_scale_2, w_branch_2, b_gate_2, w_out_2, g_mix_post_2,
    g_mem_pre_2, g_mem_kv_2, w_mem_q_2, w_mem_kv_2, w_mem_o_2, g_mem_post_2, g_ffn_pre_2,
    w_ffn_in_2, w_ffn_out_2, g_ffn_post_2,
):
    x = first_block(
        x, c, ctx, c_ctx, ada_w, ada_b, norm1_w, norm2_w, ssd_in_w, ssd_conv_w, ssd_conv_b,
        ssd_dt_bias, ssd_A_log, ssd_D, ssd_norm_w, ssd_out_w, attn_qkv_w, attn_q_norm_w,
        attn_k_norm_w, attn_out_w, moe_router_w, moe_w1, moe_w3, moe_w2, final_norm_w,
    )
    return second_block(
        x, mem_2, g_mix_pre_2, w_in_2, conv_w_2, conv_b_2, lru_w_a_2, lru_b_a_2, lru_w_x_2,
        lru_b_x_2, lru_a_param_2, w_pool_2, pool_scale_2, w_branch_2, b_gate_2, w_out_2,
        g_mix_post_2, g_mem_pre_2, g_mem_kv_2, w_mem_q_2, w_mem_kv_2, w_mem_o_2, g_mem_post_2,
        g_ffn_pre_2, w_ffn_in_2, w_ffn_out_2, g_ffn_post_2,
    )


_drawn_inputs = setup_inputs


def setup_inputs(seed=0):
    import zlib

    import numpy as np

    out = dict(_drawn_inputs(seed))
    spreads = {}
    factors = {'attn_q_norm_w': 8.0,
     'attn_k_norm_w': 8.0,
     'lru_b_a_2': 22.642,
     'lru_b_x_2': 8.0,
     'pool_scale_2': 4.909,
     'b_gate_2': 8.0,
     'g_mix_post_2': 3.454,
     'g_mem_pre_2': 4.44,
     'g_mem_kv_2': 2.959,
     'g_mem_post_2': 13.894,
     'g_ffn_pre_2': 11.422,
     'g_ffn_post_2': 22.021}
    for name, (base, spread) in spreads.items():
        noise = np.random.default_rng([zlib.crc32(name.encode()), seed]).standard_normal(out[name].shape)
        drawn = base * np.exp(spread * noise) if base else spread * noise
        out[name] = __import__('jax').numpy.asarray(drawn.astype(out[name].dtype))
    for name, factor in factors.items():
        out[name] = (out[name] * factor).astype(out[name].dtype)
    return out
```

```python
from contextlib import ExitStack

import numpy as np

import concourse.bass as bass
from concourse import mybir

F32 = mybir.dt.float32
F32R = mybir.dt.float32r
BF16 = mybir.dt.bfloat16
ALU = mybir.AluOpType
ACT = mybir.ActivationFunctionType
AX = mybir.AxisListType

P = 128
D = 1024
KD = D // P
LAT, CTX = 512, 256
NL, NC = LAT // P, CTX // P
NT = NL + NC
TOK = LAT + CTX
EPS = 1e-6
HALF = 512
DI = 2048
H = 32
HD = 64
G = 8
HPG = H // G
NS = 128
TAPS = 5
PADL = 2
LATP = LAT + 2 * PADL
PADW = LATP + CTX + 2 * PADL
E = 16
NEG = -3.0e38
QH, KVH = 16, 4
LRU_W = 512
TAPS2 = 4
FF = 2816
SLOTS = 3
X_END = NT * D
SLOT = 4096
AREA = 35072
CUT = 2 * HALF
BLOCKS = SLOT // CUT
CUTS = 4


def flat(ap):
    return ap.rearrange("p a b -> p (a b)")


class Ring:

    def __init__(self, env, plan):
        self.plan = plan
        self.slots = env.ring
        self.landed = env.landed
        self.done = env.marks
        self.loaded = 0
        self.marks = 0
        self.blocks = self.blocks_v = self.blocks_p = 0
        self.ends = []
        self.hi, self.lo = env.hi, env.lo
        self.high, self.low_v, self.low_p, self.used = env.cut_sems

    def view(self, k, a, b):
        return self.slots[:, k % SLOTS, 0:a * b].rearrange("p (a b) -> p a b", a=a)

    def take(self, marks):
        first, before = len(self.ends), self.marks
        for m in marks:
            self.marks += m
            self.ends.append([(self.done, self.marks)])
        return first, before

    def take_split(self, blocks):
        first, before = len(self.ends), (self.blocks, self.blocks_v, self.blocks_p)
        for n in blocks:
            self.blocks += n
            self.blocks_v += min(n, 3)
            self.blocks_p += n // 4
            self.ends.append([(self.low_v, self.blocks_v)] + ([(self.low_p, self.blocks_p)] if n == 4 else []))
        return (first, *before)

    def load_to(self, sp, end):
        while self.loaded < min(end, len(self.plan)):
            k = self.loaded
            if k >= SLOTS:
                for sem, count in self.ends[k - SLOTS]:
                    sp.wait_ge(sem, count)
            src = self.plan[k]
            sp.dma_start(self.view(k, src.shape[1], src.shape[2]), src).then_inc(self.landed[k % SLOTS], 16)
            self.loaded += 1

    def wait(self, pe, k):
        pe.wait_ge(self.landed[k % SLOTS], 16 * (k // SLOTS + 1))


class Stage:

    def __init__(self, env, base):
        self.env = env
        self.at = base

    def __enter__(self):
        self.es = ExitStack()
        self.bank = self.env.sem_banks[self.env.stage % 2]
        self.other = self.env.sem_banks[(self.env.stage + 1) % 2]
        self.env.stage += 1
        self.n = 0
        return self

    def sb(self, name, shape):
        size = int(np.prod(shape[1:]))
        self.at += size
        assert self.at <= AREA, (name, self.at)
        return carve(self.env, self.at - size, shape)

    def sbr(self, name, shape):
        self.at = -(-self.at // 8) * 8
        self.at += int(np.prod(shape[1:]))
        return carve_r(self.env, f"{name}_{self.env.stage}", self.at - int(np.prod(shape[1:])), shape)

    def sem(self, name):
        num = self.bank[self.n]
        self.n += 1
        return self.es.enter_context(self.env.nc.semaphore(f"{name}_{self.env.stage}", num))

    def block(self):
        b = self.es.enter_context(self.env.nc.Block())
        other = self.other

        @b.gpsimd
        def _(pool):
            pool.sem_clear(range(other[0], other[-1] + 1))

        return b

    def __exit__(self, *a):
        return self.es.__exit__(*a)


def carve(env, at, shape):
    size = int(np.prod(shape[1:]))
    assert at + size <= AREA
    v = env.area[0:shape[0], at:at + size]
    if len(shape) == 3:
        v = v.rearrange("p (a b) -> p a b", a=shape[1])
    elif len(shape) == 4:
        v = v.rearrange("p (a b c) -> p a b c", a=shape[1], b=shape[2])
    return v


def carve_r(env, name, at, shape):
    size = int(np.prod(shape[1:]))
    assert at + size <= AREA and at % 8 == 0, (name, at, size)
    env.tiles += 1
    return env.nc.alloc_sbuf_tensor_at(f"{name}_{env.tiles}", shape, F32R, offset=env.area_at + 4 * at)[:]


class Env:
    pass


PARAM_ROWS = [
    ("c", 8), ("c_ctx", 8), ("norm1_w", 16), ("norm2_w", 16), ("ssd_norm_w", 16), ("g_mix_pre_2", 8),
    ("g_mem_pre_2", 8), ("g_mem_kv_2", 8), ("g_ffn_pre_2", 8), ("ssd_conv_b", 32),
    ("ssd_conv_w", 160), ("conv_w_2", 16), ("conv_b_2", 4), ("lru_b_a_2", 4), ("lru_b_x_2", 4),
    ("lru_a_param_2", 4), ("pool_scale_2", 4), ("b_gate_2", 24),
]


def flat_rows(ap):
    names = "abcdef"[:len(ap.shape)]
    f = ap if len(ap.shape) == 1 else ap.rearrange(f"{' '.join(names)} -> ({' '.join(names)})")
    return f.rearrange("(r p) -> r p", p=P)


def setup(env):
    nc, ins = env.nc, env.ins
    with Stage(env, 0) as st:
        total = sum(n for _, n in PARAM_ROWS)
        tiles = -(-total // P)
        rows = st.sb("param_rows", [P, tiles, P])
        loaded, masks, turned = st.sem("rows_loaded"), st.sem("masks_made"), st.sem("rows_turned")
        copied = st.sem("columns_copied")
        pieces = []
        at = 0
        for name, n in PARAM_ROWS:
            env.col_at[name] = at
            src = flat_rows(ins[name])
            done = 0
            while done < n:
                k = min(n - done, P - at % P)
                pieces.append((src[done:done + k, :], at // P, at % P, k))
                at += k
                done += k
        block = st.block()
        ps = env.ps

        @block.sync
        def _(sp):
            sp.wait_ge(masks, 1)
            for src, t, r, k in pieces:
                sp.dma_start(rows[r:r + k, t, :], src).then_inc(loaded, 16)
            sp.dma_start(env.dtb[:], ins["ssd_dt_bias"].rearrange("a b c -> a (b c)")
                         .partition_broadcast(P)).then_inc(loaded, 16)
            env.ring_.load_to(sp, SLOTS)
            sp.wait_ge(loaded, 16 * (len(pieces) + 1))

        @block.gpsimd
        def _(pool):
            pool.memset(rows[:], 0.0).then_inc(masks, 1)
            pool.memset(env.ones[:], 1.0)
            pool.memset(env.ident[:], 0.0)
            for m in range(4):
                pool.memset(env.tri[:, m, :], 1.0)
            pool.drain()
            pool.affine_select(out=env.ident[:], in_=env.ident[:], compare_op=ALU.not_equal, fill=1.0,
                               base=0, pattern=[[-1, P]], channel_multiplier=1)
            for m, (op, mul, step) in enumerate([(ALU.is_ge, -1, 1), (ALU.is_ge, 1, -1),
                                                 (ALU.is_gt, 1, -1), (ALU.is_gt, -1, 1)]):
                pool.affine_select(out=env.tri[:, m, :], in_=env.tri[:, m, :], compare_op=op, fill=0.0,
                                   base=0, pattern=[[step, P]], channel_multiplier=mul)
            for m in range(2):
                pool.memset(env.mask_b[:, m, :], 0.0)
            pool.drain()
            pool.tensor_copy(env.ident_b[:], env.ident[:])
            for m, (mul, step) in enumerate([(-1, 1), (1, -1)]):
                pool.affine_select(out=env.mask_b[:, m, :], in_=env.mask_b[:, m, :], compare_op=ALU.is_ge, fill=-1e30,
                                   base=0, pattern=[[step, P]], channel_multiplier=mul)
            pool.iota(env.iota[:], pattern=[[1, P]], base=1, channel_multiplier=0,
                      allow_small_or_imprecise_dtypes=True)
            pool.drain()
            pool.memset(env.zero[:], 0.0).then_inc(masks, 1)

        @block.tensor
        def _(pe):
            pe.wait_ge(masks, 2)
            pe.wait_ge(loaded, 16 * (len(pieces) + 1))
            for t in range(tiles):
                pe.transpose(ps[:, t, 0:P], rows[:, t, :], env.ident[:]).then_inc(turned, 1)

        @block.vector
        def _(dve):
            for t in range(tiles):
                dve.wait_ge(turned, t + 1)
                dve.tensor_copy(env.cols[:, t * P:(t + 1) * P], ps[:, t, 0:P]).then_inc(copied, 1)

        @block.scalar
        def _(act):
            act.wait_ge(copied, 1)
            for v in range(2):
                act.activation(env.cond[:, :, v], env.cols[:, 8 * v:8 * v + 8], ACT.Silu)


def col(env, name, i=0):
    a = env.col_at[name] + i
    return env.cols[:, a:a + 1]


def modulation(env, layer):
    ps, ring = env.ps, env.ring_
    n_chunks = 12
    with Stage(env, 0 if layer == 0 else X_END) as st:
        mod = st.sb("mod_rows", [2, 6 * D])
        bias = st.sb("ada_bias", [2, 6 * D])
        bias_in, added, turned, stored = st.sem("bias_in"), st.sem("bias_added"), st.sem("mod_turned"), st.sem("mod_stored")
        first, m0 = ring.take([1] * n_chunks)
        block = st.block()

        @block.sync
        def _(sp):
            sp.dma_start(bias, env.ins["ada_b"][layer, :].partition_broadcast(2)).then_inc(bias_in, 16)
            ring.load_to(sp, first + n_chunks + SLOTS)
            sp.wait_ge(added, n_chunks)
            sp.dma_start(env.mod_dram[layer, :, :], mod).then_inc(stored, 16)
            sp.wait_ge(stored, 16)

        @block.tensor
        def _(pe):
            for n in range(n_chunks):
                if n >= 4:
                    pe.wait_ge(added, n - 3)
                ring.wait(pe, first + n)
                w = ring.view(first + n, KD, HALF)
                for k in range(KD):
                    mm = pe.matmul(ps[0:2, n % 4, :], env.cond[:, k, :], w[:, k, :], start=k == 0, stop=k == KD - 1)
                mm.then_inc(ring.done, 1)
            pe.wait_ge(added, n_chunks)
            for q, piece in enumerate((0, 1, 3, 4)):
                for k in range(KD):
                    a = piece * D + k * P
                    tr = pe.transpose(ps[:, 4, q * 16 + 2 * k:q * 16 + 2 * k + 2], mod[:, a:a + P], env.ident[0:2, 0:2])
            tr.then_inc(turned, 1)

        @block.vector
        def _(dve):
            dve.wait_ge(bias_in, 16)
            for n in range(n_chunks):
                dve.wait_ge(ring.done, m0 + n + 1)
                s = slice(n * HALF, (n + 1) * HALF)
                dve.tensor_tensor(mod[:, s], ps[0:2, n % 4, :], bias[:, s], ALU.add).then_inc(added, 1)
            dve.wait_ge(turned, 1)
            v = ps[:, 4, 0:64].rearrange("p (q k v) -> p q v k", q=4, k=KD)
            for q in range(4):
                dve.tensor_copy(env.modc[:, q, :, :], v[:, q, :, :])
            dve.drain()
            for q, name in ((1, "norm1_w"), (3, "norm2_w")):
                a = env.col_at[name] + layer * KD
                for u in range(2):
                    dve.scalar_tensor_tensor(env.modc[:, q, u, :], env.modc[:, q, u, :], 1.0, env.cols[:, a:a + KD],
                                             ALU.add, ALU.mult)


def norm_turn(env, base, src, hT, groups, width=D, token_out=None, load=None):
    ps, ring = env.ps, env.ring_
    nt = sum(g[1] for g in groups)
    kd = width // P
    with Stage(env, base) as st:
        junk = st.sb("squares", [P, width])
        ss = st.sb("mean_square", [P, nt])
        rstd = st.sb("rstd", [P, nt])
        xn = token_out if token_out is not None else st.sb("scaled", [P, nt, width])
        x_in, squared, eps_in, rooted = st.sem("x_in"), st.sem("squared"), st.sem("eps_in"), st.sem("rooted")
        scaled, turned = st.sem("rows_scaled"), st.sem("turned")
        out = [st.sem("even_features_out"), st.sem("odd_features_out")]
        t0 = groups[0][0]
        block = st.block()

        @block.sync
        def _(sp):
            if load is not None:
                for t, s in load:
                    sp.dma_start(src[:, t, :], s).then_inc(x_in, 16)
            ring.load_to(sp, len(ring.ends) + SLOTS)

        @block.scalar
        def _(act):
            for i in range(nt):
                if load is not None:
                    act.wait_ge(x_in, 16 * len(load))
                act.drain()
                act.activation(junk[:], src[:, t0 + i, :], ACT.Square, scale=float(width) ** -0.5,
                               accum_out=ss[:, i:i + 1]).then_inc(squared, 1)
            act.wait_ge(eps_in, 1)
            act.activation(rstd[:], ss[:], ACT.Sqrt).then_inc(rooted, 1)
            n = 0
            for gi, (_, m, sc, sh) in enumerate(groups):
                for k in range(kd):
                    if k % 2 == 1:
                        act.wait_ge(turned, n + 1)
                        o = groups[gi][0] * P
                        act.activation(hT[:, k, o:o + m * P], ps[:, n % 8, 0:m * P], ACT.Identity,
                                       scale=sc(k), bias=sh(k) if sh else 0.0).then_inc(out[1], 1)
                    n += 1

        @block.vector
        def _(dve):
            dve.wait_ge(squared, nt)
            dve.tensor_scalar(ss[:], ss[:], EPS, None, ALU.add).then_inc(eps_in, 1)
            dve.wait_ge(rooted, 1)
            dve.reciprocal(rstd[:], rstd[:])
            dve.drain()
            for i in range(nt):
                dve.tensor_scalar(xn[:, i, :], src[:, t0 + i, :], rstd[:, i:i + 1], None, ALU.mult).then_inc(scaled, 1)
            n = 0
            for gi, (_, m, sc, sh) in enumerate(groups):
                for k in range(kd):
                    if k % 2 == 0:
                        dve.wait_ge(turned, n + 1)
                        o = groups[gi][0] * P
                        if sh:
                            dve.tensor_scalar(hT[:, k, o:o + m * P], ps[:, n % 8, 0:m * P], sc(k), sh(k),
                                              ALU.mult, ALU.add).then_inc(out[0], 1)
                        else:
                            dve.tensor_scalar(hT[:, k, o:o + m * P], ps[:, n % 8, 0:m * P], sc(k), None,
                                              ALU.mult).then_inc(out[0], 1)
                    n += 1

        @block.tensor
        def _(pe):
            n = 0
            for first, m, _, _ in groups:
                pe.wait_ge(scaled, first - t0 + m)
                for k in range(kd):
                    if n >= 8:
                        pe.wait_ge(out[n % 2], (n - 8) // 2 + 1)
                    for j in range(m):
                        tr = pe.transpose(ps[:, n % 8, j * P:(j + 1) * P], xn[:, first - t0 + j, k * P:(k + 1) * P],
                                          env.ident[:])
                    tr.then_inc(turned, 1)
                    n += 1


def log1p_steps(dve, e, s, q, p):
    dve.tensor_scalar(p, e, 2.0, None, ALU.add)
    dve.drain()
    dve.reciprocal(q, p)
    dve.drain()
    dve.tensor_tensor(s, e, q, ALU.mult)
    dve.drain()
    dve.tensor_tensor(q, s, s, ALU.mult)
    dve.drain()
    dve.tensor_scalar(p, q, 1.0 / 15, None, ALU.mult)
    dve.drain()
    for odd in (13, 11, 9, 7, 5, 3):
        dve.scalar_tensor_tensor(p, p, 1.0 / odd, q, ALU.add, ALU.mult)
        dve.drain()
    dve.scalar_tensor_tensor(p, p, 1.0, s, ALU.add, ALU.mult)
    dve.drain()


def ssd_project(env, t, base):
    ps, ring, ins = env.ps, env.ring_, env.ins
    nz, nx = DI // HALF, (DI + 2 * G * NS) // HALF
    ft = nx * 4
    with Stage(env, base) as st:
        tm = st.sb("token_major", [P, 2, TOK])
        zb = st.sb("silu_z", [P, 2, HALF])
        pad = st.sb("padded", [P, 2, PADW])
        cv = st.sb("convolved", [P, 2, PADW - 4])
        sx = st.sb("x_features", [P, 2, TOK])
        raw = st.sb("dt_raw", [P, NT * 2 * H])
        e, s, q, p = (st.sb(f"softplus{i}", [P, NT * 2 * H]) for i in range(4))
        alog = st.sb("a_log", [P, 2 * H])
        out = st.sem("psum_copied")
        z_out = [st.sem("z_even_stored"), st.sem("z_odd_stored")]
        alog_in, pads, dt_neg, dt_exp, a_exp = (st.sem("alog_in"), st.sem("pads_zeroed"), st.sem("dt_negated"),
                                                st.sem("dt_exponent"), st.sem("a_exponent"))
        conv, silu, turned, filed = st.sem("convolved"), st.sem("activated"), st.sem("turned"), st.sem("filed")
        tm_out = [st.sem("even_token_tiles_stored"), st.sem("odd_token_tiles_stored")]
        fm_out = [st.sem("even_features_stored"), st.sem("odd_features_stored")]
        first, m0 = ring.take([NT] * nz + [NT] + [8] * nx)
        g0 = NT * (nz + 1)
        block = st.block()

        @block.sync
        def _(sp):
            sp.dma_start(alog[:], ins["ssd_A_log"].rearrange("a b c -> a (b c)").partition_broadcast(P)).then_inc(alog_in, 16)
            for n in range(nz):
                ring.load_to(sp, first + n + 1 + SLOTS)
                for i in range(NT):
                    g = n * NT + i
                    sp.wait_ge(out, g + 1)
                    sp.dma_start(env.z_dram[i, :, n * HALF:(n + 1) * HALF], zb[:, g % 2, :]).then_inc(z_out[g % 2], 16)
            for f in range(ft):
                if f % 4 == 0:
                    ring.load_to(sp, first + nz + 1 + f // 4 + SLOTS)
                if f >= 16:
                    sp.wait_ge(silu, f + 1)
                    dst = env.bt_dram if f < 24 else env.ct_dram
                    sp.dma_start(dst[:, f % 8, :], sx[:, f % 2, :]).then_inc(fm_out[f % 2], 16)
                if 1 <= f <= 24:
                    q_ = f - 1
                    sp.wait_ge(filed, f)
                    dst, a = (env.x_dram, q_ * P) if q_ < 16 else (env.b_dram, (q_ - 16) * P)
                    sp.dma_start(dst[:, :, a:a + P].rearrange("t p c -> p t c"),
                                 tm[:, q_ % 2, :].rearrange("p (t c) -> p t c", t=NT)).then_inc(tm_out[q_ % 2], 16)
            for par in range(2):
                sp.wait_ge(z_out[par], 16 * (nz * NT // 2))
                sp.wait_ge(tm_out[par], 16 * 12)
                sp.wait_ge(fm_out[par], 16 * 8)

        @block.tensor
        def _(pe):
            g = 0
            for n in range(nz + 1):
                k_ = first + n
                ring.wait(pe, k_)
                wide = HALF if n < nz else 2 * H
                w = ring.view(k_, KD, wide)
                for i in range(NT):
                    if g >= 4:
                        pe.wait_ge(out, g - 3)
                    for k in range(KD):
                        mm = pe.matmul(ps[:, g % 4, 0:wide], t.hT[:, k, i * P:(i + 1) * P], w[:, k, :],
                                       start=k == 0, stop=k == KD - 1)
                    mm.then_inc(ring.done, 1)
                    g += 1

            def turn(f):
                pe.wait_ge(silu, f + 1)
                if f >= 2:
                    pe.wait_ge(filed, f - 1)
                b = 4 + 2 * (f % 2)
                src = sx[:, f % 2, :]
                for i in range(NT):
                    tr = pe.transpose(ps[:, b + i // 4, (i % 4) * P:(i % 4 + 1) * P], src[:, i * P:(i + 1) * P], env.ident[:])
                tr.then_inc(turned, 1)

            for f in range(ft):
                k_ = first + nz + 1 + f // 4
                if f % 4 == 0:
                    ring.wait(pe, k_)
                w = ring.view(k_, KD, HALF)
                for o, m in ((0, LAT), (LAT, CTX)):
                    pe.wait_ge(out, g - 3)
                    for k in range(KD):
                        mm = pe.matmul(ps[:, g % 4, 0:m], w[:, k, (f % 4) * P:(f % 4 + 1) * P], t.hT[:, k, o:o + m],
                                       start=k == 0, stop=k == KD - 1)
                    mm.then_inc(ring.done, 1)
                    g += 1
                if 1 <= f <= 24:
                    turn(f - 1)

        @block.scalar
        def _(act):
            for n in range(nz):
                for i in range(NT):
                    g = n * NT + i
                    act.wait_ge(ring.done, m0 + g + 1)
                    if g >= 2:
                        act.wait_ge(z_out[g % 2], 16 * (g // 2))
                    act.activation(zb[:, g % 2, :], ps[:, g % 4, :], ACT.Silu).then_inc(out, 1)
            for i in range(NT):
                g = nz * NT + i
                act.wait_ge(ring.done, m0 + g + 1)
                act.activation(raw[:, i * 2 * H:(i + 1) * 2 * H], ps[:, g % 4, 0:2 * H], ACT.Copy).then_inc(out, 1)
            act.wait_ge(alog_in, 16)
            act.activation(alog[:], alog[:], ACT.Exp).then_inc(a_exp, 1)
            act.wait_ge(dt_neg, 1)
            act.activation(e[:], e[:], ACT.Exp).then_inc(dt_exp, 1)
            act.wait_ge(pads, 1)
            for f in range(ft):
                if f >= 2:
                    act.wait_ge(conv, f - 1)
                for j, (o, m, at) in enumerate(((0, LAT, PADL), (LAT, CTX, LATP + PADL))):
                    g = g0 + 2 * f + j
                    act.wait_ge(ring.done, m0 + g + 1)
                    act.activation(pad[:, f % 2, at:at + m], ps[:, g % 4, 0:m], ACT.Copy).then_inc(out, 1)
                act.wait_ge(conv, f + 1)
                if 2 <= f < 26:
                    act.wait_ge(turned, f - 1)
                if f >= 18:
                    act.wait_ge(fm_out[f % 2], 16 * ((f - 16) // 2))
                dst = sx[:, f % 2, :]
                act.activation(dst[:, 0:LAT], cv[:, f % 2, 0:LAT], ACT.Silu)
                act.activation(dst[:, LAT:TOK], cv[:, f % 2, LATP:LATP + CTX], ACT.Silu)
                act.drain().then_inc(silu, 1)

        @block.vector
        def _(dve):
            dve.memset(pad[:], 0.0).then_inc(pads, 1)
            dve.wait_ge(out, g0)
            r3 = raw[:].rearrange("p (t h) -> p t h", t=NT)
            dve.tensor_tensor(r3, r3, env.dtb[:].unsqueeze(1).broadcast_to([P, NT, 2 * H]), ALU.add)
            dve.drain()
            dve.scalar_tensor_tensor(e[:], raw[:], -1.0, raw[:], ALU.mult, ALU.min).then_inc(dt_neg, 1)
            dve.tensor_scalar(raw[:], raw[:], 0.0, None, ALU.max)
            dve.wait_ge(dt_exp, 1)
            log1p_steps(dve, e[:], s[:], q[:], p[:])
            dt = t.dt[:].rearrange("p t h -> p (t h)")
            dve.scalar_tensor_tensor(dt, p[:], 2.0, raw[:], ALU.mult, ALU.add)
            dve.wait_ge(a_exp, 1)
            dve.tensor_scalar(alog[:], alog[:], -1.0, None, ALU.mult)
            dve.drain()
            dve.tensor_tensor(t.a[:], t.dt[:], alog[:].unsqueeze(1).broadcast_to([P, NT, 2 * H]), ALU.mult)

            def file(f):
                dve.wait_ge(turned, f + 1)
                b = 4 + 2 * (f % 2)
                if f >= 2:
                    dve.wait_ge(tm_out[f % 2], 16 * (f // 2))
                dve.tensor_copy(tm[:, f % 2, 0:HALF], ps[:, b, :])
                dve.tensor_copy(tm[:, f % 2, HALF:TOK], ps[:, b + 1, 0:2 * P])
                dve.drain().then_inc(filed, 1)

            n = PADW - 4
            for f in range(ft):
                dve.wait_ge(out, g0 + 2 * f + 2)
                if f >= 2:
                    dve.wait_ge(silu, f - 1)
                c = cv[:, f % 2, :]
                dve.tensor_scalar(c, pad[:, f % 2, 0:n], col(env, "ssd_conv_w", f), col(env, "ssd_conv_b", f),
                                  ALU.mult, ALU.add)
                for j in range(1, TAPS):
                    dve.drain()
                    last = dve.scalar_tensor_tensor(c, pad[:, f % 2, j:j + n], col(env, "ssd_conv_w", j * 32 + f), c,
                                                    ALU.mult, ALU.add)
                last.then_inc(conv, 1)
                if 1 <= f <= 24:
                    file(f - 1)


def ssd_scan(env, t, base):
    ps = env.ps
    W = HPG * HD
    W4 = HPG * P
    with Stage(env, base) as st:
        xdt = st.sb("x_dt", [P, 2, DI])
        bt = st.sb("b_features", [P, 2, G * P])
        ct = st.sb("c_features", [P, 2, G * P])
        bk = st.sb("b_tokens", [P, 2, G * NS])
        xde = st.sb("x_dt_decayed", [P, 2, DI])
        nacum = st.sb("neg_acum", [P, NT, 2 * H])
        ea = st.sb("exp_acum", [P, NT, 2 * H])
        de = st.sb("decay_to_end", [P, NT, 2 * H])
        dec = st.sb("chunk_decay", [P, NT, 2 * H])
        state = st.sb("state", [P, DI])
        ex = st.sb("segment_exp", [P, 2, W4])
        y1 = st.sb("y_off", [P, 2, W])
        y2 = st.sb("y_sum", [P, 2, W])
        sums, sums_e, sums_v = st.sem("sums"), st.sem("sums_exp"), st.sem("sums_neg")
        cb_s, bc_s, exp_s, mt_s = st.sem("cb"), st.sem("acum_spread"), st.sem("segments"), st.sem("weights_ready")
        diag_s, y2_s, yadd_s = st.sem("y_parts"), st.sem("y_summed"), st.sem("y_added")
        in_s = [st.sem("even_chunk_in"), st.sem("odd_chunk_in")]
        st_s, new_s, xd_s = st.sem("state_part"), st.sem("state_new"), st.sem("x_scaled")
        block = st.block()
        steps = []
        for d, order in ((0, (4, 5, 0, 1, 2, 3)), (1, (5, 4, 3, 2, 1, 0))):
            for i, c in enumerate(order):
                steps.append((d, i, c))

        @block.sync
        def _(sp):
            env.ring_.load_to(sp, len(env.ring_.ends) + SLOTS)
            v = lambda x, m: x[:, m % 2, :].rearrange("p (g c) -> p g c", g=G)
            for m, (d, i, c) in enumerate(steps):
                if m >= 2:
                    sp.wait_ge(st_s, (m - 1) * G)
                tok = slice(c * P, (c + 1) * P)
                sp.dma_start(xdt[:, m % 2, :], env.x_dram[c, :, :]).then_inc(in_s[m % 2], 16)
                sp.dma_start(v(bt, m), env.bt_dram[:, :, tok]).then_inc(in_s[m % 2], 16)
                sp.dma_start(v(ct, m), env.ct_dram[:, :, tok]).then_inc(in_s[m % 2], 16)
                sp.dma_start(bk[:, m % 2, :], env.b_dram[c, :, :]).then_inc(in_s[m % 2], 16)

        @block.tensor
        def _(pe):
            af = flat(t.a[:])
            for b, lhs in enumerate((env.tri[:, 0, :], env.tri[:, 1, :], env.tri[:, 2, :], env.tri[:, 3, :], env.ones[:])):
                mm = pe.matmul(ps[:, b, 0:NT * 2 * H], lhs, af, start=True, stop=True)
            mm.then_inc(sums, 1)
            pe.wait_ge(sums_e, 1)
            pe.wait_ge(sums_v, 1)

            def front(n, m, d, c, g):
                if g == 0:
                    pe.wait_ge(in_s[m % 2], 64 * (m // 2 + 1))
                gs = slice(g * P, (g + 1) * P)
                if n >= 2:
                    pe.wait_ge(mt_s, n - 1)
                pe.matmul(ps[:, n % 2, 0:P], bt[:, m % 2, gs], ct[:, m % 2, gs], start=True, stop=True).then_inc(cb_s, 1)
                if n >= 2:
                    pe.wait_ge(exp_s, n - 1)
                pe.matmul(ps[:, 2 + n % 2, :], env.ident_b[:], env.mask_b[:, d:d + 1, :].broadcast_to([P, HPG, P]),
                          start=True, stop=False, skip_group_check=True)
                for h in range(HPG):
                    hh = d * H + g * HPG + h
                    mm = pe.matmul(ps[:, 2 + n % 2, h * P:(h + 1) * P], t.a[:, c, hh:hh + 1].broadcast_to([P, P]),
                                   env.tri[:, d, :], start=False, stop=True, skip_group_check=True)
                mm.then_inc(bc_s, 1)

            def back(n, m, d, i, c, g):
                gs = slice(g * P, (g + 1) * P)
                if n >= 2:
                    pe.wait_ge(y2_s, n - 1)
                if i > 0:
                    if n >= G:
                        pe.wait_ge(new_s, n - G + 1)
                    pe.matmul(ps[:, 4 + n % 2, 0:W], ct[:, m % 2, gs], state[:, g * W:(g + 1) * W],
                              start=True, stop=True)
                pe.wait_ge(xd_s, m + 1)
                pe.wait_ge(mt_s, n + 1)
                for h in range(HPG):
                    mm = pe.matmul(ps[:, 4 + n % 2, W + h * HD:W + (h + 1) * HD], ex[:, n % 2, h * P:(h + 1) * P],
                                   xdt[:, m % 2, (g * HPG + h) * HD:(g * HPG + h + 1) * HD], start=True, stop=True)
                mm.then_inc(diag_s, 1)
                if n >= 2:
                    pe.wait_ge(new_s, n - 1)
                pe.matmul(ps[:, 6 + n % 2, 0:W], bk[:, m % 2, gs], xde[:, m % 2, g * W:(g + 1) * W],
                          start=True, stop=True).then_inc(st_s, 1)

            todo = [(m, d, i, c, g) for m, (d, i, c) in enumerate(steps) for g in range(G)]
            front(0, 0, todo[0][1], todo[0][3], 0)
            for n, (m, d, i, c, g) in enumerate(todo):
                if n + 1 < len(todo):
                    front(n + 1, todo[n + 1][0], todo[n + 1][1], todo[n + 1][3], todo[n + 1][4])
                back(n, m, d, i, c, g)

        @block.scalar
        def _(act):
            act.wait_ge(sums, 1)
            f = lambda x, d: x[:, :, d * H:(d + 1) * H]
            v = lambda b, d: ps[:, b, 0:NT * 2 * H].rearrange("p (t h) -> p t h", t=NT)[:, :, d * H:(d + 1) * H]
            for d in range(2):
                act.activation(f(ea, d), v(d, d), ACT.Exp)
                act.activation(f(de, d), v(2 + d, d), ACT.Exp)
                act.activation(f(dec, d), v(4, d), ACT.Exp)
            act.drain().then_inc(sums_e, 1)
            act.wait_ge(sums_v, 1)
            n = 0
            for d, i, c in steps:
                for g in range(G):
                    act.wait_ge(bc_s, n + 1)
                    if n >= 2:
                        act.wait_ge(diag_s, n - 1)
                    for h in range(HPG):
                        hh = d * H + g * HPG + h
                        last = act.activation(ex[:, n % 2, h * P:(h + 1) * P], ps[:, 2 + n % 2, h * P:(h + 1) * P], ACT.Exp,
                                              bias=nacum[:, c, hh:hh + 1])
                    last.then_inc(exp_s, 1)
                    n += 1

        @block.gpsimd
        def _(pool):
            pool.wait_ge(sums_e, 1)
            hv = lambda x: x.rearrange("p (h e) -> p h e", e=HD)

            def scale_x(m):
                d, i, c = steps[m]
                pool.wait_ge(in_s[m % 2], 64 * (m // 2 + 1))
                sp_ = lambda x: x[:, c, d * H:(d + 1) * H].unsqueeze(2).broadcast_to([P, H, HD])
                pool.tensor_tensor(hv(xdt[:, m % 2, :]), hv(xdt[:, m % 2, :]), sp_(t.dt), ALU.mult)
                pool.drain()
                pool.tensor_tensor(hv(xde[:, m % 2, :]), hv(xdt[:, m % 2, :]), sp_(de), ALU.mult).then_inc(xd_s, 1)

            scale_x(0)
            scale_x(1)
            n = 0
            for m, (d, i, c) in enumerate(steps):
                for g in range(G):
                    pool.wait_ge(y2_s, n + 1)
                    yv = t.y[:, c, g * W:(g + 1) * W]
                    if d == 0:
                        pool.tensor_copy(yv, y2[:, n % 2, :]).then_inc(yadd_s, 1)
                    else:
                        pool.tensor_tensor(yv, yv, y2[:, n % 2, :], ALU.add).then_inc(yadd_s, 1)
                    n += 1
                if m + 2 < len(steps):
                    scale_x(m + 2)

        @block.vector
        def _(dve):
            dve.wait_ge(sums_e, 1)
            for d in range(2):
                v = ps[:, d, 0:NT * 2 * H].rearrange("p (t h) -> p t h", t=NT)[:, :, d * H:(d + 1) * H]
                dve.tensor_scalar(nacum[:, :, d * H:(d + 1) * H], v, -1.0, None, ALU.mult)
            dve.drain().then_inc(sums_v, 1)
            n = 0
            four = lambda x, e: x.rearrange("p (h e) -> p h e", e=e)
            for d, i, c in steps:
                for g in range(G):
                    hs = d * H + g * HPG
                    heads = lambda x: x[:, c, hs:hs + HPG].unsqueeze(2).broadcast_to([P, HPG, HD])
                    dve.wait_ge(cb_s, n + 1)
                    dve.wait_ge(exp_s, n + 1)
                    dve.tensor_tensor(four(ex[:, n % 2, :], P), four(ex[:, n % 2, :], P),
                                      ps[:, n % 2, 0:P].unsqueeze(1).broadcast_to([P, HPG, P]), ALU.mult).then_inc(mt_s, 1)
                    if n >= 2:
                        dve.wait_ge(yadd_s, n - 1)
                    if i > 0:
                        dve.wait_ge(diag_s, n + 1)
                        dve.tensor_tensor(four(y1[:, n % 2, :], HD), four(ps[:, 4 + n % 2, 0:W], HD), heads(ea), ALU.mult)
                        dve.drain()
                        dve.tensor_tensor(y2[:, n % 2, :], ps[:, 4 + n % 2, W:2 * W], y1[:, n % 2, :], ALU.add).then_inc(y2_s, 1)
                    else:
                        dve.wait_ge(diag_s, n + 1)
                        dve.tensor_copy(y2[:, n % 2, :], ps[:, 4 + n % 2, W:2 * W]).then_inc(y2_s, 1)
                    dve.wait_ge(st_s, n + 1)
                    sv = state[:, g * W:(g + 1) * W]
                    if i > 0:
                        dve.tensor_tensor(four(sv, HD), four(sv, HD), heads(dec), ALU.mult)
                        dve.drain()
                        dve.tensor_tensor(sv, ps[:, 6 + n % 2, 0:W], sv, ALU.add).then_inc(new_s, 1)
                    else:
                        dve.tensor_copy(sv, ps[:, 6 + n % 2, 0:W]).then_inc(new_s, 1)
                    n += 1


def ssd_gate(env, t, base):
    with Stage(env, base) as st:
        xb = st.sb("x_tile", [P, 2, DI])
        zb = st.sb("z_tile", [P, 2, DI])
        dsk = st.sb("d_skip", [P, H])
        d_in = st.sem("d_in")
        x_in = [st.sem("even_x_in"), st.sem("odd_x_in")]
        z_in = [st.sem("even_z_in"), st.sem("odd_z_in")]
        dx, gated = st.sem("d_times_x"), st.sem("gated")
        block = st.block()

        @block.sync
        def _(sp):
            sp.dma_start(dsk, env.ins["ssd_D"].rearrange("a h -> (a h)").partition_broadcast(P)).then_inc(d_in, 16)
            for i in range(NT):
                if i >= 2:
                    sp.wait_ge(gated, i - 1)
                sp.dma_start(xb[:, i % 2, :], env.x_dram[i, :, :]).then_inc(x_in[i % 2], 16)
                sp.dma_start(zb[:, i % 2, :], env.z_dram[i, :, :]).then_inc(z_in[i % 2], 16)

        @block.gpsimd
        def _(pool):
            pool.wait_ge(d_in, 16)
            for i in range(NT):
                pool.wait_ge(x_in[i % 2], 16 * (i // 2 + 1))
                v = xb[:, i % 2, :].rearrange("p (h e) -> p h e", e=HD)
                pool.tensor_tensor(v, v, dsk.unsqueeze(2).broadcast_to([P, H, HD]), ALU.mult).then_inc(dx, 1)

        @block.vector
        def _(dve):
            for i in range(NT):
                y = t.y[:, i, :]
                dve.wait_ge(dx, i + 1)
                dve.tensor_tensor(y, y, xb[:, i % 2, :], ALU.add)
                dve.drain()
                dve.wait_ge(z_in[i % 2], 16 * (i // 2 + 1))
                dve.tensor_tensor(y, y, zb[:, i % 2, :], ALU.mult).then_inc(gated, 1)


def project_add(env, base, X, hT, kd, tiles, gate=None, norm=None, load=None):
    ps, ring = env.ps, env.ring_
    nk = -(-kd // KD)
    n_t = len(tiles)
    with Stage(env, base) as st:
        rows = gate[1] if gate else [norm]
        spread = st.sb("row_weights", [P, len(rows), D])
        o = st.sb("product", [P, n_t, D])
        junk = st.sb("squares", [P, D])
        ss = st.sb("mean_square", [P, n_t])
        rows_in, copied, eps_in, rooted, squared = (st.sem("rows_in"), st.sem("products_out"), st.sem("eps_in"),
                                                    st.sem("rooted"), st.sem("squared"))
        x_in = st.sem("x_in")
        marks = []
        for n in range(2):
            marks += [1] * (nk - 1) + [n_t]
        first, m0 = ring.take(marks)
        per = nk - 1 + n_t
        block = st.block()

        @block.sync
        def _(sp):
            for j, r in enumerate(rows):
                sp.dma_start(spread[:, j, :], r.partition_broadcast(P)).then_inc(rows_in, 16)
            for i, s in load or ():
                sp.dma_start(X[:, i, :], s).then_inc(x_in, 16)
            ring.load_to(sp, len(ring.ends) + SLOTS)

        @block.tensor
        def _(pe):
            for n in range(2):
                for c in range(nk):
                    k_ = first + n * nk + c
                    ring.wait(pe, k_)
                    ks = min(KD, kd - c * KD)
                    w = ring.view(k_, ks, HALF)
                    for j, i in enumerate(tiles):
                        if n == 1 and c == 0:
                            pe.wait_ge(copied, j + 1)
                        for k in range(ks):
                            mm = pe.matmul(ps[:, j, :], hT[:, c * KD + k, i * P:(i + 1) * P], w[:, k, :],
                                           start=c == 0 and k == 0, stop=c == nk - 1 and k == ks - 1)
                        if c == nk - 1 or j == n_t - 1:
                            mm.then_inc(ring.done, 1)

        @block.scalar
        def _(act):
            for n in range(2):
                for j in range(n_t):
                    act.wait_ge(ring.done, m0 + n * per + nk - 1 + j + 1)
                    act.activation(o[:, j, n * HALF:(n + 1) * HALF], ps[:, j, :], ACT.Copy).then_inc(copied, 1)
            if norm is not None:
                act.drain()
                for j in range(n_t):
                    act.drain()
                    act.activation(junk, o[:, j, :], ACT.Square, scale=float(D) ** -0.5,
                                   accum_out=ss[:, j:j + 1]).then_inc(squared, 1)
                act.wait_ge(eps_in, 1)
                act.activation(ss, ss, ACT.Sqrt).then_inc(rooted, 1)

        @block.vector
        def _(dve):
            dve.wait_ge(rows_in, 16 * len(rows))
            if load:
                dve.wait_ge(x_in, 16 * len(load))
            if gate:
                for n in range(2):
                    h = slice(n * HALF, (n + 1) * HALF)
                    for j, i in enumerate(tiles):
                        dve.wait_ge(copied, n * n_t + j + 1)
                        dve.tensor_tensor(o[:, j, h], o[:, j, h], spread[:, gate[0](i), h], ALU.mult)
                        dve.drain()
                        dve.tensor_tensor(X[:, i, h], X[:, i, h], o[:, j, h], ALU.add)
            else:
                dve.wait_ge(squared, n_t)
                dve.tensor_scalar(ss, ss, EPS, None, ALU.add).then_inc(eps_in, 1)
                dve.wait_ge(rooted, 1)
                dve.reciprocal(ss, ss)
                dve.drain()
                for j, i in enumerate(tiles):
                    dve.scalar_tensor_tensor(o[:, j, :], o[:, j, :], ss[:, j:j + 1], spread[:, 0, :], ALU.mult, ALU.mult)
                    dve.drain()
                    dve.tensor_tensor(X[:, i, :], X[:, i, :], o[:, j, :], ALU.add)


def route(env, base, layer, hT, nt, aff, pos, xn, xh, xl):
    ps = env.ps
    segs = [(0, LAT)] + ([(LAT, CTX)] if nt > NL else [])
    n_tok = nt * P
    with Stage(env, base) as st:
        rw = st.sb("router_w", [P, KD, E])
        lg = st.sb("logits", [P, nt, E])
        mx = st.sb("row_max", [P, nt])
        sm = st.sb("row_sum", [P, nt])
        aT = st.sb("aff_by_expert", [E, n_tok])
        work = st.sb("left_to_pick", [E, n_tok])
        work2 = st.sb("left_after_pick", [E, n_tok])
        place = st.sb("places", [E, n_tok])
        top = st.sb("top8", [E, 8])
        w_in, logit, shifted, exped, aff_s = (st.sem("router_in"), st.sem("logits_done"), st.sem("shifted"),
                                              st.sem("exp_done"), st.sem("aff_ready"))
        turned, picked, back = st.sem("aff_turned"), st.sem("places_ready"), st.sem("places_turned")
        xh_s = st.sem("high_parts")
        block = st.block()

        @block.sync
        def _(sp):
            sp.dma_start(rw, env.ins["moe_router_w"][layer].rearrange("(k p) e -> p k e", p=P)).then_inc(w_in, 16)
            env.ring_.load_to(sp, len(env.ring_.ends) + SLOTS)

        @block.tensor
        def _(pe):
            pe.wait_ge(w_in, 16)
            for i in range(nt):
                for k in range(KD):
                    mm = pe.matmul(ps[:, 0, i * E:(i + 1) * E], hT[:, k, i * P:(i + 1) * P], rw[:, k, :],
                                   start=k == 0, stop=k == KD - 1)
            mm.then_inc(logit, 1)
            pe.wait_ge(aff_s, 1)
            for i in range(nt):
                tr = pe.transpose(ps[0:E, 1 + i // 4, (i % 4) * P:(i % 4 + 1) * P], aff[:, i, :], env.ident[:])
            tr.then_inc(turned, 1)
            pe.wait_ge(picked, 1)
            for i in range(nt):
                tr = pe.transpose(ps[:, 3, i * E:(i + 1) * E], place[:, i * P:(i + 1) * P], env.ident[0:E, 0:E])
            tr.then_inc(back, 1)

        @block.scalar
        def _(act):
            act.wait_ge(shifted, 1)
            act.activation(lg, lg, ACT.Exp).then_inc(exped, 1)
            for i in range(nt):
                act.activation(xh[:, i, :], xn[:, i, :], ACT.Copy).then_inc(xh_s, 1)

        @block.gpsimd
        def _(pool):
            for i in range(nt):
                pool.wait_ge(xh_s, i + 1)
                pool.tensor_tensor(xl[:, i, :], xn[:, i, :], xh[:, i, :], ALU.subtract)

        @block.vector
        def _(dve):
            dve.wait_ge(logit, 1)
            lp = ps[:, 0, 0:nt * E].rearrange("p (i e) -> p i e", e=E)
            spread = lambda v: v.unsqueeze(2).broadcast_to([P, nt, E])
            dve.tensor_reduce(mx, lp, AX.X, ALU.max)
            dve.drain()
            dve.tensor_tensor(lg, lp, spread(mx), ALU.subtract).then_inc(shifted, 1)
            dve.wait_ge(exped, 1)
            dve.tensor_reduce(sm, lg, AX.X, ALU.add)
            dve.drain()
            dve.reciprocal(mx, sm)
            dve.drain()
            dve.tensor_tensor(aff, lg, spread(mx), ALU.mult).then_inc(aff_s, 1)
            dve.wait_ge(turned, 1)
            for j, (o, n) in enumerate(segs):
                dve.tensor_copy(aT[:, o:o + n], ps[0:E, 1 + j, 0:n])
            dve.drain()
            for o, n in segs:
                a, b = aT[:, o:o + n], work[:, o:o + n]
                c = work2[:, o:o + n]
                for r in range(2 * n // E // 8):
                    dve.max(top, a)
                    dve.drain()
                    dve.match_replace(b, top, a, -1.0)
                    dve.drain()
                    a, b, c = b, c, b
                left, count = a, b
                v, pl = aT[:, o:o + n], place[:, o:o + n]
                dve.tensor_tensor(v, left, v, ALU.is_lt)
                dve.drain()
                dve.tensor_tensor_scan(count, env.ones[0:E, 0:1].broadcast_to([E, n]), v, 0.0, ALU.mult, ALU.add)
                dve.drain()
                dve.scalar_tensor_tensor(pl, count, float(2 * o // E), v, ALU.add, ALU.mult)
            dve.drain().then_inc(picked, 1)
            dve.wait_ge(back, 1)
            dve.tensor_copy(pos, ps[:, 3, 0:nt * E].rearrange("p (i e) -> p i e", e=E))


def experts(env, base, layer, nt, xh, xl, aff, pos, acc):
    ps, ring, ins = env.ps, env.ring_, env.ins
    segs = [(0, 2 * LAT // E, 0)] + ([(2 * LAT // E, 2 * CTX // E, 1)] if nt > NL else [])
    S = sum(s[1] for s in segs)
    BL = 4 * S
    PER = 6
    NB = PER * BLOCKS
    PAIRS = E // 2
    with Stage(env, base) as st:
        oneh = st.sbr("one_hot", [P, nt * S])
        pT = st.sbr("one_hot_turned", [S, 2, nt * P])
        xgh, xgl = st.sbr("gathered_high", [P, KD * S]), st.sbr("gathered_low", [P, KD * S])
        hTh, hTl = st.sbr("hidden_turned_high", [P, KD * S]), st.sbr("hidden_turned_low", [P, KD * S])
        yh, yl = st.sbr("expert_rows_high", [S, D]), st.sbr("expert_rows_low", [S, D])
        rows_in = st.sb("gathered_rows", [P, D])
        xg = rows_in[:, 0:KD * S]
        rows_in = rows_in[0:S, :]
        h2 = st.sb("hidden", [S, D])
        gate = st.sb("slot_gates", [S, 2])
        built, gath, taken, gt_s, xg_s = (st.sem("one_hots_built"), st.sem("gather_summed"), st.sem("gathered_copied"),
                                          st.sem("gathered_turned"), st.sem("gathered_ready"))
        turned, pt_s = st.sem("one_hots_turned"), st.sem("turned_copied")
        sil, h2_s, t_s, th_s, tl_s = (st.sem("silu_done"), st.sem("hidden_done"),
                                              st.sem("hidden_turned"), st.sem("hidden_high"), st.sem("hidden_low"))
        yh_s, yl_s, sc_s, add_s = st.sem("rows_high"), st.sem("rows_low"), st.sem("scattered"), st.sem("rows_added")
        first, b0, v0, p0 = ring.take_split([BLOCKS] * (PER * E))
        oneh3 = oneh.rearrange("p (i s) -> p i s", i=nt)
        oneh_f = oneh.bitcast(F32).rearrange("p (i s) -> p i s", i=nt)
        block = st.block()
        names = ("moe_w1", "moe_w1", "moe_w3", "moe_w3", "moe_w2", "moe_w2")

        def source(i, n):
            c = n % PER
            w = ins[names[c]][layer, n // PER:]
            h = slice((c % 2) * HALF, (c % 2 + 1) * HALF)
            return w[bass.ds(i * 2, 1), :, h].rearrange("o (k p) n -> p (o k) n", p=P)

        @block.sync
        def _(sp):
            ring.load_to(sp, first + SLOTS)
            ring.loaded = first + PER * E
            ring.load_to(sp, first + PER * E + SLOTS)

        def each_pair(eng, body):
            body(0, True, False)
            with eng.Fori(1, PAIRS - 1) as i:
                body(i, False, False)
            body(PAIRS - 1, False, True)

        @block.tensor
        def _(pe):
            def gather(e, waits):
                pe.wait_ge(built, e + 1)
                for h in range(2):
                    for t in range(nt):
                        for n, x in enumerate((xh, xl)):
                            if h == 1 and t == nt - 1 and n == 1:
                                for w in waits:
                                    pe.wait_ge(*w)
                            mm = pe.matmul(ps[0:S, 4 + h, :], oneh3[:, t, :], x[:, t, h * HALF:(h + 1) * HALF],
                                           start=t == 0 and n == 0, stop=t == nt - 1 and n == 1)
                mm.then_inc(gath, 1)

            def turn_hidden():
                for b in range(2):
                    for k in range(4 * b, 4 * b + 4):
                        tr = pe.transpose(ps[:, 2 + b, (k % 4) * S:(k % 4 + 1) * S], h2[:, k * P:(k + 1) * P],
                                          env.ident[0:S, 0:S])
                    tr.then_inc(t_s, 1)

            def turn_gathered(e):
                for t in range(nt):
                    pe.transpose(ps[0:S, 6 + t // 4, (t % 4) * P:(t % 4 + 1) * P], oneh_f[:, t, :], env.ident[:])
                pe.wait_ge(taken, 2 * e + 2)
                for t in range(nt):
                    mm = pe.matmul(ps[0:S, 7, 2 * P:2 * P + 1], oneh_f[:, t, :], aff[:, t, bass.ds(e, 1)], start=t == 0, stop=t == nt - 1)
                mm.then_inc(turned, 1)
                for k in range(KD):
                    tr = pe.transpose(ps[:, 4 + k // 4, (k % 4) * S:(k % 4 + 1) * S], rows_in[:, k * P:(k + 1) * P],
                                      env.ident[0:S, 0:S])
                tr.then_inc(gt_s, 1)

            def scatter(e, j, t):
                for h in range(2):
                    for n, y in enumerate((yh, yl)):
                        mm = pe.matmul(ps[:, 4 + 2 * (t % 2) + h, :], pT[:, j, t * P:(t + 1) * P],
                                       y[:, h * HALF:(h + 1) * HALF], start=n == 0, stop=n == 1)
                mm.then_inc(sc_s, 1)

            def product(i, j, c, high, low, bank):
                for b in range(BLOCKS):
                    m = NB * j + BLOCKS * c + b
                    if b == 3:
                        pe.wait_ge(ring.low_p, i * 12 + (p0 + m // BLOCKS + 1))
                    else:
                        pe.wait_ge(ring.low_v, i * 36 + (v0 + 3 * (m // BLOCKS) + b + 1))
                    s = (b0 + m) % CUTS
                    for q in range(2):
                        k = 2 * b + q
                        w = slice(q * HALF, (q + 1) * HALF)
                        for n, (x, y) in enumerate(((high, ring.hi), (low, ring.hi), (high, ring.lo))):
                            mm = pe.matmul(ps[0:S, bank, :], x[:, k * S:(k + 1) * S], y[:, s, w],
                                           start=k == 0 and n == 0, stop=k == KD - 1 and n == 2)
                    mm.then_inc(ring.used, 1)

            def body(i, begin, end):
                for j in range(2):
                    e = i * 2 + j
                    start, stop = begin and j == 0, end and j == 1
                    a, l = xgh, xgl
                    pe.wait_ge(xg_s, e + 1)
                    if not start:
                        pe.wait_ge(yl_s, 2 * e - 1)
                    product(i, j, 0, a, l, 0)
                    if not start:
                        pe.wait_ge(yl_s, 2 * e)
                    product(i, j, 1, a, l, 1)
                    if not start:
                        pe.wait_ge(pt_s, e + 1)
                        scatter(e - 1, 1 - j, 0)
                        scatter(e - 1, 1 - j, 1)
                        pe.wait_ge(tl_s, 2 * e)
                    product(i, j, 2, a, l, 2)
                    if not start:
                        for t in (2, 3):
                            pe.wait_ge(add_s, (e - 1) * nt + t - 1)
                            scatter(e - 1, 1 - j, t)
                    product(i, j, 3, a, l, 3)
                    if not start:
                        for t in range(4, nt):
                            pe.wait_ge(add_s, (e - 1) * nt + t - 1)
                            scatter(e - 1, 1 - j, t)
                    if stop:
                        pe.wait_ge(h2_s, 2 * e + 2)
                        turn_hidden()
                    else:
                        if not start:
                            pe.wait_ge(add_s, e * nt - 1)
                        gather(e + 1, [(h2_s, 2 * e + 2)] + ([] if start else [(add_s, e * nt)]))
                        turn_hidden()
                        turn_gathered(e + 1)
                    pe.wait_ge(tl_s, 2 * e + 2)
                    product(i, j, 4, hTh, hTl, 0)
                    product(i, j, 5, hTh, hTl, 1)

            gather(0, [])
            turn_gathered(0)
            each_pair(pe, body)
            pe.wait_ge(yl_s, 2 * E)
            for t in range(nt):
                if t >= 2:
                    pe.wait_ge(add_s, (E - 1) * nt + t - 1)
                scatter(E - 1, 1, t)

        def part_source(m):
            w = ring.slots[:, (first + m // BLOCKS) % SLOTS, :]
            return w[:, (m % BLOCKS) * CUT:(m % BLOCKS + 1) * CUT]

        @block.scalar
        def _(act):
            def high(i, end, a, b):
                for m in range(a, b):
                    if m % BLOCKS == 0:
                        n = first + m // BLOCKS
                        act.wait_ge(ring.landed[n % SLOTS], i * 16 * (12 // SLOTS) + 16 * (n // SLOTS + 1))
                    if a > 0:
                        act.wait_ge(ring.used, i * 2 * NB + b0 + m - CUTS + 1)
                    act.activation(ring.hi[:, (b0 + m) % CUTS, :], part_source(m), ACT.Copy).then_inc(ring.high, 1)
                    n = m // BLOCKS - 1 + SLOTS
                    if m % BLOCKS == 3 and n >= SLOTS and not (end and n >= 2 * PER):
                        act.dma_start(ring.view(first + n, KD, HALF), source(i, n)).then_inc(ring.landed[(first + n) % SLOTS], 16)

            def copy_gathered(e):
                act.wait_ge(gath, e + 1)
                for b in range(2):
                    act.activation(rows_in[:, b * HALF:(b + 1) * HALF], ps[0:S, 4 + b, :], ACT.Copy).then_inc(taken, 1)

            def copy_turned(e, j):
                act.wait_ge(turned, e + 1)
                act.activation(gate[:, j:j + 1], ps[0:S, 7, 2 * P:2 * P + 1], ACT.Copy)
                for b in range(-(-nt // 4)):
                    w = min(4, nt - 4 * b) * P
                    act.activation(pT[:, j, b * HALF:b * HALF + w], ps[0:S, 6 + b, 0:w], ACT.Copy)
                act.drain().then_inc(pt_s, 1)

            def silu(i, e, j, b):
                act.wait_ge(ring.used, i * 2 * NB + b0 + NB * j + BLOCKS * (b + 1))
                act.activation(h2[:, b * HALF:(b + 1) * HALF], ps[0:S, b, :], ACT.Silu).then_inc(sil, 1)

            def rows(i, e, j, b):
                act.wait_ge(ring.used, i * 2 * NB + b0 + NB * j + BLOCKS * (5 + b))
                act.activation(yh[:, b * HALF:(b + 1) * HALF], ps[0:S, b, :], ACT.Copy, scale=gate[:, j:j + 1]).then_inc(yh_s, 1)

            def body(i, begin, end):
                for j in range(2):
                    e = i * 2 + j
                    o = NB * j
                    start, stop = begin and j == 0, end and j == 1
                    if not start:
                        act.wait_ge(t_s, 2 * e)
                    high(i, end, o + CUTS, o + CUTS + 4)
                    silu(i, e, j, 0)
                    high(i, end, o + CUTS + 4, o + CUTS + 8)
                    silu(i, e, j, 1)
                    high(i, end, o + CUTS + 8, o + CUTS + 16)
                    if not stop:
                        copy_gathered(e + 1)
                    for b in range(2):
                        act.wait_ge(t_s, 2 * e + b + 1)
                        act.activation(hTh[:, b * BL:(b + 1) * BL], ps[:, 2 + b, 0:BL], ACT.Copy).then_inc(th_s, 1)
                    if not stop:
                        copy_turned(e + 1, 1 - j)
                    high(i, end, o + CUTS + 16, o + CUTS + 20)
                    rows(i, e, j, 0)
                    high(i, end, o + CUTS + 20, o + NB + (0 if stop else CUTS))
                    rows(i, e, j, 1)

            high(0, False, 0, CUTS)
            copy_gathered(0)
            copy_turned(0, 0)
            each_pair(act, body)

        @block.gpsimd
        def _(pool):
            def body(i, begin, end):
                for m in range(3, 2 * NB, BLOCKS):
                    pool.wait_ge(ring.high, i * 2 * NB + (b0 + m + 1))
                    s = (b0 + m) % CUTS
                    pool.tensor_tensor(ring.lo[:, s, :], part_source(m), ring.hi[:, s, :], ALU.subtract).then_inc(ring.low_p, 1)

            each_pair(pool, body)

        @block.vector
        def _(dve):
            def low(i, a, b):
                for m in range(a, b):
                    if m % BLOCKS == 3:
                        continue
                    dve.wait_ge(ring.high, i * 2 * NB + (b0 + m + 1))
                    s = (b0 + m) % CUTS
                    dve.tensor_tensor(ring.lo[:, s, :], part_source(m), ring.hi[:, s, :], ALU.subtract).then_inc(ring.low_v, 1)

            def build(e):
                shape = [P, nt, S]
                dve.tensor_tensor(oneh3, env.iota[:, 0:S].unsqueeze(1).broadcast_to(shape),
                                  pos[:, :, bass.ds(e, 1)].broadcast_to(shape), ALU.is_equal).then_inc(built, 1)

            def modulate(e):
                dve.wait_ge(gt_s, e + 1)
                for b in range(2):
                    g = ps[:, 4 + b, 0:BL].rearrange("p (k s) -> p k s", k=4)
                    o = xg[:, b * BL:(b + 1) * BL].rearrange("p (k s) -> p k s", k=4)
                    for s0, m, u in segs:
                        c = lambda q: env.modc[:, q, u, 4 * b:4 * b + 4].unsqueeze(2).broadcast_to([P, 4, m])
                        dve.tensor_tensor(o[:, :, s0:s0 + m], g[:, :, s0:s0 + m], c(3), ALU.mult)
                dve.drain()
                for b in range(2):
                    o = xg[:, b * BL:(b + 1) * BL].rearrange("p (k s) -> p k s", k=4)
                    for s0, m, u in segs:
                        c = lambda q: env.modc[:, q, u, 4 * b:4 * b + 4].unsqueeze(2).broadcast_to([P, 4, m])
                        dve.tensor_tensor(o[:, :, s0:s0 + m], o[:, :, s0:s0 + m], c(2), ALU.add)
                dve.drain()
                dve.tensor_copy(xgh, xg)
                dve.drain()
                dve.tensor_tensor(xgl, xg, xgh, ALU.subtract)
                dve.drain().then_inc(xg_s, 1)

            def add(e, t):
                dve.wait_ge(sc_s, e * nt + t + 1)
                b = 4 + 2 * (t % 2)
                dve.tensor_tensor(acc[:, t, :], acc[:, t, :], ps[:, b:b + 2, :].rearrange("p a b -> p (a b)"),
                                  ALU.add).then_inc(add_s, 1)

            def hidden(i, e, j, b):
                dve.wait_ge(ring.used, i * 2 * NB + b0 + NB * j + BLOCKS * (3 + b))
                dve.wait_ge(sil, 2 * e + b + 1)
                s = slice(b * HALF, (b + 1) * HALF)
                dve.tensor_tensor(h2[:, s], h2[:, s], ps[0:S, 2 + b, :], ALU.mult).then_inc(h2_s, 1)

            def rows(e, j, b):
                dve.wait_ge(yh_s, 2 * e + b + 1)
                s = slice(b * HALF, (b + 1) * HALF)
                dve.scalar_tensor_tensor(yl[:, s], ps[0:S, b, :], gate[:, j:j + 1], yh[:, s], ALU.mult,
                                         ALU.subtract).then_inc(yl_s, 1)

            def body(i, begin, end):
                for j in range(2):
                    e = i * 2 + j
                    o = NB * j
                    start, stop = begin and j == 0, end and j == 1
                    if not stop:
                        dve.wait_ge(turned, e + 1)
                        build(e + 1)
                    low(i, o + CUTS, o + CUTS + 8)
                    if not start:
                        add(e - 1, 0)
                        add(e - 1, 1)
                    low(i, o + CUTS + 8, o + CUTS + 12)
                    hidden(i, e, j, 0)
                    if not start:
                        add(e - 1, 2)
                        add(e - 1, 3)
                    low(i, o + CUTS + 12, o + CUTS + 16)
                    hidden(i, e, j, 1)
                    if not start:
                        for t in range(4, nt):
                            add(e - 1, t)
                    for b in range(2):
                        dve.wait_ge(th_s, 2 * e + b + 1)
                        dve.tensor_tensor(hTl[:, b * BL:(b + 1) * BL], ps[:, 2 + b, 0:BL], hTh[:, b * BL:(b + 1) * BL],
                                          ALU.subtract).then_inc(tl_s, 1)
                    if not stop:
                        modulate(e + 1)
                    low(i, o + CUTS + 16, o + CUTS + 20)
                    rows(e, j, 0)
                    low(i, o + CUTS + 20, o + NB + (0 if stop else CUTS))
                    rows(e, j, 1)

            build(0)
            dve.memset(acc, 0.0)
            low(0, 0, CUTS)
            modulate(0)
            each_pair(dve, body)
            for t in range(nt):
                add(E - 1, t)


def gate_add(env, base, layer, X, acc, nt):
    rows = [env.mod_dram[layer, u, 5 * D:6 * D] for u in range(2 if nt > NL else 1)]
    with Stage(env, base) as st:
        spread = st.sb("gate_rows", [P, len(rows), D])
        g_in = st.sem("gate_in")
        block = st.block()

        @block.sync
        def _(sp):
            for j, r in enumerate(rows):
                sp.dma_start(spread[:, j, :], r.partition_broadcast(P)).then_inc(g_in, 16)

        @block.vector
        def _(dve):
            dve.wait_ge(g_in, 16 * len(rows))
            for t in range(nt):
                dve.tensor_tensor(acc[:, t, :], acc[:, t, :], spread[:, int(t >= NL), :], ALU.mult)
            dve.drain()
            for t in range(nt):
                dve.tensor_tensor(X[:, t, :], X[:, t, :], acc[:, t, :], ALU.add)


def moe(env, layer, X, nt):
    mc = lambda q, u: (lambda k: env.modc[:, q, u, k:k + 1])
    xn = acc = carve(env, X_END, [P, nt, D])
    top = X_END + nt * D
    aff, pos = carve(env, top, [P, nt, E]), carve(env, top + nt * E, [P, nt, E])
    top += 2 * nt * E
    xh, xl = carve_r(env, "tokens_high", top, [P, nt, D]), carve_r(env, "tokens_low", top + nt * D, [P, nt, D])
    top += 2 * nt * D
    hT = carve(env, top, [P, KD, nt * P])
    groups = [(0, NL, mc(3, 0), mc(2, 0))] + ([(NL, NC, mc(3, 1), mc(2, 1))] if nt > NL else [])
    norm_turn(env, top + nt * D, X, hT, groups, token_out=xn)
    route(env, top + nt * D, layer, hT, nt, aff, pos, xn, xh, xl)
    experts(env, top, layer, nt, xh, xl, aff, pos, acc)
    gate_add(env, top, layer, X, acc, nt)


def project(env, base, jobs):
    ps, ring = env.ps, env.ring_
    with Stage(env, base) as st:
        left = st.sem("sums_copied")
        first, m0 = ring.take([len(groups) for _, _, groups in jobs])
        block = st.block()

        @block.sync
        def _(sp):
            ring.load_to(sp, len(ring.ends) + SLOTS)

        @block.tensor
        def _(pe):
            g = 0
            for c, (kd, width, groups) in enumerate(jobs):
                ring.wait(pe, first + c)
                w = ring.view(first + c, kd, width)
                for operands, rows, cols, _ in groups:
                    if g >= 8:
                        pe.wait_ge(left, g - 7)
                    for k in range(kd):
                        lhsT, rhs = operands(k, w)
                        mm = pe.matmul(ps[0:rows, g % 8, 0:cols], lhsT, rhs, start=k == 0, stop=k == kd - 1)
                    mm.then_inc(ring.done, 1)
                    g += 1

        @block.scalar
        def _(act):
            g = 0
            for _, _, groups in jobs:
                for _, rows, cols, copies in groups:
                    act.wait_ge(ring.done, m0 + g + 1)
                    copies(act, ps[0:rows, g % 8, 0:cols]).then_inc(left, 1)
                    g += 1


def features(hT, f, tok, copies):
    return (lambda k, w: (w[:, k, f * P:(f + 1) * P], hT[:, k, tok])), P, tok.stop - tok.start, copies


def tokens(hT, t, cols, copies):
    return (lambda k, w: (hT[:, k, t * P:(t + 1) * P], w[:, k, cols])), P, cols.stop - cols.start, copies


def copy_to(dst, func=ACT.Copy):
    return lambda act, s: act.activation(dst, s, func)


def turn(env, base, src, hT, nt, kd):
    ps = env.ps
    with Stage(env, base) as st:
        turned, left = st.sem("turned"), st.sem("copied")
        block = st.block()

        @block.tensor
        def _(pe):
            for k in range(kd):
                if k >= 8:
                    pe.wait_ge(left, k - 7)
                for t in range(nt):
                    tr = pe.transpose(ps[:, k % 8, t * P:(t + 1) * P], src[:, t, k * P:(k + 1) * P], env.ident[:])
                tr.then_inc(turned, 1)

        @block.vector
        def _(dve):
            for k in range(kd):
                dve.wait_ge(turned, k + 1)
                dve.tensor_copy(hT[:, k, :], ps[:, k % 8, 0:nt * P]).then_inc(left, 1)

        @block.sync
        def _(sp):
            env.ring_.load_to(sp, len(env.ring_.ends) + SLOTS)


def attend(env, base, steps, scale, width):
    ps = env.ps
    most = max(s[2] for s in steps)
    masked = any(s[3] is not None for s in steps)
    with Stage(env, base) as st:
        prob = st.sb("probabilities", [P, 2, most])
        pT = st.sb("probabilities_turned", [P, 2, most])
        sm = st.sb("masked_scores", [P, 2, most]) if masked else None
        stat = st.sb("row_stats", [P, 2, 4])
        score, shift, prob_s, turned = st.sem("scores"), st.sem("shift_ready"), st.sem("probabilities"), st.sem("turned")
        pT_a, pT_v, outs, left = (st.sem("turned_copied_by_act"), st.sem("turned_copied_by_dve"), st.sem("outputs"),
                                  st.sem("outputs_left"))
        block = st.block()

        @block.sync
        def _(sp):
            env.ring_.load_to(sp, len(env.ring_.ends) + SLOTS)

        @block.tensor
        def _(pe):
            def scores(n):
                q, k, keys = steps[n][:3]
                if n >= 2:
                    pe.wait_ge(prob_s, n - 1)
                    pe.wait_ge(shift, n - 1)
                for a in range(0, keys, HALF):
                    b = min(a + HALF, keys)
                    mm = pe.matmul(ps[:, 2 * (n % 2) + a // HALF, 0:b - a], q, k[:, a:b], start=True, stop=True)
                mm.then_inc(score, 1)

            def output(n):
                keys, values = steps[n][2], steps[n][4]
                kt = keys // P
                pe.wait_ge(prob_s, n + 1)
                if n >= 1:
                    pe.wait_ge(pT_a, n)
                    pe.wait_ge(pT_v, n)
                for t in range(kt):
                    tr = pe.transpose(ps[:, 4 + t // 4, (t % 4) * P:(t % 4 + 1) * P], prob[:, n % 2, t * P:(t + 1) * P], env.ident[:])
                tr.then_inc(turned, 1)
                if n >= 2:
                    pe.wait_ge(left, n - 1)
                pe.wait_ge(pT_a, n + 1)
                pe.wait_ge(pT_v, n + 1)
                for t in range(kt):
                    mm = pe.matmul(ps[:, 6 + n % 2, 0:width], pT[:, n % 2, t * P:(t + 1) * P], values[t], start=t == 0, stop=t == kt - 1)
                mm.then_inc(outs, 1)

            scores(0)
            for n in range(len(steps)):
                if n + 1 < len(steps):
                    scores(n + 1)
                output(n)

        @block.scalar
        def _(act):
            def copy_turned(n):
                act.wait_ge(turned, n + 1)
                w = min(steps[n][2], HALF)
                act.activation(pT[:, n % 2, 0:w], ps[:, 4, 0:w], ACT.Copy).then_inc(pT_a, 1)

            for n, (_, _, keys, mask, _, _) in enumerate(steps):
                act.wait_ge(shift, n + 1)
                if n >= 2:
                    act.wait_ge(turned, n - 1)
                    act.wait_ge(left, n - 1)
                src = sm[:, n % 2, 0:keys] if mask is not None else ps[:, 2 * (n % 2):2 * (n % 2) + 2, :].rearrange("p a b -> p (a b)")[:, 0:keys]
                act.activation(prob[:, n % 2, 0:keys], src, ACT.Exp, scale=scale, bias=stat[:, n % 2, 1:2],
                               accum_out=stat[:, n % 2, 2:3])
                act.drain().then_inc(prob_s, 1)
                if n >= 1:
                    copy_turned(n - 1)
            copy_turned(len(steps) - 1)

        @block.vector
        def _(dve):
            def finish(n):
                keys, out = steps[n][2], steps[n][5]
                dve.wait_ge(turned, n + 1)
                if keys > HALF:
                    dve.tensor_copy(pT[:, n % 2, HALF:keys], ps[:, 5, 0:keys - HALF]).then_inc(pT_v, 1)
                else:
                    dve.drain().then_inc(pT_v, 1)
                dve.reciprocal(stat[:, n % 2, 3:4], stat[:, n % 2, 2:3])
                dve.drain()
                dve.wait_ge(outs, n + 1)
                dve.tensor_scalar(out, ps[:, 6 + n % 2, 0:width], stat[:, n % 2, 3:4], None, ALU.mult).then_inc(left, 1)

            for n, (_, _, keys, mask, _, _) in enumerate(steps):
                dve.wait_ge(score, n + 1)
                s = ps[:, 2 * (n % 2):2 * (n % 2) + 2, :].rearrange("p a b -> p (a b)")[:, 0:keys]
                if n >= 2:
                    dve.wait_ge(prob_s, n - 1)
                if mask is not None:
                    dve.tensor_tensor(sm[:, n % 2, 0:keys], s, mask, ALU.add)
                    dve.drain()
                    s = sm[:, n % 2, 0:keys]
                dve.tensor_reduce(stat[:, n % 2, 0:1], s, AX.X, ALU.max)
                dve.drain()
                dve.tensor_scalar(stat[:, n % 2, 1:2], stat[:, n % 2, 0:1], -scale, None, ALU.mult).then_inc(shift, 1)
                if n >= 1:
                    finish(n - 1)
            finish(len(steps) - 1)


def qk_prepare(env, base, q, kv, qT, kT):
    ps, ins = env.ps, env.ins
    n_q, n_k = NL * QH, NT * KVH
    with Stage(env, base) as st:
        sq = st.sb("squares", [P, NL * D])
        sq2 = st.sb("products", [P, NL * D])
        kk = st.sb("keys_twice", [P, NT, KVH * P])
        ss = st.sb("head_rms", [P, n_q + n_k])
        wq, wk = st.sb("q_weight", [P, HD]), st.sb("k_weight", [P, HD])
        cos, sin = st.sb("cos", [P, NL, HD // 2]), st.sb("sin", [P, NL, HD // 2])
        w_in, eps_in, rooted, ready = st.sem("weights_in"), st.sem("eps_in"), st.sem("rooted"), st.sem("heads_ready")
        turned, left = st.sem("turned"), st.sem("copied")
        block = st.block()
        k = kv[:, :, 0:KVH * HD]
        heads = lambda x: x.rearrange("p t (h e) -> p t h e", e=HD)

        @block.sync
        def _(sp):
            sp.dma_start(wq, ins["attn_q_norm_w"][0].partition_broadcast(P)).then_inc(w_in, 16)
            sp.dma_start(wk, ins["attn_k_norm_w"][0].partition_broadcast(P)).then_inc(w_in, 16)
            sp.dma_start(cos, ins["rope_cos"].rearrange("(t p) c -> p t c", p=P)).then_inc(w_in, 16)
            sp.dma_start(sin, ins["rope_sin"].rearrange("(t p) c -> p t c", p=P)).then_inc(w_in, 16)
            env.ring_.load_to(sp, len(env.ring_.ends) + SLOTS)

        @block.scalar
        def _(act):
            act.wait_ge(eps_in, 1)
            act.activation(ss, ss, ACT.Sqrt).then_inc(rooted, 1)

        @block.vector
        def _(dve):
            dve.wait_ge(w_in, 64)
            flat_q = flat(q)
            dve.tensor_tensor(sq, flat_q, flat_q, ALU.mult)
            s2 = sq2[:, 0:NT * KVH * HD].rearrange("p (t c) -> p t c", t=NT)
            dve.tensor_tensor(s2, k, k, ALU.mult)
            dve.drain()
            dve.tensor_reduce(ss[:, 0:n_q], sq.rearrange("p (n e) -> p n e", e=HD), AX.X, ALU.add)
            dve.tensor_reduce(ss[:, n_q:], sq2[:, 0:NT * KVH * HD].rearrange("p (n e) -> p n e", e=HD), AX.X, ALU.add)
            dve.drain()
            dve.tensor_scalar(ss, ss, 1.0 / HD, EPS, ALU.mult, ALU.add).then_inc(eps_in, 1)
            dve.wait_ge(rooted, 1)
            dve.reciprocal(ss, ss)
            dve.drain()
            for x, nt, nh, at, w in ((q, NL, QH, 0, wq), (k, NT, KVH, n_q, wk)):
                for t in range(nt):
                    xt = x[:, t, :].rearrange("p (h e) -> p h e", e=HD)
                    shape = [P, nh, HD]
                    dve.tensor_tensor(xt, xt, ss[:, at + t * nh:at + (t + 1) * nh].unsqueeze(2).broadcast_to(shape), ALU.mult)
                    dve.drain()
                    dve.tensor_tensor(xt, xt, w.unsqueeze(1).broadcast_to(shape), ALU.mult)
            dve.drain()
            half = HD // 2
            for x, nh in ((q, QH), (k, KVH)):
                for t in range(NL):
                    shape = [P, nh, half]
                    xt = x[:, t, :].rearrange("p (h e) -> p h e", e=HD)
                    lo, hi = xt[:, :, 0:half], xt[:, :, half:HD]
                    c, s = cos[:, t, :].unsqueeze(1).broadcast_to(shape), sin[:, t, :].unsqueeze(1).broadcast_to(shape)
                    a, b, d, e = (sq[:, i * nh * half:(i + 1) * nh * half].rearrange("p (h e) -> p h e", e=half) for i in range(4))
                    dve.tensor_tensor(a, lo, c, ALU.mult)
                    dve.tensor_tensor(b, hi, s, ALU.mult)
                    dve.tensor_tensor(d, hi, c, ALU.mult)
                    dve.tensor_tensor(e, lo, s, ALU.mult)
                    dve.drain()
                    dve.tensor_tensor(lo, a, b, ALU.subtract)
                    dve.tensor_tensor(hi, d, e, ALU.add)
                    dve.drain()
            for t in range(NT):
                for r in range(2):
                    dve.tensor_copy(kk[:, t, :].rearrange("p (h r e) -> p h r e", r=2, e=HD)[:, :, r, :],
                                    k[:, t, :].rearrange("p (h e) -> p h e", e=HD))
            dve.drain().then_inc(ready, 1)
            n = 0
            for j in range(QH // 2):
                dve.wait_ge(turned, n + 1)
                dve.tensor_copy(qT[:, j, :], ps[:, 2 * (n % 4), :]).then_inc(left, 1)
                n += 1
            for g in range(KVH):
                dve.wait_ge(turned, n + 1)
                b = 2 * (n % 4)
                dve.tensor_copy(kT[:, g, :], ps[:, b:b + 2, :].rearrange("p a b -> p (a b)")[:, 0:TOK]).then_inc(left, 1)
                n += 1

        @block.tensor
        def _(pe):
            pe.wait_ge(ready, 1)
            n = 0
            for src, nt, m in ((q, NL, QH // 2), (kk, NT, KVH)):
                for j in range(m):
                    if n >= 4:
                        pe.wait_ge(left, n - 3)
                    for t in range(nt):
                        tr = pe.transpose(ps[:, 2 * (n % 4) + t // 4, (t % 4) * P:(t % 4 + 1) * P], src[:, t, j * P:(j + 1) * P],
                                          env.ident[:])
                    tr.then_inc(turned, 1)
                    n += 1


def norm_rows(env, base, X, nt, weight):
    with Stage(env, base) as st:
        junk = st.sb("squares", [P, D])
        ss = st.sb("mean_square", [P, nt])
        row = st.sb("weight_rows", [P, D])
        w_in, squared, eps_in, rooted = st.sem("weight_in"), st.sem("squared"), st.sem("eps_in"), st.sem("rooted")
        block = st.block()

        @block.sync
        def _(sp):
            sp.dma_start(row, weight.partition_broadcast(P)).then_inc(w_in, 16)

        @block.scalar
        def _(act):
            for t in range(nt):
                act.drain()
                act.activation(junk, X[:, t, :], ACT.Square, scale=float(D) ** -0.5, accum_out=ss[:, t:t + 1]).then_inc(squared, 1)
            act.wait_ge(eps_in, 1)
            act.activation(ss, ss, ACT.Sqrt).then_inc(rooted, 1)

        @block.vector
        def _(dve):
            dve.wait_ge(squared, nt)
            dve.tensor_scalar(ss, ss, EPS, None, ALU.add).then_inc(eps_in, 1)
            dve.wait_ge(rooted, 1)
            dve.reciprocal(ss, ss)
            dve.drain()
            dve.wait_ge(w_in, 16)
            for t in range(nt):
                dve.scalar_tensor_tensor(X[:, t, :], X[:, t, :], ss[:, t:t + 1], row, ALU.mult, ALU.mult)


PAD3, PAD15 = TAPS2 - 1, 15


def recurrence(env, base, lx, gate, yT):
    ps, ins = env.ps, env.ins
    with Stage(env, base) as st:
        wg = st.sb("gate_blocks", [P, 2, 4 * P])
        ua = st.sb("convolved", [P, 4, LAT])
        ri = st.sb("sigmoids", [P, 2, LAT])
        w, sw, q, a = (st.sb(n, [P, LAT]) for n in ("w", "sqrt_w", "q", "decay"))
        sp_ = [st.sb(f"softplus{i}", [P, 4]) for i in range(6)]
        zeroed, w_in, conv = st.sem("blocks_zeroed"), st.sem("blocks_in"), st.sem("convolved")
        neg, ex, scl = st.sem("negated"), st.sem("exponent"), st.sem("scale_ready")
        sums, sig, th, done = st.sem("gate_sums"), st.sem("sigmoids"), st.sem("tanh_sqrt"), st.sem("tile_done")
        block = st.block()

        @block.sync
        def _(sp):
            sp.wait_ge(zeroed, 1)
            for m, name in enumerate(("lru_w_a_2", "lru_w_x_2")):
                for b in range(2):
                    src = ins[name][0].rearrange("(c b) i j -> b i c j", b=2)[b]
                    dst = wg[b * 64:(b + 1) * 64, m, :].rearrange("p (c j) -> p c j", c=4)[:, :, b * 64:(b + 1) * 64]
                    sp.dma_start(dst, src).then_inc(w_in, 16)
            env.ring_.load_to(sp, len(env.ring_.ends) + SLOTS)

        @block.tensor
        def _(pe):
            pe.wait_ge(w_in, 64)
            for c in range(4):
                pe.wait_ge(conv, c + 1)
                if c >= 2:
                    pe.wait_ge(sig, c - 1)
                for m in range(2):
                    mm = pe.matmul(ps[:, 2 * (c % 2) + m, :], wg[:, m, c * P:(c + 1) * P], ua[:, c, :], start=True, stop=True)
                mm.then_inc(sums, 1)

        @block.scalar
        def _(act):
            act.wait_ge(neg, 1)
            act.activation(sp_[1], sp_[1], ACT.Exp).then_inc(ex, 1)
            act.wait_ge(scl, 1)
            for c in range(4):
                act.wait_ge(sums, c + 1)
                if c >= 1:
                    act.wait_ge(done, c)
                act.activation(ri[:, 0, :], ps[:, 2 * (c % 2), :], ACT.Sigmoid, bias=col(env, "lru_b_a_2", c))
                act.activation(ri[:, 1, :], ps[:, 2 * (c % 2) + 1, :], ACT.Sigmoid, bias=col(env, "lru_b_x_2", c))
                act.drain().then_inc(sig, 1)
                act.activation(w, ri[:, 0, :], ACT.Tanh, scale=sp_[5][:, c:c + 1])
                act.drain()
                act.activation(sw, w, ACT.Sqrt)
                act.drain().then_inc(th, 1)

        @block.vector
        def _(dve):
            dve.memset(wg, 0.0).then_inc(zeroed, 1)
            at = env.col_at["lru_a_param_2"]
            v, e, s, q4, p, out = sp_
            dve.tensor_scalar(v, env.cols[:, at:at + 4], -1.0, None, ALU.mult)
            dve.drain()
            dve.scalar_tensor_tensor(e, v, -1.0, v, ALU.mult, ALU.min).then_inc(neg, 1)
            dve.tensor_scalar(v, v, 0.0, None, ALU.max)
            dve.wait_ge(ex, 1)
            log1p_steps(dve, e, s, q4, p)
            dve.scalar_tensor_tensor(v, p, 2.0, v, ALU.mult, ALU.add)
            dve.drain()
            dve.tensor_scalar(out, v, 4.0, None, ALU.mult).then_inc(scl, 1)
            for c in range(4):
                u = ua[:, c, :]
                dve.tensor_scalar(u, lx[:, c, 0:LAT], col(env, "conv_w_2", c), col(env, "conv_b_2", c), ALU.mult, ALU.add)
                for j in range(1, TAPS2):
                    dve.drain()
                    last = dve.scalar_tensor_tensor(u, lx[:, c, j:j + LAT], col(env, "conv_w_2", 4 * j + c), u, ALU.mult, ALU.add)
                last.then_inc(conv, 1)
            for c in range(4):
                u = ua[:, c, :]
                dve.wait_ge(th, c + 1)
                dve.tensor_scalar(q, w, 1.0, None, ALU.add)
                dve.tensor_scalar(a, w, -1.0, 1.0, ALU.mult, ALU.add)
                dve.drain()
                dve.reciprocal(q, q)
                dve.tensor_tensor(u, u, ri[:, 1, :], ALU.mult)
                dve.drain()
                dve.tensor_tensor(a, a, q, ALU.mult)
                dve.scalar_tensor_tensor(q, q, 2.0, sw, ALU.mult, ALU.mult)
                dve.drain()
                dve.tensor_tensor(u, u, q, ALU.mult).then_inc(done, 1)
                dve.drain()
                dve.tensor_tensor_scan(yT[:, c, :], a, u, 0.0, ALU.mult, ALU.add)
                dve.drain()
                dve.tensor_tensor(yT[:, c, :], yT[:, c, :], gate[:, c, :], ALU.mult)


def pool_branch(env, base, pl, yT):
    ps, ins = env.ps, env.ins
    with Stage(env, base) as st:
        wp = st.sb("w_pool", [P, 4, P])
        s = [st.sb(f"window_sum{i}", [P, PAD15 + LAT]) for i in range(2)]
        pooled = st.sb("pooled", [P, 4, LAT])
        cnt = st.sb("counts", [P, 4, 16])
        w_in, ready, mixed = st.sem("w_in"), st.sem("pooled"), st.sem("mixed")
        block = st.block()

        @block.sync
        def _(sp):
            sp.dma_start(wp, ins["w_pool_2"][0].rearrange("g c d -> c g d")).then_inc(w_in, 16)
            env.ring_.load_to(sp, len(env.ring_.ends) + SLOTS)

        @block.tensor
        def _(pe):
            pe.wait_ge(w_in, 16)
            for g in range(4):
                pe.wait_ge(ready, g + 1)
                pe.matmul(ps[:, g, :], wp[:, g, :], pooled[:, g, :], start=True, stop=True).then_inc(mixed, 1)

        @block.scalar
        def _(act):
            for g in range(4):
                act.wait_ge(mixed, g + 1)
                act.activation(yT[:, g, :], ps[:, g, :], ACT.Copy, scale=col(env, "pool_scale_2", g))

        @block.vector
        def _(dve):
            n = PAD15 + LAT
            for g in range(4):
                dve.tensor_scalar(cnt[:, g, :], env.iota[:, 0:16], float(2 << g), None, ALU.min)
            dve.drain()
            dve.reciprocal(cnt, cnt)
            for g in range(4):
                src, step = pl[:, g, :], 1
                for r in range(g + 1):
                    dst = s[r % 2]
                    dve.drain()
                    dve.tensor_copy(dst[:, 0:step], src[:, 0:step])
                    dve.tensor_tensor(dst[:, step:n], src[:, step:n], src[:, 0:n - step], ALU.add)
                    src, step = dst, 2 * step
                dve.drain()
                x = pl[:, g, PAD15:n]
                dve.scalar_tensor_tensor(pooled[:, g, 16:LAT], src[:, PAD15 + 16:n], 1.0 / step, x[:, 16:LAT], ALU.mult, ALU.subtract)
                dve.tensor_tensor(pooled[:, g, 0:16], src[:, PAD15:PAD15 + 16], cnt[:, g, :], ALU.mult)
                dve.drain()
                dve.tensor_tensor(pooled[:, g, 0:16], pooled[:, g, 0:16], x[:, 0:16], ALU.subtract)
                dve.drain().then_inc(ready, 1)


def index_masks(env, base, qi, ki, wi, mask):
    ps = env.ps
    heads, chunk, top_k = 8, 64, 128
    with Stage(env, base) as st:
        r = st.sb("relu", [P, 2, LAT])
        sc = st.sb("scores", [P, 2, LAT])
        work = st.sb("left_to_pick", [P, 2, LAT])
        top = st.sb("top8", [P, 8])
        w8 = st.sb("weights", [P, NL, heads])
        logit, relu, used = st.sem("logits"), st.sem("relu_done"), st.sem("relu_used")
        block = st.block()
        order = [(t, h) for t in range(NL) for h in range(heads)]

        @block.sync
        def _(sp):
            env.ring_.load_to(sp, len(env.ring_.ends) + SLOTS)

        @block.tensor
        def _(pe):
            for n, (t, h) in enumerate(order):
                if n >= 4:
                    pe.wait_ge(relu, n - 3)
                b = slice((h % 2) * 64, (h % 2 + 1) * 64)
                pe.matmul(ps[:, n % 4, 0:(t + 1) * P], qi[b, h // 2, t * P:(t + 1) * P], ki[b, 0:(t + 1) * P],
                          start=True, stop=True).then_inc(logit, 1)

        @block.scalar
        def _(act):
            for n, (t, h) in enumerate(order):
                act.wait_ge(logit, n + 1)
                if n >= 2:
                    act.wait_ge(used, n - 1)
                act.activation(r[:, n % 2, 0:(t + 1) * P], ps[:, n % 4, 0:(t + 1) * P], ACT.Relu, scale=64 ** -0.5).then_inc(relu, 1)

        @block.vector
        def _(dve):
            dve.tensor_scalar(w8, wi, heads ** -0.5, None, ALU.mult)
            n = 0
            for t in range(NL):
                keys = (t + 1) * P
                s = sc[:, t % 2, 0:keys]
                dve.drain()
                for h in range(heads):
                    dve.wait_ge(relu, n + 1)
                    if h == 0:
                        dve.tensor_scalar(s, r[:, n % 2, 0:keys], w8[:, t, h:h + 1], None, ALU.mult).then_inc(used, 1)
                    else:
                        dve.scalar_tensor_tensor(s, r[:, n % 2, 0:keys], w8[:, t, h:h + 1], s, ALU.mult, ALU.add).then_inc(used, 1)
                    dve.drain()
                    n += 1
                dve.memset(sc[0:chunk, t % 2, keys - chunk:keys], NEG)
                dve.drain()
                if t == 0:
                    dve.tensor_scalar(mask[:, t, 0:keys], s, NEG / 2, -1e30, ALU.is_lt, ALU.mult)
                    continue
                a = s
                for k in range(top_k // 8):
                    b = work[:, k % 2, 0:keys]
                    dve.max(top, a)
                    dve.drain()
                    dve.match_replace(b, top, a, NEG)
                    dve.drain()
                    a = b
                dve.tensor_tensor(mask[:, t, 0:keys], a, s, ALU.is_ge)
                dve.drain()
                dve.tensor_scalar(mask[:, t, 0:keys], mask[:, t, 0:keys], -1e30, None, ALU.mult)


def merge(env, base, hT, branches, mT):
    ps, ring = env.ps, env.ring_
    with Stage(env, base) as st:
        gs = st.sb("gates", [P, 4, LAT])
        tmp = st.sb("gated", [P, 2, LAT])
        sig, used = st.sem("gates_ready"), st.sem("ups_used")
        first, m0 = ring.take([4, 4] * 6)
        block = st.block()

        @block.sync
        def _(sp):
            ring.load_to(sp, len(ring.ends) + SLOTS)

        @block.tensor
        def _(pe):
            for c in range(6):
                dg, n = c // 3, c % 3
                for part in range(2):
                    k_ = first + 2 * c + part
                    ring.wait(pe, k_)
                    kd, src = (KD, hT) if part == 0 else (4, branches[n])
                    w = ring.view(k_, kd, HALF)
                    for f in range(4):
                        if c >= 1:
                            pe.wait_ge(*((sig, 4 * (c - 1) + f + 1) if part == 0 else (used, 4 * (c - 1) + f + 1)))
                        for k in range(kd):
                            mm = pe.matmul(ps[:, 4 * part + f, :], w[:, k, f * P:(f + 1) * P], src[:, k, :], start=k == 0, stop=k == kd - 1)
                        mm.then_inc(ring.done, 1)

        @block.scalar
        def _(act):
            for c in range(6):
                dg, n = c // 3, c % 3
                for f in range(4):
                    act.wait_ge(ring.done, m0 + 8 * c + f + 1)
                    if c >= 1:
                        act.wait_ge(used, 4 * (c - 1) + f + 1)
                    act.activation(gs[:, f, :], ps[:, f, :], ACT.Sigmoid, bias=col(env, "b_gate_2", n * KD + dg * 4 + f)).then_inc(sig, 1)

        @block.vector
        def _(dve):
            for c in range(6):
                dg, n = c // 3, c % 3
                for f in range(4):
                    dve.wait_ge(ring.done, m0 + 8 * c + 4 + f + 1)
                    dve.wait_ge(sig, 4 * c + f + 1)
                    m = mT[:, dg * 4 + f, :]
                    dst = m if n == 0 else tmp[:, f % 2, :]
                    dve.tensor_tensor(dst, gs[:, f, :], ps[:, 4 + f, :], ALU.mult).then_inc(used, 1)
                    if n > 0:
                        dve.drain()
                        dve.tensor_tensor(m, m, tmp[:, f % 2, :], ALU.add)


def ffn_hidden(env, base, hT, aT):
    ps, ring = env.ps, env.ring_
    tiles = FF // P
    sizes = [min(4, tiles - 4 * c) for c in range(-(-tiles // 4))]
    with Stage(env, base) as st:
        sg = st.sb("silu_gate", [P, 4, LAT])
        act_s, used = st.sem("silu_done"), st.sem("ups_used")
        marks = [m for m in sizes for _ in range(2)]
        first, m0 = ring.take(marks)
        block = st.block()

        @block.sync
        def _(sp):
            ring.load_to(sp, len(ring.ends) + SLOTS)

        @block.tensor
        def _(pe):
            for c, m in enumerate(sizes):
                for part in range(2):
                    k_ = first + 2 * c + part
                    ring.wait(pe, k_)
                    w = ring.view(k_, KD, m * P)
                    for f in range(m):
                        if c >= 1:
                            pe.wait_ge(*((act_s, 4 * (c - 1) + f + 1) if part == 0 else (used, 4 * (c - 1) + f + 1)))
                        for k in range(KD):
                            mm = pe.matmul(ps[:, 4 * part + f, :], w[:, k, f * P:(f + 1) * P], hT[:, k, :], start=k == 0, stop=k == KD - 1)
                        mm.then_inc(ring.done, 1)

        @block.scalar
        def _(act):
            for c, m in enumerate(sizes):
                for f in range(m):
                    act.wait_ge(ring.done, m0 + 8 * c + f + 1)
                    if c >= 1:
                        act.wait_ge(used, 4 * (c - 1) + f + 1)
                    act.activation(sg[:, f, :], ps[:, f, :], ACT.Silu).then_inc(act_s, 1)

        @block.vector
        def _(dve):
            for c, m in enumerate(sizes):
                for f in range(m):
                    dve.wait_ge(ring.done, m0 + 8 * c + m + f + 1)
                    dve.wait_ge(act_s, 4 * c + f + 1)
                    dve.tensor_tensor(aT[:, 4 * c + f, :], sg[:, f, :], ps[:, 4 + f, :], ALU.mult).then_inc(used, 1)


def store(env, X, out):
    with Stage(env, X_END) as st:
        stored = st.sem("stored")
        block = st.block()

        @block.sync
        def _(sp):
            sp.dma_start(out[0].rearrange("(t p) d -> p t d", p=P), X[:, 0:NL, :]).then_inc(stored, 16)
            sp.wait_ge(stored, 16)


def build(nc, ins, out):
    env = Env()
    env.nc, env.ins, env.out, env.stage, env.col_at = nc, ins, out, 0, {}

    def dram(name, shape):
        return nc.dram_tensor(name, shape, F32).ap()

    env.mod_dram = dram("mod_rows_dram", (2, 2, 6 * D))
    env.z_dram = dram("z_dram", (NT, P, DI))
    env.x_dram = dram("x_dram", (NT, P, DI))
    env.b_dram = dram("b_dram", (NT, P, G * NS))
    env.bt_dram = dram("bt_dram", (P, G, TOK))
    env.ct_dram = dram("ct_dram", (P, G, TOK))

    def kview(w, cols):
        return w[:, cols].rearrange("(k p) n -> p k n", p=P)

    with ExitStack() as es:
        sb = lambda name, shape: es.enter_context(nc.sbuf_tensor(name, shape, F32))
        env.tiles, env.area_at = 0, -(-nc.sbuf_base // 32) * 32
        env.area = sb("area", [P, AREA])
        env.ring = sb("ring", [P, SLOTS, SLOT])
        env.hi = es.enter_context(nc.sbuf_tensor("weights_high", [P, CUTS, CUT], F32R))
        env.lo = es.enter_context(nc.sbuf_tensor("weights_low", [P, CUTS, CUT], F32R))
        env.cols = sb("param_columns", [P, 3 * P])
        env.ident, env.ones, env.iota = sb("identity", [P, P]), sb("ones", [P, P]), sb("iota", [P, P])
        env.ident_b = es.enter_context(nc.sbuf_tensor("identity_bf16", [P, P], BF16))
        env.mask_b = es.enter_context(nc.sbuf_tensor("order_mask", [P, 2, P], BF16))
        env.tri = sb("triangles", [P, 4, P])
        env.cond, env.modc = sb("conditions", [P, KD, 2]), sb("modulation_columns", [P, 4, 2, KD])
        env.dtb, env.zero = sb("dt_bias", [P, 2 * H]), sb("zero", [P, 8])
        env.ps = es.enter_context(nc.psum_tensor("ps", [P, 8, HALF], F32))
        env.landed = [es.enter_context(nc.semaphore(f"slot{i}_landed")) for i in range(SLOTS)]
        env.marks = es.enter_context(nc.semaphore("matmul_marks"))
        env.cut_sems = [es.enter_context(nc.semaphore(n)) for n in ("high_parts", "low_parts_by_dve", "low_parts_by_pool", "parts_used")]
        banks = []
        for b in range(2):
            held = ExitStack()
            nums = [held.enter_context(nc.semaphore(f"bank{b}_{i}")).num for i in range(32)]
            banks.append((held, nums))
        env.sem_banks = [nums for _, nums in banks]
        for held, _ in banks:
            held.close()

        chunks = []
        halves = lambda w, a, b: [kview(w, slice(c, min(c + HALF, b))) for c in range(a, b, HALF)]
        chunks += halves(ins["ada_w"][0], 0, 6 * D)
        w = ins["ssd_in_w"][0]
        nx = DI + 2 * G * NS
        chunks += halves(w, 0, DI) + halves(w, DI + nx, DI + nx + 2 * H) + halves(w, DI, DI + nx)
        w = ins["ssd_out_w"][0]
        for n in range(2):
            for c in range(2):
                chunks.append(kview(w[c * D:(c + 1) * D, :], slice(n * HALF, (n + 1) * HALF)))
        def moe_chunks(layer):
            return [kview(ins[n][layer, e], slice(h * HALF, (h + 1) * HALF))
                    for e in range(E) for n in ("moe_w1", "moe_w3", "moe_w2") for h in range(2)]

        chunks += moe_chunks(0)
        chunks += halves(ins["ada_w"][1], 0, 6 * D)
        chunks += halves(ins["attn_qkv_w"][0], 0, 1536) + halves(ins["attn_out_w"][0], 0, D)
        chunks += moe_chunks(1)
        w = ins["w_in_2"][0]
        chunks += halves(w, 0, 2048) + halves(w, 2048, 2176) + halves(w, 2176, 2688) + halves(w, 2688, 2760)
        for dg in range(2):
            for n in range(3):
                a = 2760 + n * D + dg * HALF
                chunks += halves(w, a, a + HALF) + halves(ins["w_branch_2"][0, n], dg * HALF, (dg + 1) * HALF)
        chunks += halves(ins["w_out_2"][0], 0, D)
        chunks += halves(ins["w_mem_q_2"][0], 0, HALF) + halves(ins["w_mem_kv_2"][0], 0, D) + halves(ins["w_mem_o_2"][0], 0, D)
        w = ins["w_ffn_in_2"][0]
        for a in range(0, FF, HALF):
            b = min(a + HALF, FF)
            chunks += halves(w, a, b) + halves(w, FF + a, FF + b)
        w = ins["w_ffn_out_2"][0]
        for n in range(2):
            for a in range(0, FF, D):
                chunks.append(kview(w[a:min(a + D, FF), :], slice(n * HALF, (n + 1) * HALF)))
        env.ring_ = Ring(env, chunks)

        X = carve(env, 0, [P, NT, D])
        mc = lambda q, u: (lambda k: env.modc[:, q, u, k:k + 1])
        setup(env)
        modulation(env, 0)
        t = Env()
        t.dt, t.a = carve(env, 0, [P, NT, 2 * H]), carve(env, NT * 2 * H, [P, NT, 2 * H])
        base = 2 * NT * 2 * H
        t.hT = carve(env, base, [P, KD, TOK])
        xin = [(i, ins["x"][0, i * P:(i + 1) * P, :]) for i in range(NL)]
        xin += [(NL + i, ins["ctx"][0, i * P:(i + 1) * P, :]) for i in range(NC)]
        b1 = base + KD * TOK
        Xt = carve(env, b1, [P, NT, D])
        norm_turn(env, b1 + NT * D, Xt, t.hT, [(0, NL, mc(1, 0), mc(0, 0)), (NL, NC, mc(1, 1), mc(0, 1))], load=xin)
        ssd_project(env, t, b1)
        t.y = carve(env, base, [P, NT, DI])
        ssd_scan(env, t, base + NT * DI)
        ssd_gate(env, t, base + NT * DI)
        t.yT = carve(env, base + NT * DI, [P, 2 * KD, TOK])
        nw = lambda k: col(env, "ssd_norm_w", k)
        norm_turn(env, base + 2 * NT * DI, t.y, t.yT, [(0, NL, nw, None), (NL, NC, nw, None)], width=DI, token_out=t.y)
        md = env.mod_dram
        project_add(env, base + 2 * NT * DI, X, t.yT, 2 * KD, list(range(NT)),
                    gate=(lambda i: int(i >= NL), [md[0, 0, 2 * D:3 * D], md[0, 1, 2 * D:3 * D]]), load=xin)
        moe(env, 0, X, NT)

        modulation(env, 1)
        hT = carve(env, X_END, [P, KD, TOK])
        at = X_END + KD * TOK
        norm_turn(env, at, X, hT, [(0, NL, mc(1, 0), mc(0, 0)), (NL, NC, mc(1, 1), mc(0, 1))])
        q, kv = carve(env, at, [P, NL, D]), carve(env, at + NL * D, [P, NT, HALF])
        top = at + NL * D + NT * HALF
        jobs = [(KD, HALF, [tokens(hT, t_, slice(0, HALF), copy_to(q[:, t_, h * HALF:(h + 1) * HALF])) for t_ in range(NL)])
                for h in range(2)]
        jobs.append((KD, HALF, [tokens(hT, t_, slice(0, HALF), copy_to(kv[:, t_, :])) for t_ in range(NT)]))
        project(env, top, jobs)
        qT, kT = carve(env, X_END, [P, QH // 2, LAT]), carve(env, top, [P, KVH, TOK])
        qk_prepare(env, top + KVH * TOK, q, kv, qT, kT)
        o = q
        steps = []
        for h in range(QH):
            b, g = slice((h % 2) * HD, (h % 2 + 1) * HD), h // (QH // KVH)
            vs = [kv[:, t_, KVH * HD + g * HD:KVH * HD + (g + 1) * HD] for t_ in range(NT)]
            for t_ in range(NL):
                steps.append((qT[b, h // 2, t_ * P:(t_ + 1) * P], kT[b, g, :], TOK, None, vs, o[:, t_, h * HD:(h + 1) * HD]))
        attend(env, top + KVH * TOK, steps, HD ** -0.5, HD)
        oT = carve(env, X_END, [P, KD, LAT])
        turn(env, at + NL * D, o, oT, NL, KD)
        project_add(env, at, X, oT, KD, list(range(NL)), gate=(lambda i: 0, [env.mod_dram[1, 0, 2 * D:3 * D]]))
        moe(env, 1, X, NL)
        norm_rows(env, X_END, X, NL, ins["final_norm_w"])

        NLD = NL * D
        hT = carve(env, NLD, [P, KD, LAT])
        norm_turn(env, 2 * NLD, X, hT, [(0, NL, lambda k: col(env, "g_mix_pre_2", k), None)])
        at = 2 * NLD
        part = {}
        for name, shape in (("lx", [P, 4, PAD3 + LAT]), ("gate", [P, 4, LAT]), ("pool", [P, 4, PAD15 + LAT]), ("q", [P, 4, LAT]),
                            ("qi", [P, 4, LAT]), ("k", [P, LAT]), ("ki", [P, LAT]), ("v", [P, NL, HD]), ("wi", [P, NL, 8]),
                            ("ya", [P, 4, LAT]), ("yb", [P, 4, LAT]), ("yc", [P, 4, LAT])):
            part[name] = carve(env, at, shape)
            at += int(np.prod(shape[1:]))
        all_ = slice(0, LAT)

        def wide(name, pad, func=ACT.Copy):
            def copies(f):
                dst = part[name][:, f, pad:pad + LAT]

                def go(act, s):
                    if pad:
                        act.activation(part[name][:, f, 0:pad], s[:, 0:pad], ACT.Copy, scale=0.0)
                    return act.activation(dst, s, func)
                return go
            return (KD, HALF, [features(hT, f, all_, copies(f)) for f in range(4)])

        def twice(dst, cols):
            def copies(act, s):
                act.activation(dst[0:HD, :], s, ACT.Copy)
                return act.activation(dst[HD:P, :], s, ACT.Copy)
            return (lambda k, w: (w[:, k, cols], hT[:, k, all_])), HD, LAT, copies

        jobs = [wide("lx", PAD3), wide("gate", 0, ACT.Gelu_apprx_tanh), wide("pool", PAD15), wide("q", 0)]
        jobs.append((KD, 2 * HD, [twice(part["k"], slice(0, HD))]
                     + [tokens(hT, t_, slice(HD, 2 * HD), copy_to(part["v"][:, t_, :])) for t_ in range(NL)]))
        jobs.append(wide("qi", 0))
        jobs.append((KD, HD + 8, [twice(part["ki"], slice(0, HD))]
                     + [tokens(hT, t_, slice(HD, HD + 8), copy_to(part["wi"][:, t_, :])) for t_ in range(NL)]))
        project(env, at, jobs)
        recurrence(env, at, part["lx"], part["gate"], part["ya"])
        pool_branch(env, at, part["pool"], part["yb"])
        mask = carve(env, 2 * NLD, [P, NL, LAT])
        index_masks(env, at, part["qi"], part["ki"], part["wi"], mask)
        o = carve(env, 2 * NLD + NL * LAT, [P, NL, LAT])
        steps = []
        for t_ in range(NL):
            for h in range(8):
                b, keys = slice((h % 2) * HD, (h % 2 + 1) * HD), (t_ + 1) * P
                steps.append((part["q"][b, h // 2, t_ * P:(t_ + 1) * P], part["k"][b, :], keys, mask[:, t_, 0:keys],
                              [part["v"][:, k, :] for k in range(t_ + 1)], o[:, t_, h * HD:(h + 1) * HD]))
        attend(env, at, steps, HD ** -0.5, HD)
        turn(env, at, o, part["yc"], NL, 4)
        mT = carve(env, 2 * NLD, [P, KD, LAT])
        merge(env, at, hT, [part["ya"], part["yb"], part["yc"]], mT)
        project_add(env, 3 * NLD, X, mT, KD, list(range(NL)), norm=ins["g_mix_post_2"][0])

        NM = 2
        mem = carve(env, 2 * NLD, [P, NM, D])
        memT = carve(env, 2 * NLD + NM * D, [P, KD, NM * P])
        at = 2 * NLD + 2 * NM * D
        norm_turn(env, at, mem, memT, [(0, NM, lambda k: col(env, "g_mem_kv_2", k), None)],
                  load=[(i, ins["mem_2"][0, i * P:(i + 1) * P, :]) for i in range(NM)])
        norm_turn(env, at, X, hT, [(0, NL, lambda k: col(env, "g_mem_pre_2", k), None)])
        qT, kT, v = carve(env, at, [P, 4, LAT]), carve(env, at + 4 * LAT, [P, 4, NM * P]), carve(env, at + 6 * LAT, [P, NM, LAT])
        o, oT = carve(env, at + 8 * LAT, [P, NL, LAT]), carve(env, at + 12 * LAT, [P, 4, LAT])
        at += 16 * LAT
        ms = slice(0, NM * P)
        project(env, at, [(KD, HALF, [features(hT, f, all_, copy_to(qT[:, f, :])) for f in range(4)]),
                          (KD, HALF, [features(memT, f, ms, copy_to(kT[:, f, :])) for f in range(4)]),
                          (KD, HALF, [tokens(memT, t_, slice(0, HALF), copy_to(v[:, t_, :])) for t_ in range(NM)])])
        steps = [(qT[:, h, t_ * P:(t_ + 1) * P], kT[:, h, :], NM * P, None, [v[:, m, h * P:(h + 1) * P] for m in range(NM)],
                  o[:, t_, h * P:(h + 1) * P]) for h in range(4) for t_ in range(NL)]
        attend(env, at, steps, P ** -0.5, P)
        turn(env, at, o, oT, NL, 4)
        project_add(env, at, X, oT, 4, list(range(NL)), norm=ins["g_mem_post_2"][0])

        norm_turn(env, 2 * NLD, X, hT, [(0, NL, lambda k: col(env, "g_ffn_pre_2", k), None)])
        aT = carve(env, 2 * NLD, [P, FF // P, LAT])
        ffn_hidden(env, 2 * NLD + FF // P * LAT, hT, aT)
        project_add(env, 2 * NLD + FF // P * LAT, X, aT, FF // P, list(range(NL)), norm=ins["g_ffn_post_2"][0])
        store(env, X, out)


_INS = ["x", "c", "ctx", "c_ctx", "ada_w", "ada_b", "norm1_w", "norm2_w", "ssd_in_w", "ssd_conv_w", "ssd_conv_b",
        "ssd_dt_bias", "ssd_A_log", "ssd_D", "ssd_norm_w", "ssd_out_w", "attn_qkv_w", "attn_q_norm_w",
        "attn_k_norm_w", "attn_out_w", "moe_router_w", "moe_w1", "moe_w3", "moe_w2", "final_norm_w", "mem_2",
        "g_mix_pre_2", "w_in_2", "conv_w_2", "conv_b_2", "lru_w_a_2", "lru_b_a_2", "lru_w_x_2", "lru_b_x_2",
        "lru_a_param_2", "w_pool_2", "pool_scale_2", "w_branch_2", "b_gate_2", "w_out_2", "g_mix_post_2",
        "g_mem_pre_2", "g_mem_kv_2", "w_mem_q_2", "w_mem_kv_2", "w_mem_o_2", "g_mem_post_2", "g_ffn_pre_2",
        "w_ffn_in_2", "w_ffn_out_2", "g_ffn_post_2", "rope_cos", "rope_sin"]


def rope_tables():
    row = np.repeat(np.arange(LAT // 64), 64).astype(np.float32)
    column = np.tile(np.arange(64), LAT // 64).astype(np.float32)
    freq = np.float32(10000.0) ** (-np.arange(0, 32, 2, dtype=np.float32) / np.float32(32))
    ang = np.concatenate([row[:, None] * freq, column[:, None] * freq], axis=-1)
    return {"rope_cos": np.cos(ang).astype(np.float32), "rope_sin": np.sin(ang).astype(np.float32)}


_NAMES = _INS[:-2]


def kernel(**inputs):
    import concourse.bacc as bacc
    from concourse.bass_utils import run_bass_kernel_spmd

    nc = bacc.Bacc("TRN2", target_bir_lowering=False, num_devices=1, dynamic_dma_scratch_size=64)
    arrays, ins = {}, {}
    values = {name: np.ascontiguousarray(inputs[name]) for name in _NAMES}
    values.update(rope_tables())
    for name in _INS:
        a = values[name]
        arrays[f"in_{name}"] = a
        ins[name] = nc.dram_tensor(f"in_{name}", a.shape, mybir.dt.from_np(a.dtype), kind="ExternalInput").ap()
    out = nc.dram_tensor("out", (1, LAT, D), F32, kind="ExternalOutput").ap()
    build(nc, ins, out)
    result = run_bass_kernel_spmd(nc, [arrays], core_ids=[0])
    return result.results[0]["out"]
```

```python
from contextlib import ExitStack

import numpy as np

import concourse.bass as bass
from concourse import mybir

F32 = mybir.dt.float32
F32R = mybir.dt.float32r
BF16 = mybir.dt.bfloat16
ALU = mybir.AluOpType
ACT = mybir.ActivationFunctionType
AX = mybir.AxisListType

P = 128
D = 1024
KD = D // P
LAT, CTX = 512, 256
NL, NC = LAT // P, CTX // P
NT = NL + NC
TOK = LAT + CTX
EPS = 1e-6
HALF = 512
DI = 2048
H = 32
HD = 64
G = 8
HPG = H // G
NS = 128
TAPS = 5
PADL = 2
LATP = LAT + 2 * PADL
PADW = LATP + CTX + 2 * PADL
E = 16
NEG = -3.0e38
QH, KVH = 16, 4
LRU_W = 512
TAPS2 = 4
FF = 2816
SLOTS = 3
X_END = NT * D
SLOT = 4096
AREA = 35072
CUT = 2 * HALF
BLOCKS = SLOT // CUT
CUTS = 4


def flat(ap):
    return ap.rearrange("p a b -> p (a b)")


class Ring:

    def __init__(self, env, plan):
        self.plan = plan
        self.slots = env.ring
        self.landed = env.landed
        self.done = env.marks
        self.loaded = 0
        self.marks = 0
        self.blocks = self.blocks_v = self.blocks_p = 0
        self.ends = []
        self.hi, self.lo = env.hi, env.lo
        self.high, self.low_v, self.low_p, self.used, self.high_s = env.cut_sems
        self.act, self.highs = env.nc.scalar, 0

    def view(self, k, a, b):
        return self.slots[:, k % SLOTS, 0:a * b].rearrange("p (a b) -> p a b", a=a)

    def take(self, marks):
        first, before = len(self.ends), self.marks
        for m in marks:
            self.marks += m
            self.ends.append([(self.done, self.marks)])
        return first, before

    def take_split(self, blocks):
        first, before = len(self.ends), (self.blocks, self.blocks_v, self.blocks_p)
        for n in blocks:
            self.blocks += n
            self.blocks_v += min(n, 3)
            self.blocks_p += n // 4
            self.ends.append([(self.low_v, self.blocks_v)] + ([(self.low_p, self.blocks_p)] if n == 4 else []))
        return (first, *before)

    def take_cut(self, chunks):
        before, blocks_before, out = self.marks, self.blocks_p, []
        for blocks in chunks:
            if isinstance(blocks, int):
                self.marks += blocks
                self.ends.append([(self.done, self.marks)])
                continue
            for ks, cols, marks in blocks:
                self.marks += marks
                self.blocks_p += 1
                out.append((len(self.ends), ks, cols, self.marks))
            self.ends.append([(self.low_p, self.blocks_p)])
        return out, before, blocks_before

    def cut_high(self, eng, blocks, views, m):
        k, ks, cols, _ = blocks[m]
        if m == 0 or blocks[m - 1][0] != k:
            self.wait(eng, k)
        if m >= CUTS:
            eng.wait_ge(self.done, blocks[m - CUTS][3])
        src, hi = views[k][:, ks, cols], self.part(self.hi, m, ks, cols)
        if eng is self.act:
            return eng.activation(hi, src, ACT.Copy)
        return eng.tensor_copy(hi, src)

    def cut_low(self, pool, blocks, views, m):
        k, ks, cols, _ = blocks[m]
        hi, lo = self.part(self.hi, m, ks, cols), self.part(self.lo, m, ks, cols)
        pool.tensor_tensor(lo, views[k][:, ks, cols], hi, ALU.subtract).then_inc(self.low_p, 1)

    def cut(self, pool, blocks, views):
        for m in range(len(blocks)):
            self.cut_high(pool, blocks, views, m)
            pool.drain()
            self.cut_low(pool, blocks, views, m)

    def cut_after(self, act, blocks, views, m, marks):
        while m < len(blocks) and (m < CUTS or blocks[m - CUTS][3] <= marks):
            self.cut_high(act, blocks, views, m).then_inc(self.high_s, 1)
            m += 1
        return m

    def cut_rest(self, pool, blocks, views):
        for m in range(len(blocks)):
            self.highs += 1
            pool.wait_ge(self.high_s, self.highs)
            self.cut_low(pool, blocks, views, m)

    def part(self, x, m, ks, cols):
        a, b = ks.stop - ks.start, cols.stop - cols.start
        return x[:, m % CUTS, 0:a * b].rearrange("p (a b) -> p a b", a=a)

    def load_to(self, sp, end):
        while self.loaded < min(end, len(self.plan)):
            k = self.loaded
            if k >= SLOTS:
                for sem, count in self.ends[k - SLOTS]:
                    sp.wait_ge(sem, count)
            src = self.plan[k]
            sp.dma_start(self.view(k, src.shape[1], src.shape[2]), src).then_inc(self.landed[k % SLOTS], 16)
            self.loaded += 1

    def wait(self, pe, k):
        pe.wait_ge(self.landed[k % SLOTS], 16 * (k // SLOTS + 1))


class Stage:

    def __init__(self, env, base):
        self.env = env
        self.at = base

    def __enter__(self):
        self.es = ExitStack()
        self.bank = self.env.sem_banks[self.env.stage % 2]
        self.other = self.env.sem_banks[(self.env.stage + 1) % 2]
        self.env.stage += 1
        self.n = 0
        return self

    def sb(self, name, shape):
        size = int(np.prod(shape[1:]))
        self.at += size
        assert self.at <= AREA, (name, self.at)
        return carve(self.env, self.at - size, shape)

    def sbr(self, name, shape, dtype=F32R):
        self.at = -(-self.at // 8) * 8
        self.at += int(np.prod(shape[1:]))
        return carve_r(self.env, f"{name}_{self.env.stage}", self.at - int(np.prod(shape[1:])), shape, dtype)

    def sem(self, name):
        num = self.bank[self.n]
        self.n += 1
        return self.es.enter_context(self.env.nc.semaphore(f"{name}_{self.env.stage}", num))

    def block(self):
        b = self.es.enter_context(self.env.nc.Block())
        other = self.other

        @b.gpsimd
        def _(pool):
            pool.sem_clear(range(other[0], other[-1] + 1))

        return b

    def __exit__(self, *a):
        return self.es.__exit__(*a)


def carve(env, at, shape):
    size = int(np.prod(shape[1:]))
    assert at + size <= AREA
    v = env.area[0:shape[0], at:at + size]
    if len(shape) == 3:
        v = v.rearrange("p (a b) -> p a b", a=shape[1])
    elif len(shape) == 4:
        v = v.rearrange("p (a b c) -> p a b c", a=shape[1], b=shape[2])
    return v


def carve_r(env, name, at, shape, dtype=F32R):
    size = int(np.prod(shape[1:]))
    assert at + size <= AREA and at % 8 == 0, (name, at, size)
    env.tiles += 1
    return env.nc.alloc_sbuf_tensor_at(f"{name}_{env.tiles}", shape, dtype, offset=env.area_at + 4 * at)[:]


class Env:
    pass


PARAM_ROWS = [
    ("c", 8), ("c_ctx", 8), ("norm1_w", 16), ("norm2_w", 16), ("ssd_norm_w", 16), ("g_mix_pre_2", 8),
    ("g_mem_pre_2", 8), ("g_mem_kv_2", 8), ("g_ffn_pre_2", 8), ("ssd_conv_b", 32),
    ("ssd_conv_w", 160), ("conv_w_2", 16), ("conv_b_2", 4), ("lru_b_a_2", 4), ("lru_b_x_2", 4),
    ("lru_a_param_2", 4), ("pool_scale_2", 4), ("b_gate_2", 24),
]


def flat_rows(ap):
    names = "abcdef"[:len(ap.shape)]
    f = ap if len(ap.shape) == 1 else ap.rearrange(f"{' '.join(names)} -> ({' '.join(names)})")
    return f.rearrange("(r p) -> r p", p=P)


def setup(env):
    nc, ins = env.nc, env.ins
    with Stage(env, 0) as st:
        total = sum(n for _, n in PARAM_ROWS)
        tiles = -(-total // P)
        rows = st.sb("param_rows", [P, tiles, P])
        loaded, masks, turned = st.sem("rows_loaded"), st.sem("masks_made"), st.sem("rows_turned")
        copied = st.sem("columns_copied")
        pieces = []
        at = 0
        for name, n in PARAM_ROWS:
            env.col_at[name] = at
            src = flat_rows(ins[name])
            done = 0
            while done < n:
                k = min(n - done, P - at % P)
                pieces.append((src[done:done + k, :], at // P, at % P, k))
                at += k
                done += k
        block = st.block()
        ps = env.ps

        @block.sync
        def _(sp):
            sp.wait_ge(masks, 1)
            for src, t, r, k in pieces:
                sp.dma_start(rows[r:r + k, t, :], src).then_inc(loaded, 16)
            sp.dma_start(env.dtb[:], ins["ssd_dt_bias"].rearrange("a b c -> a (b c)")
                         .partition_broadcast(P)).then_inc(loaded, 16)
            env.ring_.load_to(sp, SLOTS)
            sp.wait_ge(loaded, 16 * (len(pieces) + 1))

        @block.gpsimd
        def _(pool):
            pool.memset(rows[:], 0.0).then_inc(masks, 1)
            pool.memset(env.ones[:], 1.0)
            pool.memset(env.ident[:], 0.0)
            for m in range(4):
                pool.memset(env.tri[:, m, :], 1.0)
            pool.drain()
            pool.affine_select(out=env.ident[:], in_=env.ident[:], compare_op=ALU.not_equal, fill=1.0,
                               base=0, pattern=[[-1, P]], channel_multiplier=1)
            for m, (op, mul, step) in enumerate([(ALU.is_ge, -1, 1), (ALU.is_ge, 1, -1),
                                                 (ALU.is_gt, 1, -1), (ALU.is_gt, -1, 1)]):
                pool.affine_select(out=env.tri[:, m, :], in_=env.tri[:, m, :], compare_op=op, fill=0.0,
                                   base=0, pattern=[[step, P]], channel_multiplier=mul)
            for m in range(2):
                pool.memset(env.mask_b[:, m, :], 0.0)
            pool.drain()
            pool.tensor_copy(env.ident_b[:], env.ident[:])
            for m, (mul, step) in enumerate([(-1, 1), (1, -1)]):
                pool.affine_select(out=env.mask_b[:, m, :], in_=env.mask_b[:, m, :], compare_op=ALU.is_ge, fill=-1e30,
                                   base=0, pattern=[[step, P]], channel_multiplier=mul)
            pool.iota(env.iota[:], pattern=[[1, P]], base=1, channel_multiplier=0,
                      allow_small_or_imprecise_dtypes=True)
            pool.drain()
            pool.memset(env.zero[:], 0.0).then_inc(masks, 1)

        @block.tensor
        def _(pe):
            pe.wait_ge(masks, 2)
            pe.wait_ge(loaded, 16 * (len(pieces) + 1))
            for t in range(tiles):
                pe.transpose(ps[:, t, 0:P], rows[:, t, :], env.ident[:]).then_inc(turned, 1)

        @block.vector
        def _(dve):
            for t in range(tiles):
                dve.wait_ge(turned, t + 1)
                dve.tensor_copy(env.cols[:, t * P:(t + 1) * P], ps[:, t, 0:P]).then_inc(copied, 1)

        @block.scalar
        def _(act):
            act.wait_ge(copied, 1)
            for v in range(2):
                act.activation(env.cond[:, :, v], env.cols[:, 8 * v:8 * v + 8], ACT.Silu)


def col(env, name, i=0):
    a = env.col_at[name] + i
    return env.cols[:, a:a + 1]


def modulation(env, layer):
    ps, ring = env.ps, env.ring_
    n_chunks = 12
    with Stage(env, 0 if layer == 0 else X_END) as st:
        mod = st.sb("mod_rows", [2, 6 * D])
        bias = st.sb("ada_bias", [2, 6 * D])
        bias_in, added, turned, stored = st.sem("bias_in"), st.sem("bias_added"), st.sem("mod_turned"), st.sem("mod_stored")
        first, m0 = ring.take([1] * n_chunks)
        block = st.block()

        @block.sync
        def _(sp):
            sp.dma_start(bias, env.ins["ada_b"][layer, :].partition_broadcast(2)).then_inc(bias_in, 16)
            ring.load_to(sp, first + n_chunks + SLOTS)
            sp.wait_ge(added, n_chunks)
            sp.dma_start(env.mod_dram[layer, :, :], mod).then_inc(stored, 16)
            sp.wait_ge(stored, 16)

        @block.tensor
        def _(pe):
            for n in range(n_chunks):
                if n >= 4:
                    pe.wait_ge(added, n - 3)
                ring.wait(pe, first + n)
                w = ring.view(first + n, KD, HALF)
                for k in range(KD):
                    mm = pe.matmul(ps[0:2, n % 4, :], env.cond[:, k, :], w[:, k, :], start=k == 0, stop=k == KD - 1)
                mm.then_inc(ring.done, 1)
            pe.wait_ge(added, n_chunks)
            for q, piece in enumerate((0, 1, 3, 4)):
                for k in range(KD):
                    a = piece * D + k * P
                    tr = pe.transpose(ps[:, 4, q * 16 + 2 * k:q * 16 + 2 * k + 2], mod[:, a:a + P], env.ident[0:2, 0:2])
            tr.then_inc(turned, 1)

        @block.vector
        def _(dve):
            dve.wait_ge(bias_in, 16)
            for n in range(n_chunks):
                dve.wait_ge(ring.done, m0 + n + 1)
                s = slice(n * HALF, (n + 1) * HALF)
                dve.tensor_tensor(mod[:, s], ps[0:2, n % 4, :], bias[:, s], ALU.add).then_inc(added, 1)
            dve.wait_ge(turned, 1)
            v = ps[:, 4, 0:64].rearrange("p (q k v) -> p q v k", q=4, k=KD)
            for q in range(4):
                dve.tensor_copy(env.modc[:, q, :, :], v[:, q, :, :])
            dve.drain()
            for q, name in ((1, "norm1_w"), (3, "norm2_w")):
                a = env.col_at[name] + layer * KD
                for u in range(2):
                    dve.scalar_tensor_tensor(env.modc[:, q, u, :], env.modc[:, q, u, :], 1.0, env.cols[:, a:a + KD],
                                             ALU.add, ALU.mult)


def products(pe, out, x, y, start, stop):
    if not isinstance(x, tuple):
        return pe.matmul(out, x, y, start=start, stop=stop)
    for n, (a, b) in enumerate(((x[0], y[0]), (x[0], y[1]), (x[1], y[0]))):
        mm = pe.matmul(out, a, b, start=start and n == 0, stop=stop and n == 2)
    return mm


def norm_turn(env, base, src, hT, groups, width=D, token_out=None, load=None, keep=None, ssd=False):
    parts = isinstance(hT, tuple)
    ps, ring = env.ps, env.ring_
    nt = sum(g[1] for g in groups)
    kd = width // P
    with Stage(env, base) as st:
        if ssd:
            xb, zb, dsk = st.sb("x_tiles", [P, 2, width]), st.sb("z_tiles", [P, 2, width]), st.sb("d_skip", [P, H])
            junk = lambda i: zb[:, i % 2, :]
        else:
            squares = st.sb("squares", [P, width])
            junk = lambda i: squares
        ss = st.sb("mean_square", [P, nt])
        rstd = st.sb("rstd", [P, nt])
        xn = token_out if token_out is not None else st.sb("scaled", [P, nt, width])
        x_in, squared, eps_in, rooted = st.sem("x_in"), st.sem("squared"), st.sem("eps_in"), st.sem("rooted")
        scaled, turned = st.sem("rows_scaled"), st.sem("turned")
        out = [st.sem("even_features_out"), st.sem("odd_features_out")]
        t0 = groups[0][0]
        whole = st.sb("features", [P, 2, HALF]) if parts else None
        kept = st.sem("copy_kept")
        parted, inverse = st.sem("parts_made"), st.sem("rstd_ready")
        d_in, dx, gated = st.sem("d_in"), st.sem("d_times_x"), st.sem("gated")
        xt_in = [st.sem("even_x_in"), st.sem("odd_x_in")]
        zt_in = [st.sem("even_z_in"), st.sem("odd_z_in")]
        block = st.block()

        @block.sync
        def _(sp):
            if load is not None:
                for t, s in load:
                    sp.dma_start(src[:, t, :], s).then_inc(x_in, 16)
            if ssd:
                sp.dma_start(dsk, env.ins["ssd_D"].rearrange("a h -> (a h)").partition_broadcast(P)).then_inc(d_in, 16)
                for i in range(nt):
                    if i >= 2:
                        sp.wait_ge(gated, i - 1)
                        sp.wait_ge(squared, i - 1)
                    sp.dma_start(xb[:, i % 2, :], env.x_dram[i, :, :]).then_inc(xt_in[i % 2], 16)
                    sp.dma_start(zb[:, i % 2, :], env.z_dram[i, :, :]).then_inc(zt_in[i % 2], 16)
            if keep is not None:
                sp.dma_start(keep.rearrange("t p d -> p t d"), src[:, 0:nt, :]).then_inc(kept, 16)
            ring.load_to(sp, len(ring.ends) + SLOTS)
            if keep is not None:
                sp.wait_ge(kept, 16)

        @block.gpsimd
        def _(pool):
            if ssd:
                pool.wait_ge(d_in, 16)
                for i in range(nt):
                    pool.wait_ge(xt_in[i % 2], 16 * (i // 2 + 1))
                    v = xb[:, i % 2, :].rearrange("p (h e) -> p h e", e=HD)
                    pool.tensor_tensor(v, v, dsk.unsqueeze(2).broadcast_to([P, H, HD]), ALU.mult).then_inc(dx, 1)

        @block.scalar
        def _(act):
            for i in range(nt + 2):
                if i < nt:
                    if load is not None:
                        act.wait_ge(x_in, 16 * len(load))
                    if ssd:
                        act.wait_ge(gated, i + 1)
                    act.drain()
                    act.activation(junk(i), src[:, t0 + i, :], ACT.Square, scale=float(width) ** -0.5,
                                   accum_out=ss[:, i:i + 1]).then_inc(squared, 1)
                if 1 <= i <= nt:
                    act.wait_ge(eps_in, i)
                    act.activation(rstd[:, i - 1:i], ss[:, i - 1:i], ACT.Sqrt).then_inc(rooted, 1)
                if ssd and i >= 2:
                    act.wait_ge(inverse, i - 1)
                    act.activation(xn[:, i - 2, :], src[:, t0 + i - 2, :], ACT.Copy, scale=rstd[:, i - 2:i - 1]).then_inc(scaled, 1)
            n = 0
            for gi, (_, m, sc, sh) in enumerate(groups):
                for k in range(kd):
                    if parts:
                        act.wait_ge(turned, n + 1)
                        if n >= 2:
                            act.wait_ge(parted, n - 1)
                        act.activation(whole[:, n % 2, 0:m * P], ps[:, n % 8, 0:m * P], ACT.Identity,
                                       scale=sc(k), bias=sh(k) if sh else 0.0).then_inc(out[n % 2], 1)
                    elif k % 2 == 1:
                        act.wait_ge(turned, n + 1)
                        o = groups[gi][0] * P
                        act.activation(hT[:, k, o:o + m * P], ps[:, n % 8, 0:m * P], ACT.Identity,
                                       scale=sc(k), bias=sh(k) if sh else 0.0).then_inc(out[1], 1)
                    n += 1

        @block.vector
        def _(dve):
            for i in range(nt + 2):
                if ssd and i < nt:
                    y = src[:, t0 + i, :]
                    dve.wait_ge(dx, i + 1)
                    dve.tensor_tensor(y, y, xb[:, i % 2, :], ALU.add)
                    dve.drain()
                    dve.wait_ge(zt_in[i % 2], 16 * (i // 2 + 1))
                    dve.tensor_tensor(y, y, zb[:, i % 2, :], ALU.mult).then_inc(gated, 1)
                if 1 <= i <= nt:
                    dve.wait_ge(squared, i)
                    dve.tensor_scalar(ss[:, i - 1:i], ss[:, i - 1:i], EPS, None, ALU.add).then_inc(eps_in, 1)
                if i >= 2:
                    dve.wait_ge(rooted, i - 1)
                    dve.reciprocal(rstd[:, i - 2:i - 1], rstd[:, i - 2:i - 1]).then_inc(inverse, 1)
                    if not ssd:
                        dve.drain()
                        dve.tensor_scalar(xn[:, i - 2, :], src[:, t0 + i - 2, :], rstd[:, i - 2:i - 1], None, ALU.mult).then_inc(scaled, 1)
            n = 0
            for gi, (_, m, sc, sh) in enumerate(groups):
                for k in range(kd):
                    if parts:
                        o = groups[gi][0] * P
                        w, hi, lo = whole[:, n % 2, 0:m * P], hT[0][:, k, o:o + m * P], hT[1][:, k, o:o + m * P]
                        dve.wait_ge(out[n % 2], n // 2 + 1)
                        dve.tensor_copy(hi, w)
                        dve.drain()
                        dve.tensor_tensor(lo, w, hi, ALU.subtract).then_inc(parted, 1)
                    elif k % 2 == 0:
                        dve.wait_ge(turned, n + 1)
                        o = groups[gi][0] * P
                        if sh:
                            dve.tensor_scalar(hT[:, k, o:o + m * P], ps[:, n % 8, 0:m * P], sc(k), sh(k),
                                              ALU.mult, ALU.add).then_inc(out[0], 1)
                        else:
                            dve.tensor_scalar(hT[:, k, o:o + m * P], ps[:, n % 8, 0:m * P], sc(k), None,
                                              ALU.mult).then_inc(out[0], 1)
                    n += 1

        @block.tensor
        def _(pe):
            n = 0
            for first, m, _, _ in groups:
                pe.wait_ge(scaled, first - t0 + m)
                for k in range(kd):
                    if n >= 8:
                        pe.wait_ge(out[n % 2], (n - 8) // 2 + 1)
                    for j in range(m):
                        tr = pe.transpose(ps[:, n % 8, j * P:(j + 1) * P], xn[:, first - t0 + j, k * P:(k + 1) * P],
                                          env.ident[:])
                    tr.then_inc(turned, 1)
                    n += 1


def log1p_steps(dve, e, s, q, p):
    dve.tensor_scalar(p, e, 2.0, None, ALU.add)
    dve.drain()
    dve.reciprocal(q, p)
    dve.drain()
    dve.tensor_tensor(s, e, q, ALU.mult)
    dve.drain()
    dve.tensor_tensor(q, s, s, ALU.mult)
    dve.drain()
    dve.tensor_scalar(p, q, 1.0 / 15, None, ALU.mult)
    dve.drain()
    for odd in (13, 11, 9, 7, 5, 3):
        dve.scalar_tensor_tensor(p, p, 1.0 / odd, q, ALU.add, ALU.mult)
        dve.drain()
    dve.scalar_tensor_tensor(p, p, 1.0, s, ALU.add, ALU.mult)
    dve.drain()


def ssd_project(env, t, base):
    ps, ring, ins = env.ps, env.ring_, env.ins
    nz, nx = DI // HALF, (DI + 2 * G * NS) // HALF
    ft = nx * 4
    with Stage(env, base) as st:
        tm = st.sb("token_major", [P, 2, TOK])
        zb = st.sb("silu_z", [P, 2, HALF])
        pad = st.sb("padded", [P, 2, PADW])
        cv = st.sb("convolved", [P, 2, PADW - 4])
        sx = st.sb("x_features", [P, 2, TOK])
        raw = st.sb("dt_raw", [P, NT * 2 * H])
        e, s, q, p = (st.sb(f"softplus{i}", [P, NT * 2 * H]) for i in range(4))
        alog = st.sb("a_log", [P, 2 * H])
        out = st.sem("psum_copied")
        z_out = [st.sem("z_even_stored"), st.sem("z_odd_stored")]
        alog_in, pads, dt_neg, dt_exp, a_exp = (st.sem("alog_in"), st.sem("pads_zeroed"), st.sem("dt_negated"),
                                                st.sem("dt_exponent"), st.sem("a_exponent"))
        conv, silu, turned, filed = st.sem("convolved"), st.sem("activated"), st.sem("turned"), st.sem("filed")
        tm_out = [st.sem("even_token_tiles_stored"), st.sem("odd_token_tiles_stored")]
        fm_out = [st.sem("even_features_stored"), st.sem("odd_features_stored")]
        two = [slice(2 * b, 2 * b + 2) for b in range(4)]
        marked = lambda w: [(ks, slice(0, w), NT if b == 3 else 1) for b, ks in enumerate(two)]
        all_k = slice(0, KD)
        blocks, m0, b0 = ring.take_cut([marked(HALF)] * nz + [marked(2 * H)]
                                       + [[(all_k, slice(f * P, (f + 1) * P), 2) for f in range(4)]] * nx)
        first = blocks[0][0]
        views = {first + n: ring.view(first + n, KD, 2 * H if n == nz else HALF) for n in range(nz + 1 + nx)}
        closed = [(NT + 3) * (g // NT) + 3 + g % NT + 1 for g in range(NT * (nz + 1))]
        g0 = NT * (nz + 1)
        closed += [closed[-1] + n + 1 for n in range(2 * ft)]
        block = st.block()

        @block.sync
        def _(sp):
            sp.dma_start(alog[:], ins["ssd_A_log"].rearrange("a b c -> a (b c)").partition_broadcast(P)).then_inc(alog_in, 16)
            for n in range(nz):
                ring.load_to(sp, first + n + 1 + SLOTS)
                for i in range(NT):
                    g = n * NT + i
                    sp.wait_ge(out, g + 1)
                    sp.dma_start(env.z_dram[i, :, n * HALF:(n + 1) * HALF], zb[:, g % 2, :]).then_inc(z_out[g % 2], 16)
            for f in range(ft):
                if f % 4 == 0:
                    ring.load_to(sp, first + nz + 1 + f // 4 + SLOTS)
                if f >= 16:
                    sp.wait_ge(silu, f + 1)
                    dst = env.bt_dram if f < 24 else env.ct_dram
                    sp.dma_start(dst[:, f % 8, :], sx[:, f % 2, :]).then_inc(fm_out[f % 2], 16)
                if 1 <= f <= 24:
                    q_ = f - 1
                    sp.wait_ge(filed, f)
                    dst, a = (env.x_dram, q_ * P) if q_ < 16 else (env.b_dram, (q_ - 16) * P)
                    sp.dma_start(dst[:, :, a:a + P].rearrange("t p c -> p t c"),
                                 tm[:, q_ % 2, :].rearrange("p (t c) -> p t c", t=NT)).then_inc(tm_out[q_ % 2], 16)
            for par in range(2):
                sp.wait_ge(z_out[par], 16 * (nz * NT // 2))
                sp.wait_ge(tm_out[par], 16 * 12)
                sp.wait_ge(fm_out[par], 16 * 8)

        @block.tensor
        def _(pe):
            for n in range(nz + 1):
                wide = HALF if n < nz else 2 * H
                for b in range(4):
                    m = 4 * n + b
                    pe.wait_ge(ring.low_p, b0 + m + 1)
                    hi, lo = (ring.part(x, m, two[b], slice(0, wide)) for x in (ring.hi, ring.lo))
                    for i in range(NT):
                        g = n * NT + i
                        if g >= 8 and b == 0:
                            pe.wait_ge(out, g - 7)
                        t_ = slice(i * P, (i + 1) * P)
                        for q in range(2):
                            k = 2 * b + q
                            mm = products(pe, ps[:, g % 8, 0:wide], (t.hh[:, k, t_], t.hl[:, k, t_]),
                                          (hi[:, q, :], lo[:, q, :]), k == 0, k == KD - 1)
                        if b == 3 or i == NT - 1:
                            mm.then_inc(ring.done, 1)
            g = g0

            def turn(f):
                pe.wait_ge(silu, f + 1)
                if f >= 2:
                    pe.wait_ge(filed, f - 1)
                b = 4 + 2 * (f % 2)
                src = sx[:, f % 2, :]
                for i in range(NT):
                    tr = pe.transpose(ps[:, b + i // 4, (i % 4) * P:(i % 4 + 1) * P], src[:, i * P:(i + 1) * P], env.ident[:])
                tr.then_inc(turned, 1)

            pe.wait_ge(out, g0)
            for f in range(ft):
                m = 4 * (nz + 1) + f
                pe.wait_ge(ring.low_p, b0 + m + 1)
                hi, lo = (ring.part(x, m, all_k, slice(0, P)) for x in (ring.hi, ring.lo))
                for o, w_ in ((0, LAT), (LAT, CTX)):
                    if g >= g0 + 4:
                        pe.wait_ge(out, g - 3)
                    for k in range(KD):
                        mm = products(pe, ps[:, (g - g0) % 4, 0:w_], (hi[:, k, :], lo[:, k, :]),
                                      (t.hh[:, k, o:o + w_], t.hl[:, k, o:o + w_]), k == 0, k == KD - 1)
                    mm.then_inc(ring.done, 1)
                    g += 1
                if 1 <= f <= 24:
                    turn(f - 1)

        @block.gpsimd
        def _(pool):
            ring.cut(pool, blocks, views)

        @block.scalar
        def _(act):
            for n in range(nz):
                for i in range(NT):
                    g = n * NT + i
                    act.wait_ge(ring.done, m0 + closed[g])
                    if g >= 2:
                        act.wait_ge(z_out[g % 2], 16 * (g // 2))
                    act.activation(zb[:, g % 2, :], ps[:, g % 8, :], ACT.Silu).then_inc(out, 1)
            for i in range(NT):
                g = nz * NT + i
                act.wait_ge(ring.done, m0 + closed[g])
                act.activation(raw[:, i * 2 * H:(i + 1) * 2 * H], ps[:, g % 8, 0:2 * H], ACT.Copy).then_inc(out, 1)
            act.wait_ge(alog_in, 16)
            act.activation(alog[:], alog[:], ACT.Exp).then_inc(a_exp, 1)
            act.wait_ge(dt_neg, 1)
            act.activation(e[:], e[:], ACT.Exp).then_inc(dt_exp, 1)
            act.wait_ge(pads, 1)
            for f in range(ft):
                if f >= 2:
                    act.wait_ge(conv, f - 1)
                for j, (o, m, at) in enumerate(((0, LAT, PADL), (LAT, CTX, LATP + PADL))):
                    g = g0 + 2 * f + j
                    act.wait_ge(ring.done, m0 + closed[g])
                    act.activation(pad[:, f % 2, at:at + m], ps[:, (g - g0) % 4, 0:m], ACT.Copy).then_inc(out, 1)
                act.wait_ge(conv, f + 1)
                if 2 <= f < 26:
                    act.wait_ge(turned, f - 1)
                if f >= 18:
                    act.wait_ge(fm_out[f % 2], 16 * ((f - 16) // 2))
                dst = sx[:, f % 2, :]
                act.activation(dst[:, 0:LAT], cv[:, f % 2, 0:LAT], ACT.Silu)
                act.activation(dst[:, LAT:TOK], cv[:, f % 2, LATP:LATP + CTX], ACT.Silu)
                act.drain().then_inc(silu, 1)

        @block.vector
        def _(dve):
            dve.memset(pad[:], 0.0).then_inc(pads, 1)
            dve.wait_ge(out, g0)
            r3 = raw[:].rearrange("p (t h) -> p t h", t=NT)
            dve.tensor_tensor(r3, r3, env.dtb[:].unsqueeze(1).broadcast_to([P, NT, 2 * H]), ALU.add)
            dve.drain()
            dve.scalar_tensor_tensor(e[:], raw[:], -1.0, raw[:], ALU.mult, ALU.min).then_inc(dt_neg, 1)
            dve.tensor_scalar(raw[:], raw[:], 0.0, None, ALU.max)
            dve.wait_ge(dt_exp, 1)
            log1p_steps(dve, e[:], s[:], q[:], p[:])
            dt = t.dt[:].rearrange("p t h -> p (t h)")
            dve.scalar_tensor_tensor(dt, p[:], 2.0, raw[:], ALU.mult, ALU.add)
            dve.wait_ge(a_exp, 1)
            dve.tensor_scalar(alog[:], alog[:], -1.0, None, ALU.mult)
            dve.drain()
            dve.tensor_tensor(t.a[:], t.dt[:], alog[:].unsqueeze(1).broadcast_to([P, NT, 2 * H]), ALU.mult)

            def file(f):
                dve.wait_ge(turned, f + 1)
                b = 4 + 2 * (f % 2)
                if f >= 2:
                    dve.wait_ge(tm_out[f % 2], 16 * (f // 2))
                dve.tensor_copy(tm[:, f % 2, 0:HALF], ps[:, b, :])
                dve.tensor_copy(tm[:, f % 2, HALF:TOK], ps[:, b + 1, 0:2 * P])
                dve.drain().then_inc(filed, 1)

            n = PADW - 4
            for f in range(ft):
                dve.wait_ge(out, g0 + 2 * f + 2)
                if f >= 2:
                    dve.wait_ge(silu, f - 1)
                c = cv[:, f % 2, :]
                dve.tensor_scalar(c, pad[:, f % 2, 0:n], col(env, "ssd_conv_w", f), col(env, "ssd_conv_b", f),
                                  ALU.mult, ALU.add)
                for j in range(1, TAPS):
                    dve.drain()
                    last = dve.scalar_tensor_tensor(c, pad[:, f % 2, j:j + n], col(env, "ssd_conv_w", j * 32 + f), c,
                                                    ALU.mult, ALU.add)
                last.then_inc(conv, 1)
                if 1 <= f <= 24:
                    file(f - 1)


def ssd_scan(env, t, base):
    ps = env.ps
    W = HPG * HD
    W4 = HPG * P
    with Stage(env, base) as st:
        xdt = st.sb("x_dt", [P, 2, DI])
        bt = st.sb("b_features", [P, 2, G * P])
        ct = st.sb("c_features", [P, 2, G * P])
        bk = st.sb("b_tokens", [P, 2, G * NS])
        xde = st.sb("x_dt_decayed", [P, 2, DI])
        nacum = st.sb("neg_acum", [P, NT, 2 * H])
        ea = st.sb("exp_acum", [P, NT, 2 * H])
        de = st.sb("decay_to_end", [P, NT, 2 * H])
        dec = st.sb("chunk_decay", [P, NT, 2 * H])
        state = st.sb("state", [P, DI])
        ex = st.sb("segment_exp", [P, 2, W4])
        y1 = st.sb("y_off", [P, 2, W])
        y2 = st.sb("y_sum", [P, 2, W])
        sums, sums_e, sums_v = st.sem("sums"), st.sem("sums_exp"), st.sem("sums_neg")
        cb_s, bc_s, exp_s, mt_s = st.sem("cb"), st.sem("acum_spread"), st.sem("segments"), st.sem("weights_ready")
        diag_s, y2_s, yadd_s = st.sem("y_parts"), st.sem("y_summed"), st.sem("y_added")
        in_s = [st.sem("even_chunk_in"), st.sem("odd_chunk_in")]
        st_s, new_s, xd_s = st.sem("state_part"), st.sem("state_new"), st.sem("x_scaled")
        block = st.block()
        steps = []
        for d, order in ((0, (4, 5, 0, 1, 2, 3)), (1, (5, 4, 3, 2, 1, 0))):
            for i, c in enumerate(order):
                steps.append((d, i, c))

        @block.sync
        def _(sp):
            env.ring_.load_to(sp, len(env.ring_.ends) + SLOTS)
            v = lambda x, m: x[:, m % 2, :].rearrange("p (g c) -> p g c", g=G)
            for m, (d, i, c) in enumerate(steps):
                if m >= 2:
                    sp.wait_ge(st_s, (m - 1) * G)
                tok = slice(c * P, (c + 1) * P)
                sp.dma_start(xdt[:, m % 2, :], env.x_dram[c, :, :]).then_inc(in_s[m % 2], 16)
                sp.dma_start(v(bt, m), env.bt_dram[:, :, tok]).then_inc(in_s[m % 2], 16)
                sp.dma_start(v(ct, m), env.ct_dram[:, :, tok]).then_inc(in_s[m % 2], 16)
                sp.dma_start(bk[:, m % 2, :], env.b_dram[c, :, :]).then_inc(in_s[m % 2], 16)

        @block.tensor
        def _(pe):
            af = flat(t.a[:])
            for b, lhs in enumerate((env.tri[:, 0, :], env.tri[:, 1, :], env.tri[:, 2, :], env.tri[:, 3, :], env.ones[:])):
                mm = pe.matmul(ps[:, b, 0:NT * 2 * H], lhs, af, start=True, stop=True)
            mm.then_inc(sums, 1)
            pe.wait_ge(sums_e, 1)
            pe.wait_ge(sums_v, 1)

            def front(n, m, d, c, g):
                if g == 0:
                    pe.wait_ge(in_s[m % 2], 64 * (m // 2 + 1))
                gs = slice(g * P, (g + 1) * P)
                if n >= 2:
                    pe.wait_ge(mt_s, n - 1)
                pe.matmul(ps[:, n % 2, 0:P], bt[:, m % 2, gs], ct[:, m % 2, gs], start=True, stop=True).then_inc(cb_s, 1)
                if n >= 2:
                    pe.wait_ge(exp_s, n - 1)
                pe.matmul(ps[:, 2 + n % 2, :], env.ident_b[:], env.mask_b[:, d:d + 1, :].broadcast_to([P, HPG, P]),
                          start=True, stop=False, skip_group_check=True)
                for h in range(HPG):
                    hh = d * H + g * HPG + h
                    mm = pe.matmul(ps[:, 2 + n % 2, h * P:(h + 1) * P], t.a[:, c, hh:hh + 1].broadcast_to([P, P]),
                                   env.tri[:, d, :], start=False, stop=True, skip_group_check=True)
                mm.then_inc(bc_s, 1)

            def back(n, m, d, i, c, g):
                gs = slice(g * P, (g + 1) * P)
                if n >= 2:
                    pe.wait_ge(y2_s, n - 1)
                if i > 0:
                    if n >= G:
                        pe.wait_ge(new_s, n - G + 1)
                    pe.matmul(ps[:, 4 + n % 2, 0:W], ct[:, m % 2, gs], state[:, g * W:(g + 1) * W],
                              start=True, stop=True)
                pe.wait_ge(xd_s, m + 1)
                pe.wait_ge(mt_s, n + 1)
                for h in range(HPG):
                    mm = pe.matmul(ps[:, 4 + n % 2, W + h * HD:W + (h + 1) * HD], ex[:, n % 2, h * P:(h + 1) * P],
                                   xdt[:, m % 2, (g * HPG + h) * HD:(g * HPG + h + 1) * HD], start=True, stop=True)
                mm.then_inc(diag_s, 1)
                if n >= 2:
                    pe.wait_ge(new_s, n - 1)
                pe.matmul(ps[:, 6 + n % 2, 0:W], bk[:, m % 2, gs], xde[:, m % 2, g * W:(g + 1) * W],
                          start=True, stop=True).then_inc(st_s, 1)

            todo = [(m, d, i, c, g) for m, (d, i, c) in enumerate(steps) for g in range(G)]
            front(0, 0, todo[0][1], todo[0][3], 0)
            for n, (m, d, i, c, g) in enumerate(todo):
                if n + 1 < len(todo):
                    front(n + 1, todo[n + 1][0], todo[n + 1][1], todo[n + 1][3], todo[n + 1][4])
                back(n, m, d, i, c, g)

        @block.scalar
        def _(act):
            act.wait_ge(sums, 1)
            f = lambda x, d: x[:, :, d * H:(d + 1) * H]
            v = lambda b, d: ps[:, b, 0:NT * 2 * H].rearrange("p (t h) -> p t h", t=NT)[:, :, d * H:(d + 1) * H]
            for d in range(2):
                act.activation(f(ea, d), v(d, d), ACT.Exp)
                act.activation(f(de, d), v(2 + d, d), ACT.Exp)
                act.activation(f(dec, d), v(4, d), ACT.Exp)
            act.drain().then_inc(sums_e, 1)
            act.wait_ge(sums_v, 1)
            n = 0
            for d, i, c in steps:
                for g in range(G):
                    act.wait_ge(bc_s, n + 1)
                    if n >= 2:
                        act.wait_ge(diag_s, n - 1)
                    for h in range(HPG):
                        hh = d * H + g * HPG + h
                        last = act.activation(ex[:, n % 2, h * P:(h + 1) * P], ps[:, 2 + n % 2, h * P:(h + 1) * P], ACT.Exp,
                                              bias=nacum[:, c, hh:hh + 1])
                    last.then_inc(exp_s, 1)
                    n += 1

        @block.gpsimd
        def _(pool):
            pool.wait_ge(sums_e, 1)
            hv = lambda x: x.rearrange("p (h e) -> p h e", e=HD)

            def scale_x(m, g0, g1):
                d, i, c = steps[m]
                if g0 == 0:
                    pool.wait_ge(in_s[m % 2], 64 * (m // 2 + 1))
                w = slice(g0 * W, g1 * W)
                n_h = (g1 - g0) * HPG
                sp_ = lambda x: x[:, c, d * H + g0 * HPG:d * H + g1 * HPG].unsqueeze(2).broadcast_to([P, n_h, HD])
                pool.tensor_tensor(hv(xdt[:, m % 2, w]), hv(xdt[:, m % 2, w]), sp_(t.dt), ALU.mult)
                pool.drain()
                last = pool.tensor_tensor(hv(xde[:, m % 2, w]), hv(xdt[:, m % 2, w]), sp_(de), ALU.mult)
                if g1 == G:
                    last.then_inc(xd_s, 1)

            scale_x(0, 0, G)
            scale_x(1, 0, G)
            for m, (d, i, c) in enumerate(steps):
                for g in range(G):
                    n = m * G + g
                    if d == 1:
                        pool.wait_ge(y2_s, n + 1)
                        yv = t.y[:, c, g * W:(g + 1) * W]
                        pool.tensor_tensor(yv, yv, y2[:, n % 2, :], ALU.add).then_inc(yadd_s, 1)
                    if m >= 1 and m + 1 < len(steps) and 3 <= g < 7:
                        scale_x(m + 1, 2 * (g - 3), 2 * (g - 3) + 2)

        @block.vector
        def _(dve):
            dve.wait_ge(sums_e, 1)
            for d in range(2):
                v = ps[:, d, 0:NT * 2 * H].rearrange("p (t h) -> p t h", t=NT)[:, :, d * H:(d + 1) * H]
                dve.tensor_scalar(nacum[:, :, d * H:(d + 1) * H], v, -1.0, None, ALU.mult)
            dve.drain().then_inc(sums_v, 1)
            four = lambda x, e: x.rearrange("p (h e) -> p h e", e=e)

            def weights(n):
                dve.wait_ge(cb_s, n + 1)
                dve.wait_ge(exp_s, n + 1)
                dve.tensor_tensor(four(ex[:, n % 2, :], P), four(ex[:, n % 2, :], P),
                                  ps[:, n % 2, 0:P].unsqueeze(1).broadcast_to([P, HPG, P]), ALU.mult).then_inc(mt_s, 1)

            n = 0
            weights(0)
            for d, i, c in steps:
                for g in range(G):
                    hs = d * H + g * HPG
                    heads = lambda x: x[:, c, hs:hs + HPG].unsqueeze(2).broadcast_to([P, HPG, HD])
                    if n + 1 < len(steps) * G:
                        weights(n + 1)
                    if n >= G * NT + 2:
                        dve.wait_ge(yadd_s, n - G * NT - 1)
                    dst = t.y[:, c, g * W:(g + 1) * W] if d == 0 else y2[:, n % 2, :]
                    dve.wait_ge(diag_s, n + 1)
                    if i > 0:
                        dve.tensor_tensor(four(y1[:, n % 2, :], HD), four(ps[:, 4 + n % 2, 0:W], HD), heads(ea), ALU.mult)
                        dve.drain()
                        dve.tensor_tensor(dst, ps[:, 4 + n % 2, W:2 * W], y1[:, n % 2, :], ALU.add).then_inc(y2_s, 1)
                    else:
                        dve.tensor_copy(dst, ps[:, 4 + n % 2, W:2 * W]).then_inc(y2_s, 1)
                    dve.wait_ge(st_s, n + 1)
                    sv = state[:, g * W:(g + 1) * W]
                    if i > 0:
                        dve.tensor_tensor(four(sv, HD), four(sv, HD), heads(dec), ALU.mult)
                        dve.drain()
                        dve.tensor_tensor(sv, ps[:, 6 + n % 2, 0:W], sv, ALU.add).then_inc(new_s, 1)
                    else:
                        dve.tensor_copy(sv, ps[:, 6 + n % 2, 0:W]).then_inc(new_s, 1)
                    n += 1


def project_add(env, base, X, hT, kd, tiles, gate=None, norm=None, load=None):
    parts = isinstance(hT, tuple)
    ps, ring = env.ps, env.ring_
    nk = -(-kd // KD)
    n_t = len(tiles)
    with Stage(env, base) as st:
        rows = gate[1] if gate else [norm]
        spread = st.sb("row_weights", [P, len(rows), D])
        o = st.sb("product", [P, n_t, D])
        junk = st.sb("squares", [P, D])
        ss = st.sb("mean_square", [P, n_t])
        rows_in, copied, eps_in, rooted, squared = (st.sem("rows_in"), st.sem("products_out"), st.sem("eps_in"),
                                                    st.sem("rooted"), st.sem("squared"))
        x_in = st.sem("x_in")
        marks = []
        for n in range(2):
            marks += [1] * (nk - 1) + [n_t]
        if parts:
            sizes = [min(KD, kd - c * KD) for c in range(nk)]
            cuts, m0, b0 = ring.take_cut([[(slice(k, k + 2), slice(0, HALF), n_t if c == nk - 1 and k + 2 == ks else 1)
                                           for k in range(0, ks, 2)] for _ in range(2) for c, ks in enumerate(sizes)])
            views = {cuts[0][0] + n: ring.view(cuts[0][0] + n, sizes[n % nk], HALF) for n in range(2 * nk)}
            per = kd // 2 - 1 + n_t
        else:
            first, m0 = ring.take(marks)
            per = nk - 1 + n_t
        block = st.block()

        @block.gpsimd
        def _(pool):
            if parts:
                ring.cut_rest(pool, cuts, views)

        @block.sync
        def _(sp):
            for j, r in enumerate(rows):
                sp.dma_start(spread[:, j, :], r.partition_broadcast(P)).then_inc(rows_in, 16)
            for i, s in load or ():
                sp.dma_start(X[:, i, :], s).then_inc(x_in, 16)
            ring.load_to(sp, len(ring.ends) + SLOTS)

        @block.tensor
        def _(pe):
            for m, (_, ks, cols, _) in enumerate(cuts if parts else ()):
                n, q = m // (kd // 2), m % (kd // 2)
                pe.wait_ge(ring.low_p, b0 + m + 1)
                hi, lo = (ring.part(x, m, ks, cols) for x in (ring.hi, ring.lo))
                for j, i in enumerate(tiles):
                    if n == 1 and q == 0:
                        pe.wait_ge(copied, j + 1)
                    for k in (2 * q, 2 * q + 1):
                        mm = products(pe, ps[:, j, :], tuple(x[:, k, i * P:(i + 1) * P] for x in hT),
                                      (hi[:, k % 2, :], lo[:, k % 2, :]), k == 0, k == kd - 1)
                    if q == kd // 2 - 1 or j == n_t - 1:
                        mm.then_inc(ring.done, 1)
            for n in range(0 if parts else 2):
                for c in range(nk):
                    k_ = first + n * nk + c
                    ring.wait(pe, k_)
                    ks = min(KD, kd - c * KD)
                    w = ring.view(k_, ks, HALF)
                    for j, i in enumerate(tiles):
                        if n == 1 and c == 0:
                            pe.wait_ge(copied, j + 1)
                        for k in range(ks):
                            mm = pe.matmul(ps[:, j, :], hT[:, c * KD + k, i * P:(i + 1) * P], w[:, k, :],
                                           start=c == 0 and k == 0, stop=c == nk - 1 and k == ks - 1)
                        if c == nk - 1 or j == n_t - 1:
                            mm.then_inc(ring.done, 1)

        @block.scalar
        def _(act):
            m = 0
            for n in range(2):
                if parts:
                    for q in range(kd // 2 - 1):
                        m = ring.cut_after(act, cuts, views, m, m0 + n * per + q)
                    m = ring.cut_after(act, cuts, views, m, m0 + n * per + kd // 2 - 1)
                for j in range(n_t):
                    act.wait_ge(ring.done, m0 + n * per + per - n_t + j + 1)
                    act.activation(o[:, j, n * HALF:(n + 1) * HALF], ps[:, j, :], ACT.Copy).then_inc(copied, 1)
            if norm is not None:
                act.drain()
                for j in range(n_t):
                    act.drain()
                    act.activation(junk, o[:, j, :], ACT.Square, scale=float(D) ** -0.5,
                                   accum_out=ss[:, j:j + 1]).then_inc(squared, 1)
                act.wait_ge(eps_in, 1)
                act.activation(ss, ss, ACT.Sqrt).then_inc(rooted, 1)

        @block.vector
        def _(dve):
            dve.wait_ge(rows_in, 16 * len(rows))
            if load:
                dve.wait_ge(x_in, 16 * len(load))
            if gate:
                for n in range(2):
                    h = slice(n * HALF, (n + 1) * HALF)
                    for j, i in enumerate(tiles):
                        dve.wait_ge(copied, n * n_t + j + 1)
                        dve.tensor_tensor(o[:, j, h], o[:, j, h], spread[:, gate[0](i), h], ALU.mult)
                        dve.drain()
                        dve.tensor_tensor(X[:, i, h], X[:, i, h], o[:, j, h], ALU.add)
            else:
                dve.wait_ge(squared, n_t)
                dve.tensor_scalar(ss, ss, EPS, None, ALU.add).then_inc(eps_in, 1)
                dve.wait_ge(rooted, 1)
                dve.reciprocal(ss, ss)
                dve.drain()
                for j, i in enumerate(tiles):
                    dve.scalar_tensor_tensor(o[:, j, :], o[:, j, :], ss[:, j:j + 1], spread[:, 0, :], ALU.mult, ALU.mult)
                    dve.drain()
                    dve.tensor_tensor(X[:, i, :], X[:, i, :], o[:, j, :], ALU.add)


def route(env, base, layer, hT, nt, aff, pos, xn, xh, xl):
    ps = env.ps
    segs = [(0, LAT)] + ([(LAT, CTX)] if nt > NL else [])
    n_tok = nt * P
    with Stage(env, base) as st:
        rw = st.sb("router_w", [P, KD, E])
        lg = st.sb("logits", [P, nt, E])
        mx = st.sb("row_max", [P, nt])
        sm = st.sb("row_sum", [P, nt])
        aT = st.sb("aff_by_expert", [E, n_tok])
        work = st.sb("left_to_pick", [E, n_tok])
        work2 = st.sb("left_after_pick", [E, n_tok])
        place = st.sb("places", [E, n_tok])
        top = st.sb("top8", [E, 8])
        w_in, logit, shifted, exped, aff_s = (st.sem("router_in"), st.sem("logits_done"), st.sem("shifted"),
                                              st.sem("exp_done"), st.sem("aff_ready"))
        turned, picked, back = st.sem("aff_turned"), st.sem("places_ready"), st.sem("places_turned")
        xh_s = st.sem("high_parts")
        block = st.block()

        @block.sync
        def _(sp):
            sp.dma_start(rw, env.ins["moe_router_w"][layer].rearrange("(k p) e -> p k e", p=P)).then_inc(w_in, 16)
            env.ring_.load_to(sp, len(env.ring_.ends) + SLOTS)

        @block.tensor
        def _(pe):
            pe.wait_ge(w_in, 16)
            for i in range(nt):
                for k in range(KD):
                    mm = pe.matmul(ps[:, 0, i * E:(i + 1) * E], hT[:, k, i * P:(i + 1) * P], rw[:, k, :],
                                   start=k == 0, stop=k == KD - 1)
            mm.then_inc(logit, 1)
            pe.wait_ge(aff_s, 1)
            for i in range(nt):
                tr = pe.transpose(ps[0:E, 1 + i // 4, (i % 4) * P:(i % 4 + 1) * P], aff[:, i, :], env.ident[:])
            tr.then_inc(turned, 1)
            pe.wait_ge(picked, 1)
            for i in range(nt):
                tr = pe.transpose(ps[:, 3, i * E:(i + 1) * E], place[:, i * P:(i + 1) * P], env.ident[0:E, 0:E])
            tr.then_inc(back, 1)

        @block.scalar
        def _(act):
            act.wait_ge(shifted, 1)
            act.activation(lg, lg, ACT.Exp).then_inc(exped, 1)
            for i in range(nt):
                act.activation(xh[:, i, :], xn[:, i, :], ACT.Copy).then_inc(xh_s, 1)

        @block.gpsimd
        def _(pool):
            for i in range(nt):
                pool.wait_ge(xh_s, i + 1)
                pool.tensor_tensor(xl[:, i, :], xn[:, i, :], xh[:, i, :], ALU.subtract)

        @block.vector
        def _(dve):
            dve.wait_ge(logit, 1)
            lp = ps[:, 0, 0:nt * E].rearrange("p (i e) -> p i e", e=E)
            spread = lambda v: v.unsqueeze(2).broadcast_to([P, nt, E])
            dve.tensor_reduce(mx, lp, AX.X, ALU.max)
            dve.drain()
            dve.tensor_tensor(lg, lp, spread(mx), ALU.subtract).then_inc(shifted, 1)
            dve.wait_ge(exped, 1)
            dve.tensor_reduce(sm, lg, AX.X, ALU.add)
            dve.drain()
            dve.reciprocal(mx, sm)
            dve.drain()
            dve.tensor_tensor(aff, lg, spread(mx), ALU.mult).then_inc(aff_s, 1)
            dve.wait_ge(turned, 1)
            for j, (o, n) in enumerate(segs):
                dve.tensor_copy(aT[:, o:o + n], ps[0:E, 1 + j, 0:n])
            dve.drain()
            for o, n in segs:
                a, b = aT[:, o:o + n], work[:, o:o + n]
                c = work2[:, o:o + n]
                for r in range(2 * n // E // 8):
                    dve.max(top, a)
                    dve.drain()
                    dve.match_replace(b, top, a, -1.0)
                    dve.drain()
                    a, b, c = b, c, b
                left, count = a, b
                v, pl = aT[:, o:o + n], place[:, o:o + n]
                dve.tensor_tensor(v, left, v, ALU.is_lt)
                dve.drain()
                dve.tensor_tensor_scan(count, env.ones[0:E, 0:1].broadcast_to([E, n]), v, 0.0, ALU.mult, ALU.add)
                dve.drain()
                dve.scalar_tensor_tensor(pl, count, float(2 * o // E), v, ALU.add, ALU.mult)
            dve.drain().then_inc(picked, 1)
            dve.wait_ge(back, 1)
            dve.tensor_copy(pos, ps[:, 3, 0:nt * E].rearrange("p (i e) -> p i e", e=E))


def experts(env, base, layer, nt, xh, xl, aff, pos, acc):
    ps, ring, ins = env.ps, env.ring_, env.ins
    segs = [(0, 2 * LAT // E, 0)] + ([(2 * LAT // E, 2 * CTX // E, 1)] if nt > NL else [])
    S = sum(s[1] for s in segs)
    BL = 4 * S
    PER = 6
    NB = PER * BLOCKS
    PAIRS = E // 2
    with Stage(env, base) as st:
        oneh = st.sbr("one_hot", [P, nt * S])
        pT = st.sbr("one_hot_turned", [S, 2, nt * P])
        xgh, xgl = st.sbr("gathered_high", [P, KD * S]), st.sbr("gathered_low", [P, KD * S])
        hTh, hTl = st.sbr("hidden_turned_high", [P, KD * S]), st.sbr("hidden_turned_low", [P, KD * S])
        yh, yl = st.sbr("expert_rows_high", [S, D]), st.sbr("expert_rows_low", [S, D])
        rows_in = st.sb("gathered_rows", [P, D])
        xg = rows_in[:, 0:KD * S]
        rows_in = rows_in[0:S, :]
        h2 = st.sb("hidden", [S, D])
        gate = st.sb("slot_gates", [S, 2])
        built, gath, taken, gt_s, xg_s = (st.sem("one_hots_built"), st.sem("gather_summed"), st.sem("gathered_copied"),
                                          st.sem("gathered_turned"), st.sem("gathered_ready"))
        turned, pt_s = st.sem("one_hots_turned"), st.sem("turned_copied")
        sil, h2_s, t_s, th_s, tl_s = (st.sem("silu_done"), st.sem("hidden_done"),
                                              st.sem("hidden_turned"), st.sem("hidden_high"), st.sem("hidden_low"))
        yh_s, yl_s, sc_s, add_s = st.sem("rows_high"), st.sem("rows_low"), st.sem("scattered"), st.sem("rows_added")
        first, b0, v0, p0 = ring.take_split([BLOCKS] * (PER * E))
        oneh3 = oneh.rearrange("p (i s) -> p i s", i=nt)
        oneh_f = oneh.bitcast(F32).rearrange("p (i s) -> p i s", i=nt)
        block = st.block()
        names = ("moe_w1", "moe_w1", "moe_w3", "moe_w3", "moe_w2", "moe_w2")

        def source(i, n):
            c = n % PER
            w = ins[names[c]][layer, n // PER:]
            h = slice((c % 2) * HALF, (c % 2 + 1) * HALF)
            return w[bass.ds(i * 2, 1), :, h].rearrange("o (k p) n -> p (o k) n", p=P)

        @block.sync
        def _(sp):
            ring.load_to(sp, first + SLOTS)
            ring.loaded = first + PER * E
            ring.load_to(sp, first + PER * E + SLOTS)

        def each_pair(eng, body):
            body(0, True, False)
            with eng.Fori(1, PAIRS - 1) as i:
                body(i, False, False)
            body(PAIRS - 1, False, True)

        @block.tensor
        def _(pe):
            def gather(e, waits):
                pe.wait_ge(built, e + 1)
                for h in range(2):
                    for t in range(nt):
                        for n, x in enumerate((xh, xl)):
                            if h == 1 and t == nt - 1 and n == 1:
                                for w in waits:
                                    pe.wait_ge(*w)
                            mm = pe.matmul(ps[0:S, 4 + h, :], oneh3[:, t, :], x[:, t, h * HALF:(h + 1) * HALF],
                                           start=t == 0 and n == 0, stop=t == nt - 1 and n == 1)
                mm.then_inc(gath, 1)

            def turn_hidden():
                for b in range(2):
                    for k in range(4 * b, 4 * b + 4):
                        tr = pe.transpose(ps[:, 2 + b, (k % 4) * S:(k % 4 + 1) * S], h2[:, k * P:(k + 1) * P],
                                          env.ident[0:S, 0:S])
                    tr.then_inc(t_s, 1)

            def turn_gathered(e):
                for t in range(nt):
                    pe.transpose(ps[0:S, 6 + t // 4, (t % 4) * P:(t % 4 + 1) * P], oneh_f[:, t, :], env.ident[:])
                pe.wait_ge(taken, 2 * e + 2)
                for t in range(nt):
                    mm = pe.matmul(ps[0:S, 7, 2 * P:2 * P + 1], oneh_f[:, t, :], aff[:, t, bass.ds(e, 1)], start=t == 0, stop=t == nt - 1)
                mm.then_inc(turned, 1)
                for k in range(KD):
                    tr = pe.transpose(ps[:, 4 + k // 4, (k % 4) * S:(k % 4 + 1) * S], rows_in[:, k * P:(k + 1) * P],
                                      env.ident[0:S, 0:S])
                tr.then_inc(gt_s, 1)

            def scatter(e, j, t):
                for h in range(2):
                    for n, y in enumerate((yh, yl)):
                        mm = pe.matmul(ps[:, 4 + 2 * (t % 2) + h, :], pT[:, j, t * P:(t + 1) * P],
                                       y[:, h * HALF:(h + 1) * HALF], start=n == 0, stop=n == 1)
                mm.then_inc(sc_s, 1)

            def product(i, j, c, high, low, bank):
                for b in range(BLOCKS):
                    m = NB * j + BLOCKS * c + b
                    if b == 3:
                        pe.wait_ge(ring.low_p, i * 12 + (p0 + m // BLOCKS + 1))
                    else:
                        pe.wait_ge(ring.low_v, i * 36 + (v0 + 3 * (m // BLOCKS) + b + 1))
                    s = (b0 + m) % CUTS
                    for q in range(2):
                        k = 2 * b + q
                        w = slice(q * HALF, (q + 1) * HALF)
                        for n, (x, y) in enumerate(((high, ring.hi), (low, ring.hi), (high, ring.lo))):
                            mm = pe.matmul(ps[0:S, bank, :], x[:, k * S:(k + 1) * S], y[:, s, w],
                                           start=k == 0 and n == 0, stop=k == KD - 1 and n == 2)
                    mm.then_inc(ring.used, 1)

            def body(i, begin, end):
                for j in range(2):
                    e = i * 2 + j
                    start, stop = begin and j == 0, end and j == 1
                    a, l = xgh, xgl
                    pe.wait_ge(xg_s, e + 1)
                    if not start:
                        pe.wait_ge(yl_s, 2 * e - 1)
                    product(i, j, 0, a, l, 0)
                    if not start:
                        pe.wait_ge(yl_s, 2 * e)
                    product(i, j, 1, a, l, 1)
                    if not start:
                        pe.wait_ge(pt_s, e + 1)
                        scatter(e - 1, 1 - j, 0)
                        scatter(e - 1, 1 - j, 1)
                        pe.wait_ge(tl_s, 2 * e)
                    product(i, j, 2, a, l, 2)
                    if not start:
                        for t in (2, 3):
                            pe.wait_ge(add_s, (e - 1) * nt + t - 1)
                            scatter(e - 1, 1 - j, t)
                    product(i, j, 3, a, l, 3)
                    if not start:
                        for t in range(4, nt):
                            pe.wait_ge(add_s, (e - 1) * nt + t - 1)
                            scatter(e - 1, 1 - j, t)
                    if stop:
                        pe.wait_ge(h2_s, 2 * e + 2)
                        turn_hidden()
                    else:
                        if not start:
                            pe.wait_ge(add_s, e * nt - 1)
                        gather(e + 1, [(h2_s, 2 * e + 2)] + ([] if start else [(add_s, e * nt)]))
                        turn_hidden()
                        turn_gathered(e + 1)
                    pe.wait_ge(tl_s, 2 * e + 2)
                    product(i, j, 4, hTh, hTl, 0)
                    product(i, j, 5, hTh, hTl, 1)

            gather(0, [])
            turn_gathered(0)
            each_pair(pe, body)
            pe.wait_ge(yl_s, 2 * E)
            for t in range(nt):
                if t >= 2:
                    pe.wait_ge(add_s, (E - 1) * nt + t - 1)
                scatter(E - 1, 1, t)

        def part_source(m):
            w = ring.slots[:, (first + m // BLOCKS) % SLOTS, :]
            return w[:, (m % BLOCKS) * CUT:(m % BLOCKS + 1) * CUT]

        @block.scalar
        def _(act):
            def high(i, end, a, b):
                for m in range(a, b):
                    if m % BLOCKS == 0:
                        n = first + m // BLOCKS
                        act.wait_ge(ring.landed[n % SLOTS], i * 16 * (12 // SLOTS) + 16 * (n // SLOTS + 1))
                    if a > 0:
                        act.wait_ge(ring.used, i * 2 * NB + b0 + m - CUTS + 1)
                    act.activation(ring.hi[:, (b0 + m) % CUTS, :], part_source(m), ACT.Copy).then_inc(ring.high, 1)
                    n = m // BLOCKS - 1 + SLOTS
                    if m % BLOCKS == 3 and n >= SLOTS and not (end and n >= 2 * PER):
                        act.dma_start(ring.view(first + n, KD, HALF), source(i, n)).then_inc(ring.landed[(first + n) % SLOTS], 16)

            def copy_gathered(e):
                act.wait_ge(gath, e + 1)
                for b in range(2):
                    act.activation(rows_in[:, b * HALF:(b + 1) * HALF], ps[0:S, 4 + b, :], ACT.Copy).then_inc(taken, 1)

            def copy_turned(e, j):
                act.wait_ge(turned, e + 1)
                act.activation(gate[:, j:j + 1], ps[0:S, 7, 2 * P:2 * P + 1], ACT.Copy)
                for b in range(-(-nt // 4)):
                    w = min(4, nt - 4 * b) * P
                    act.activation(pT[:, j, b * HALF:b * HALF + w], ps[0:S, 6 + b, 0:w], ACT.Copy)
                act.drain().then_inc(pt_s, 1)

            def silu(i, e, j, b):
                act.wait_ge(ring.used, i * 2 * NB + b0 + NB * j + BLOCKS * (b + 1))
                act.activation(h2[:, b * HALF:(b + 1) * HALF], ps[0:S, b, :], ACT.Silu).then_inc(sil, 1)

            def rows(i, e, j, b):
                act.wait_ge(ring.used, i * 2 * NB + b0 + NB * j + BLOCKS * (5 + b))
                act.activation(yh[:, b * HALF:(b + 1) * HALF], ps[0:S, b, :], ACT.Copy, scale=gate[:, j:j + 1]).then_inc(yh_s, 1)

            def body(i, begin, end):
                for j in range(2):
                    e = i * 2 + j
                    o = NB * j
                    start, stop = begin and j == 0, end and j == 1
                    if not start:
                        act.wait_ge(t_s, 2 * e)
                    high(i, end, o + CUTS, o + CUTS + 4)
                    silu(i, e, j, 0)
                    high(i, end, o + CUTS + 4, o + CUTS + 8)
                    silu(i, e, j, 1)
                    high(i, end, o + CUTS + 8, o + CUTS + 16)
                    if not stop:
                        copy_gathered(e + 1)
                    for b in range(2):
                        act.wait_ge(t_s, 2 * e + b + 1)
                        act.activation(hTh[:, b * BL:(b + 1) * BL], ps[:, 2 + b, 0:BL], ACT.Copy).then_inc(th_s, 1)
                    if not stop:
                        copy_turned(e + 1, 1 - j)
                    high(i, end, o + CUTS + 16, o + CUTS + 20)
                    rows(i, e, j, 0)
                    high(i, end, o + CUTS + 20, o + NB + (0 if stop else CUTS))
                    rows(i, e, j, 1)

            high(0, False, 0, CUTS)
            copy_gathered(0)
            copy_turned(0, 0)
            each_pair(act, body)

        @block.gpsimd
        def _(pool):
            def body(i, begin, end):
                for m in range(3, 2 * NB, BLOCKS):
                    pool.wait_ge(ring.high, i * 2 * NB + (b0 + m + 1))
                    s = (b0 + m) % CUTS
                    pool.tensor_tensor(ring.lo[:, s, :], part_source(m), ring.hi[:, s, :], ALU.subtract).then_inc(ring.low_p, 1)

            each_pair(pool, body)

        @block.vector
        def _(dve):
            def low(i, a, b):
                for m in range(a, b):
                    if m % BLOCKS == 3:
                        continue
                    dve.wait_ge(ring.high, i * 2 * NB + (b0 + m + 1))
                    s = (b0 + m) % CUTS
                    dve.tensor_tensor(ring.lo[:, s, :], part_source(m), ring.hi[:, s, :], ALU.subtract).then_inc(ring.low_v, 1)

            def build(e):
                shape = [P, nt, S]
                dve.tensor_tensor(oneh3, env.iota[:, 0:S].unsqueeze(1).broadcast_to(shape),
                                  pos[:, :, bass.ds(e, 1)].broadcast_to(shape), ALU.is_equal).then_inc(built, 1)

            def modulate(e):
                dve.wait_ge(gt_s, e + 1)
                for b in range(2):
                    g = ps[:, 4 + b, 0:BL].rearrange("p (k s) -> p k s", k=4)
                    o = xg[:, b * BL:(b + 1) * BL].rearrange("p (k s) -> p k s", k=4)
                    for s0, m, u in segs:
                        c = lambda q: env.modc[:, q, u, 4 * b:4 * b + 4].unsqueeze(2).broadcast_to([P, 4, m])
                        dve.tensor_tensor(o[:, :, s0:s0 + m], g[:, :, s0:s0 + m], c(3), ALU.mult)
                dve.drain()
                for b in range(2):
                    o = xg[:, b * BL:(b + 1) * BL].rearrange("p (k s) -> p k s", k=4)
                    for s0, m, u in segs:
                        c = lambda q: env.modc[:, q, u, 4 * b:4 * b + 4].unsqueeze(2).broadcast_to([P, 4, m])
                        dve.tensor_tensor(o[:, :, s0:s0 + m], o[:, :, s0:s0 + m], c(2), ALU.add)
                dve.drain()
                dve.tensor_copy(xgh, xg)
                dve.drain()
                dve.tensor_tensor(xgl, xg, xgh, ALU.subtract)
                dve.drain().then_inc(xg_s, 1)

            def add(e, t):
                dve.wait_ge(sc_s, e * nt + t + 1)
                b = 4 + 2 * (t % 2)
                dve.tensor_tensor(acc[:, t, :], acc[:, t, :], ps[:, b:b + 2, :].rearrange("p a b -> p (a b)"),
                                  ALU.add).then_inc(add_s, 1)

            def hidden(i, e, j, b):
                dve.wait_ge(ring.used, i * 2 * NB + b0 + NB * j + BLOCKS * (3 + b))
                dve.wait_ge(sil, 2 * e + b + 1)
                s = slice(b * HALF, (b + 1) * HALF)
                dve.tensor_tensor(h2[:, s], h2[:, s], ps[0:S, 2 + b, :], ALU.mult).then_inc(h2_s, 1)

            def rows(e, j, b):
                dve.wait_ge(yh_s, 2 * e + b + 1)
                s = slice(b * HALF, (b + 1) * HALF)
                dve.scalar_tensor_tensor(yl[:, s], ps[0:S, b, :], gate[:, j:j + 1], yh[:, s], ALU.mult,
                                         ALU.subtract).then_inc(yl_s, 1)

            def body(i, begin, end):
                for j in range(2):
                    e = i * 2 + j
                    o = NB * j
                    start, stop = begin and j == 0, end and j == 1
                    if not stop:
                        dve.wait_ge(turned, e + 1)
                        build(e + 1)
                    low(i, o + CUTS, o + CUTS + 8)
                    if not start:
                        add(e - 1, 0)
                        add(e - 1, 1)
                    low(i, o + CUTS + 8, o + CUTS + 12)
                    hidden(i, e, j, 0)
                    if not start:
                        add(e - 1, 2)
                        add(e - 1, 3)
                    low(i, o + CUTS + 12, o + CUTS + 16)
                    hidden(i, e, j, 1)
                    if not start:
                        for t in range(4, nt):
                            add(e - 1, t)
                    for b in range(2):
                        dve.wait_ge(th_s, 2 * e + b + 1)
                        dve.tensor_tensor(hTl[:, b * BL:(b + 1) * BL], ps[:, 2 + b, 0:BL], hTh[:, b * BL:(b + 1) * BL],
                                          ALU.subtract).then_inc(tl_s, 1)
                    if not stop:
                        modulate(e + 1)
                    low(i, o + CUTS + 16, o + CUTS + 20)
                    rows(e, j, 0)
                    low(i, o + CUTS + 20, o + NB + (0 if stop else CUTS))
                    rows(e, j, 1)

            build(0)
            dve.memset(acc, 0.0)
            low(0, 0, CUTS)
            modulate(0)
            each_pair(dve, body)
            for t in range(nt):
                add(E - 1, t)


def gate_add(env, base, layer, X, acc, nt):
    rows = [env.mod_dram[layer, u, 5 * D:6 * D] for u in range(2 if nt > NL else 1)]
    with Stage(env, base) as st:
        spread = st.sb("gate_rows", [P, len(rows), D])
        g_in = st.sem("gate_in")
        block = st.block()

        @block.sync
        def _(sp):
            for j, r in enumerate(rows):
                sp.dma_start(spread[:, j, :], r.partition_broadcast(P)).then_inc(g_in, 16)

        @block.vector
        def _(dve):
            dve.wait_ge(g_in, 16 * len(rows))
            for t in range(nt):
                dve.tensor_tensor(acc[:, t, :], acc[:, t, :], spread[:, int(t >= NL), :], ALU.mult)
            dve.drain()
            for t in range(nt):
                dve.tensor_tensor(X[:, t, :], X[:, t, :], acc[:, t, :], ALU.add)


def moe(env, layer, X, nt):
    mc = lambda q, u: (lambda k: env.modc[:, q, u, k:k + 1])
    xn = acc = carve(env, X_END, [P, nt, D])
    top = X_END + nt * D
    aff, pos = carve(env, top, [P, nt, E]), carve(env, top + nt * E, [P, nt, E])
    top += 2 * nt * E
    xh, xl = carve_r(env, "tokens_high", top, [P, nt, D]), carve_r(env, "tokens_low", top + nt * D, [P, nt, D])
    top += 2 * nt * D
    hT = carve(env, top, [P, KD, nt * P])
    groups = [(0, NL, mc(3, 0), mc(2, 0))] + ([(NL, NC, mc(3, 1), mc(2, 1))] if nt > NL else [])
    norm_turn(env, top + nt * D, X, hT, groups, token_out=xn)
    route(env, top + nt * D, layer, hT, nt, aff, pos, xn, xh, xl)
    experts(env, top, layer, nt, xh, xl, aff, pos, acc)
    gate_add(env, top, layer, X, acc, nt)


def project(env, base, jobs):
    ps, ring = env.ps, env.ring_
    with Stage(env, base) as st:
        left = st.sem("sums_copied")
        closes = lambda kd, ks: ks.stop == kd
        cuts, m0, b0 = ring.take_cut([[(ks, cols, len(groups) if closes(kd, ks) else 1) for ks, cols, groups in blocks]
                                      for kd, _, blocks in jobs])
        views = {cuts[0][0] + c: ring.view(cuts[0][0] + c, kd, width) for c, (kd, width, _) in enumerate(jobs)}
        block = st.block()

        @block.sync
        def _(sp):
            ring.load_to(sp, len(ring.ends) + SLOTS)

        @block.gpsimd
        def _(pool):
            ring.cut_rest(pool, cuts, views)

        @block.tensor
        def _(pe):
            g = m = 0
            for kd, _, blocks in jobs:
                for ks, cols, groups in blocks:
                    pe.wait_ge(ring.low_p, b0 + m + 1)
                    hi, lo = (ring.part(x, m, ks, cols) for x in (ring.hi, ring.lo))
                    for j, (operands, rows, n, _) in enumerate(groups):
                        if ks.start == 0 and g + j >= 8:
                            pe.wait_ge(left, g + j - 7)
                        for k in range(ks.start, ks.stop):
                            q = k - ks.start
                            x, y = operands(k, (hi[:, q, :], lo[:, q, :]))
                            mm = products(pe, ps[0:rows, (g + j) % 8, 0:n], x, y, k == 0, k == kd - 1)
                        if closes(kd, ks) or j == len(groups) - 1:
                            mm.then_inc(ring.done, 1)
                    if closes(kd, ks):
                        g += len(groups)
                    m += 1

        @block.scalar
        def _(act):
            g, marks = 0, m0
            m = ring.cut_after(act, cuts, views, 0, m0)
            for kd, _, blocks in jobs:
                for ks, _, groups in blocks:
                    if not closes(kd, ks):
                        marks += 1
                        m = ring.cut_after(act, cuts, views, m, marks)
                        continue
                    for _, rows, n, copies in groups:
                        marks += 1
                        act.wait_ge(ring.done, marks)
                        copies(act, ps[0:rows, g % 8, 0:n]).then_inc(left, 1)
                        g += 1
                    m = ring.cut_after(act, cuts, views, m, marks)


ALL_K = slice(0, KD)


def features(h, cols, tok, copies):
    return ALL_K, cols, [(lambda k, w: (w, tuple(x[:, k, tok] for x in h)), cols.stop - cols.start, tok.stop - tok.start, copies)]


def tokens(h, cols, tiles):
    groups = [((lambda k, w, t=t: (tuple(x[:, k, t * P:(t + 1) * P] for x in h), w)), P, cols.stop - cols.start, copies)
              for t, copies in tiles]
    step = min(KD, CUT // (cols.stop - cols.start))
    return [(slice(k, k + step), cols, groups) for k in range(0, KD, step)]


def tile(f):
    return slice(f * P, (f + 1) * P)


def copy_to(dst, func=ACT.Copy):
    return lambda act, s: act.activation(dst, s, func)


def turn(env, base, src, hT, nt, kd):
    ps = env.ps
    with Stage(env, base) as st:
        turned, left = st.sem("turned"), st.sem("copied")
        block = st.block()

        @block.tensor
        def _(pe):
            for k in range(kd):
                if k >= 8:
                    pe.wait_ge(left, k - 7)
                for t in range(nt):
                    tr = pe.transpose(ps[:, k % 8, t * P:(t + 1) * P], src[:, t, k * P:(k + 1) * P], env.ident[:])
                tr.then_inc(turned, 1)

        @block.vector
        def _(dve):
            for k in range(kd):
                dve.wait_ge(turned, k + 1)
                dve.tensor_copy(hT[:, k, :], ps[:, k % 8, 0:nt * P]).then_inc(left, 1)

        @block.sync
        def _(sp):
            env.ring_.load_to(sp, len(env.ring_.ends) + SLOTS)


def attend(env, base, steps, scale, width):
    ps = env.ps
    most = max(s[2] for s in steps)
    masked = any(s[3] is not None for s in steps)
    with Stage(env, base) as st:
        prob = st.sb("probabilities", [P, 2, most])
        pT = st.sb("probabilities_turned", [P, 2, most])
        sm = st.sb("masked_scores", [P, 2, most]) if masked else None
        stat = st.sb("row_stats", [P, 4, 4])
        score, shift, prob_s, turned = st.sem("scores"), st.sem("shift_ready"), st.sem("probabilities"), st.sem("turned")
        pT_a, pT_v, outs, left = (st.sem("turned_copied_by_act"), st.sem("turned_copied_by_dve"), st.sem("outputs"),
                                  st.sem("outputs_left"))
        block = st.block()

        @block.sync
        def _(sp):
            env.ring_.load_to(sp, len(env.ring_.ends) + SLOTS)

        @block.tensor
        def _(pe):
            def scores(n):
                q, k, keys = steps[n][:3]
                if n >= 2:
                    pe.wait_ge(prob_s, n - 1)
                    pe.wait_ge(shift, n - 1)
                for a in range(0, keys, HALF):
                    b = min(a + HALF, keys)
                    mm = pe.matmul(ps[:, 2 * (n % 2) + a // HALF, 0:b - a], q, k[:, a:b], start=True, stop=True)
                mm.then_inc(score, 1)

            def turn_probabilities(n):
                pe.wait_ge(prob_s, n + 1)
                if n >= 1:
                    pe.wait_ge(pT_a, n)
                    pe.wait_ge(pT_v, n)
                for t in range(steps[n][2] // P):
                    tr = pe.transpose(ps[:, 4 + t // 4, (t % 4) * P:(t % 4 + 1) * P], prob[:, n % 2, t * P:(t + 1) * P], env.ident[:])
                tr.then_inc(turned, 1)

            def output(n):
                keys, values = steps[n][2], steps[n][4]
                kt = keys // P
                if n >= 2:
                    pe.wait_ge(left, n - 1)
                pe.wait_ge(pT_a, n + 1)
                pe.wait_ge(pT_v, n + 1)
                for t in range(kt):
                    mm = pe.matmul(ps[:, 6 + n % 2, 0:width], pT[:, n % 2, t * P:(t + 1) * P], values[t], start=t == 0, stop=t == kt - 1)
                mm.then_inc(outs, 1)

            scores(0)
            scores(1)
            for n in range(len(steps)):
                turn_probabilities(n)
                if n + 2 < len(steps):
                    scores(n + 2)
                output(n)

        @block.scalar
        def _(act):
            def copy_turned(n):
                act.wait_ge(turned, n + 1)
                w = min(steps[n][2], HALF)
                act.activation(pT[:, n % 2, 0:w], ps[:, 4, 0:w], ACT.Copy).then_inc(pT_a, 1)

            for n, (_, _, keys, mask, _, _) in enumerate(steps):
                act.wait_ge(shift, n + 1)
                if n >= 2:
                    act.wait_ge(turned, n - 1)
                if n >= 4:
                    act.wait_ge(left, n - 3)
                src = sm[:, n % 2, 0:keys] if mask is not None else ps[:, 2 * (n % 2):2 * (n % 2) + 2, :].rearrange("p a b -> p (a b)")[:, 0:keys]
                act.activation(prob[:, n % 2, 0:keys], src, ACT.Exp, scale=scale, bias=stat[:, n % 4, 1:2],
                               accum_out=stat[:, n % 4, 2:3])
                act.drain().then_inc(prob_s, 1)
                if n >= 1:
                    copy_turned(n - 1)
            copy_turned(len(steps) - 1)

        @block.vector
        def _(dve):
            def copy_turned(n):
                keys = steps[n][2]
                dve.wait_ge(turned, n + 1)
                if keys > HALF:
                    dve.tensor_copy(pT[:, n % 2, HALF:keys], ps[:, 5, 0:keys - HALF]).then_inc(pT_v, 1)
                else:
                    dve.drain().then_inc(pT_v, 1)

            def finish(n):
                dve.reciprocal(stat[:, n % 4, 3:4], stat[:, n % 4, 2:3])
                dve.drain()
                dve.wait_ge(outs, n + 1)
                dve.tensor_scalar(steps[n][5], ps[:, 6 + n % 2, 0:width], stat[:, n % 4, 3:4], None, ALU.mult).then_inc(left, 1)

            for n, (_, _, keys, mask, _, _) in enumerate(steps):
                dve.wait_ge(score, n + 1)
                s = ps[:, 2 * (n % 2):2 * (n % 2) + 2, :].rearrange("p a b -> p (a b)")[:, 0:keys]
                if n >= 2:
                    dve.wait_ge(prob_s, n - 1)
                if mask is not None:
                    dve.tensor_tensor(sm[:, n % 2, 0:keys], s, mask, ALU.add)
                    dve.drain()
                    s = sm[:, n % 2, 0:keys]
                dve.tensor_reduce(stat[:, n % 4, 0:1], s, AX.X, ALU.max)
                dve.drain()
                dve.tensor_scalar(stat[:, n % 4, 1:2], stat[:, n % 4, 0:1], -scale, None, ALU.mult).then_inc(shift, 1)
                if n >= 1:
                    copy_turned(n - 1)
                if n >= 2:
                    finish(n - 2)
            copy_turned(len(steps) - 1)
            finish(len(steps) - 2)
            finish(len(steps) - 1)


def attend_heads(env, base, heads, keys, scale, width):
    ps = env.ps
    kt, n_steps = keys // P, NL * len(heads)
    with Stage(env, base) as st:
        prob = st.sb("probabilities", [P, 2, keys])
        pT = st.sb("probabilities_turned", [P, 2, kt * LAT])
        stat = st.sb("row_stats", [P, 4, 4])
        score, shift, exped, prob_s = st.sem("scores"), st.sem("shift_ready"), st.sem("exponentials"), st.sem("probabilities")
        turned, pT_a, pT_v = st.sem("turned"), st.sem("turned_copied_by_act"), st.sem("turned_copied_by_dve")
        outs, high, left = st.sem("outputs"), st.sem("outputs_high"), st.sem("outputs_left")
        block = st.block()
        first_kt = min(kt, 4)

        def turned_place(n, a, b):
            v = pT[:, (n // NL) % 2, :].rearrange("p (k q) -> p k q", k=kt)
            return v[:, a:b, (n % NL) * P:(n % NL + 1) * P]

        @block.sync
        def _(sp):
            env.ring_.load_to(sp, len(env.ring_.ends) + SLOTS)

        @block.tensor
        def _(pe):
            def scores(n):
                q, k = heads[n // NL][:2]
                if n >= 2:
                    pe.wait_ge(exped, n - 1)
                    pe.wait_ge(shift, n - 1)
                for a in range(0, keys, HALF):
                    b = min(a + HALF, keys)
                    mm = pe.matmul(ps[:, 2 * (n % 2) + a // HALF, 0:b - a], q[:, (n % NL) * P:(n % NL + 1) * P], k[:, a:b],
                                   start=True, stop=True)
                mm.then_inc(score, 1)

            def turn_probabilities(n):
                pe.wait_ge(prob_s, n + 1)
                if n >= 1:
                    pe.wait_ge(pT_a, n)
                    if kt > 4:
                        pe.wait_ge(pT_v, n)
                for t in range(kt):
                    tr = pe.transpose(ps[:, 4 + t // 4, (t % 4) * P:(t % 4 + 1) * P], prob[:, n % 2, t * P:(t + 1) * P], env.ident[:])
                tr.then_inc(turned, 1)

            def output(h):
                if h >= 2:
                    pe.wait_ge(left, h - 1)
                pe.wait_ge(pT_a, NL * (h + 1))
                if kt > 4:
                    pe.wait_ge(pT_v, NL * (h + 1))
                for t in range(kt):
                    mm = pe.matmul(ps[0:width, 6 + h % 2, :], heads[h][2][t], pT[:, h % 2, t * LAT:(t + 1) * LAT],
                                   start=t == 0, stop=t == kt - 1)
                mm.then_inc(outs, 1)

            scores(0)
            scores(1)
            for n in range(n_steps):
                turn_probabilities(n)
                if n + 2 < n_steps:
                    scores(n + 2)
                if n % NL == 0 and n > 0:
                    output(n // NL - 1)
            output(len(heads) - 1)

        @block.scalar
        def _(act):
            def copy_turned(n):
                act.wait_ge(turned, n + 1)
                act.activation(turned_place(n, 0, first_kt),
                               ps[:, 4, 0:first_kt * P].rearrange("p (k q) -> p k q", k=first_kt), ACT.Copy).then_inc(pT_a, 1)

            def leave(h):
                act.wait_ge(outs, h + 1)
                act.activation(heads[h][3][0], ps[0:width, 6 + h % 2, :], ACT.Copy).then_inc(high, 1)

            for n in range(n_steps):
                act.wait_ge(shift, n + 1)
                if n >= 2:
                    act.wait_ge(turned, n - 1)
                src = ps[:, 2 * (n % 2):2 * (n % 2) + 2, :].rearrange("p a b -> p (a b)")[:, 0:keys]
                act.activation(prob[:, n % 2, :], src, ACT.Exp, scale=scale, bias=stat[:, n % 4, 1:2], accum_out=stat[:, n % 4, 2:3])
                act.drain().then_inc(exped, 1)
                if n >= 1:
                    copy_turned(n - 1)
                if n >= NL + 2 and (n - 1) % NL == 1:
                    leave((n - 1) // NL - 1)
            copy_turned(n_steps - 1)
            leave(len(heads) - 1)

        @block.vector
        def _(dve):
            def normalise(n):
                dve.wait_ge(exped, n + 1)
                dve.reciprocal(stat[:, n % 4, 3:4], stat[:, n % 4, 2:3])
                dve.drain()
                dve.tensor_scalar(prob[:, n % 2, :], prob[:, n % 2, :], stat[:, n % 4, 3:4], None, ALU.mult).then_inc(prob_s, 1)

            def copy_turned(n):
                if kt > 4:
                    dve.wait_ge(turned, n + 1)
                    dve.tensor_copy(turned_place(n, 4, kt),
                                    ps[:, 5, 0:(kt - 4) * P].rearrange("p (k q) -> p k q", k=kt - 4)).then_inc(pT_v, 1)

            def leave(h):
                dve.wait_ge(high, h + 1)
                hi, lo = heads[h][3]
                dve.tensor_tensor(lo, ps[0:width, 6 + h % 2, :], hi, ALU.subtract).then_inc(left, 1)

            def maximum(n):
                dve.wait_ge(score, n + 1)
                s = ps[:, 2 * (n % 2):2 * (n % 2) + 2, :].rearrange("p a b -> p (a b)")[:, 0:keys]
                dve.tensor_reduce(stat[:, n % 4, 0:1], s, AX.X, ALU.max)
                dve.drain()
                dve.tensor_scalar(stat[:, n % 4, 1:2], stat[:, n % 4, 0:1], -scale, None, ALU.mult).then_inc(shift, 1)

            maximum(0)
            for n in range(n_steps):
                normalise(n)
                if n + 1 < n_steps:
                    maximum(n + 1)
                copy_turned(n)
                if n >= NL and n % NL == 2:
                    leave(n // NL - 1)
            leave(len(heads) - 1)


def qk_prepare(env, base, q, kv, qT, kT):
    ps, ins = env.ps, env.ins
    n_q, n_k = NL * QH, NT * KVH
    with Stage(env, base) as st:
        sq = st.sb("squares", [P, NL * D])
        sq2 = st.sb("products", [P, NL * D])
        kk = st.sb("keys_twice", [P, NT, KVH * P])
        ss = st.sb("head_rms", [P, n_q + n_k])
        wq, wk = st.sb("q_weight", [P, HD]), st.sb("k_weight", [P, HD])
        cos, sin = st.sb("cos", [P, NL, HD // 2]), st.sb("sin", [P, NL, HD // 2])
        w_in, eps_in, rooted, ready = st.sem("weights_in"), st.sem("eps_in"), st.sem("rooted"), st.sem("heads_ready")
        turned, left = st.sem("turned"), st.sem("copied")
        block = st.block()
        k = kv[:, :, 0:KVH * HD]
        heads = lambda x: x.rearrange("p t (h e) -> p t h e", e=HD)

        @block.sync
        def _(sp):
            sp.dma_start(wq, ins["attn_q_norm_w"][0].partition_broadcast(P)).then_inc(w_in, 16)
            sp.dma_start(wk, ins["attn_k_norm_w"][0].partition_broadcast(P)).then_inc(w_in, 16)
            sp.dma_start(cos, ins["rope_cos"].rearrange("(t p) c -> p t c", p=P)).then_inc(w_in, 16)
            sp.dma_start(sin, ins["rope_sin"].rearrange("(t p) c -> p t c", p=P)).then_inc(w_in, 16)
            env.ring_.load_to(sp, len(env.ring_.ends) + SLOTS)

        @block.scalar
        def _(act):
            act.wait_ge(eps_in, 1)
            act.activation(ss, ss, ACT.Sqrt).then_inc(rooted, 1)

        @block.vector
        def _(dve):
            dve.wait_ge(w_in, 64)
            flat_q = flat(q)
            dve.tensor_tensor(sq, flat_q, flat_q, ALU.mult)
            s2 = sq2[:, 0:NT * KVH * HD].rearrange("p (t c) -> p t c", t=NT)
            dve.tensor_tensor(s2, k, k, ALU.mult)
            dve.drain()
            dve.tensor_reduce(ss[:, 0:n_q], sq.rearrange("p (n e) -> p n e", e=HD), AX.X, ALU.add)
            dve.tensor_reduce(ss[:, n_q:], sq2[:, 0:NT * KVH * HD].rearrange("p (n e) -> p n e", e=HD), AX.X, ALU.add)
            dve.drain()
            dve.tensor_scalar(ss, ss, 1.0 / HD, EPS, ALU.mult, ALU.add).then_inc(eps_in, 1)
            dve.wait_ge(rooted, 1)
            dve.reciprocal(ss, ss)
            dve.drain()
            for x, nt, nh, at, w in ((q, NL, QH, 0, wq), (k, NT, KVH, n_q, wk)):
                for t in range(nt):
                    xt = x[:, t, :].rearrange("p (h e) -> p h e", e=HD)
                    shape = [P, nh, HD]
                    dve.tensor_tensor(xt, xt, ss[:, at + t * nh:at + (t + 1) * nh].unsqueeze(2).broadcast_to(shape), ALU.mult)
                    dve.drain()
                    dve.tensor_tensor(xt, xt, w.unsqueeze(1).broadcast_to(shape), ALU.mult)
            dve.drain()
            half = HD // 2
            for x, nh in ((q, QH), (k, KVH)):
                for t in range(NL):
                    shape = [P, nh, half]
                    xt = x[:, t, :].rearrange("p (h e) -> p h e", e=HD)
                    lo, hi = xt[:, :, 0:half], xt[:, :, half:HD]
                    c, s = cos[:, t, :].unsqueeze(1).broadcast_to(shape), sin[:, t, :].unsqueeze(1).broadcast_to(shape)
                    a, b, d, e = (sq[:, i * nh * half:(i + 1) * nh * half].rearrange("p (h e) -> p h e", e=half) for i in range(4))
                    dve.tensor_tensor(a, lo, c, ALU.mult)
                    dve.tensor_tensor(b, hi, s, ALU.mult)
                    dve.tensor_tensor(d, hi, c, ALU.mult)
                    dve.tensor_tensor(e, lo, s, ALU.mult)
                    dve.drain()
                    dve.tensor_tensor(lo, a, b, ALU.subtract)
                    dve.tensor_tensor(hi, d, e, ALU.add)
                    dve.drain()
            for t in range(NT):
                for r in range(2):
                    dve.tensor_copy(kk[:, t, :].rearrange("p (h r e) -> p h r e", r=2, e=HD)[:, :, r, :],
                                    k[:, t, :].rearrange("p (h e) -> p h e", e=HD))
            dve.drain().then_inc(ready, 1)
            n = 0
            for j in range(QH // 2):
                dve.wait_ge(turned, n + 1)
                dve.tensor_copy(qT[:, j, :], ps[:, 2 * (n % 4), :]).then_inc(left, 1)
                n += 1
            for g in range(KVH):
                dve.wait_ge(turned, n + 1)
                b = 2 * (n % 4)
                dve.tensor_copy(kT[:, g, :], ps[:, b:b + 2, :].rearrange("p a b -> p (a b)")[:, 0:TOK]).then_inc(left, 1)
                n += 1

        @block.tensor
        def _(pe):
            pe.wait_ge(ready, 1)
            n = 0
            for src, nt, m in ((q, NL, QH // 2), (kk, NT, KVH)):
                for j in range(m):
                    if n >= 4:
                        pe.wait_ge(left, n - 3)
                    for t in range(nt):
                        tr = pe.transpose(ps[:, 2 * (n % 4) + t // 4, (t % 4) * P:(t % 4 + 1) * P], src[:, t, j * P:(j + 1) * P],
                                          env.ident[:])
                    tr.then_inc(turned, 1)
                    n += 1


def norm_rows(env, base, X, nt, weight):
    with Stage(env, base) as st:
        junk = st.sb("squares", [P, D])
        ss = st.sb("mean_square", [P, nt])
        row = st.sb("weight_rows", [P, D])
        w_in, squared, eps_in, rooted = st.sem("weight_in"), st.sem("squared"), st.sem("eps_in"), st.sem("rooted")
        block = st.block()

        @block.sync
        def _(sp):
            sp.dma_start(row, weight.partition_broadcast(P)).then_inc(w_in, 16)

        @block.scalar
        def _(act):
            for t in range(nt):
                act.drain()
                act.activation(junk, X[:, t, :], ACT.Square, scale=float(D) ** -0.5, accum_out=ss[:, t:t + 1]).then_inc(squared, 1)
            act.wait_ge(eps_in, 1)
            act.activation(ss, ss, ACT.Sqrt).then_inc(rooted, 1)

        @block.vector
        def _(dve):
            dve.wait_ge(squared, nt)
            dve.tensor_scalar(ss, ss, EPS, None, ALU.add).then_inc(eps_in, 1)
            dve.wait_ge(rooted, 1)
            dve.reciprocal(ss, ss)
            dve.drain()
            dve.wait_ge(w_in, 16)
            for t in range(nt):
                dve.scalar_tensor_tensor(X[:, t, :], X[:, t, :], ss[:, t:t + 1], row, ALU.mult, ALU.mult)


PAD3, PAD15 = TAPS2 - 1, 15


def recurrence(env, base, lx, gate, yT):
    ps, ins = env.ps, env.ins
    with Stage(env, base) as st:
        wg = st.sb("gate_blocks", [P, 2, 4 * P])
        ua = st.sb("convolved", [P, 4, LAT])
        ri = st.sb("sigmoids", [P, 2, 2, LAT])
        w2, sw2 = st.sb("w", [P, 2, LAT]), st.sb("sqrt_w", [P, 2, LAT])
        q, a = st.sb("q", [P, LAT]), st.sb("decay", [P, LAT])
        sp_ = [st.sb(f"softplus{i}", [P, 4]) for i in range(6)]
        zeroed, w_in, conv = st.sem("blocks_zeroed"), st.sem("blocks_in"), st.sem("convolved")
        neg, ex, scl = st.sem("negated"), st.sem("exponent"), st.sem("scale_ready")
        sums, sig, th, done = st.sem("gate_sums"), st.sem("sigmoids"), st.sem("tanh_sqrt"), st.sem("tile_done")
        block = st.block()

        @block.sync
        def _(sp):
            sp.wait_ge(zeroed, 1)
            for m, name in enumerate(("lru_w_a_2", "lru_w_x_2")):
                for b in range(2):
                    src = ins[name][0].rearrange("(c b) i j -> b i c j", b=2)[b]
                    dst = wg[b * 64:(b + 1) * 64, m, :].rearrange("p (c j) -> p c j", c=4)[:, :, b * 64:(b + 1) * 64]
                    sp.dma_start(dst, src).then_inc(w_in, 16)
            env.ring_.load_to(sp, len(env.ring_.ends) + SLOTS)

        @block.tensor
        def _(pe):
            pe.wait_ge(w_in, 64)
            for c in range(4):
                pe.wait_ge(conv, c + 1)
                if c >= 2:
                    pe.wait_ge(sig, c - 1)
                for m in range(2):
                    mm = pe.matmul(ps[:, 2 * (c % 2) + m, :], wg[:, m, c * P:(c + 1) * P], ua[:, c, :], start=True, stop=True)
                mm.then_inc(sums, 1)

        @block.scalar
        def _(act):
            act.wait_ge(neg, 1)
            act.activation(sp_[1], sp_[1], ACT.Exp).then_inc(ex, 1)
            act.wait_ge(scl, 1)
            for pair in ((0, 1), (2, 3)):
                for c in pair:
                    act.wait_ge(sums, c + 1)
                    if c >= 2:
                        act.wait_ge(done, c - 1)
                    act.activation(ri[:, c % 2, 0, :], ps[:, 2 * (c % 2), :], ACT.Sigmoid, bias=col(env, "lru_b_a_2", c))
                    act.activation(ri[:, c % 2, 1, :], ps[:, 2 * (c % 2) + 1, :], ACT.Sigmoid, bias=col(env, "lru_b_x_2", c))
                    act.drain().then_inc(sig, 1)
                for c in pair:
                    act.activation(w2[:, c % 2, :], ri[:, c % 2, 0, :], ACT.Tanh, scale=sp_[5][:, c:c + 1])
                act.drain()
                for c in pair:
                    act.activation(sw2[:, c % 2, :], w2[:, c % 2, :], ACT.Sqrt)
                    act.drain().then_inc(th, 1)

        @block.vector
        def _(dve):
            dve.memset(wg, 0.0).then_inc(zeroed, 1)
            at = env.col_at["lru_a_param_2"]
            v, e, s, q4, p, out = sp_
            dve.tensor_scalar(v, env.cols[:, at:at + 4], -1.0, None, ALU.mult)
            dve.drain()
            dve.scalar_tensor_tensor(e, v, -1.0, v, ALU.mult, ALU.min).then_inc(neg, 1)
            dve.tensor_scalar(v, v, 0.0, None, ALU.max)
            dve.wait_ge(ex, 1)
            log1p_steps(dve, e, s, q4, p)
            dve.scalar_tensor_tensor(v, p, 2.0, v, ALU.mult, ALU.add)
            dve.drain()
            dve.tensor_scalar(out, v, 4.0, None, ALU.mult).then_inc(scl, 1)
            for c in range(4):
                u = ua[:, c, :]
                dve.tensor_scalar(u, lx[:, c, 0:LAT], col(env, "conv_w_2", c), col(env, "conv_b_2", c), ALU.mult, ALU.add)
                for j in range(1, TAPS2):
                    dve.drain()
                    last = dve.scalar_tensor_tensor(u, lx[:, c, j:j + LAT], col(env, "conv_w_2", 4 * j + c), u, ALU.mult, ALU.add)
                last.then_inc(conv, 1)
            for c in range(4):
                u = ua[:, c, :]
                w, sw = w2[:, c % 2, :], sw2[:, c % 2, :]
                dve.wait_ge(th, c + 1)
                dve.tensor_scalar(q, w, 1.0, None, ALU.add)
                dve.tensor_scalar(a, w, -1.0, 1.0, ALU.mult, ALU.add)
                dve.drain()
                dve.reciprocal(q, q)
                dve.tensor_tensor(u, u, ri[:, c % 2, 1, :], ALU.mult)
                dve.drain()
                dve.tensor_tensor(a, a, q, ALU.mult)
                dve.scalar_tensor_tensor(q, q, 2.0, sw, ALU.mult, ALU.mult)
                dve.drain()
                dve.tensor_tensor(u, u, q, ALU.mult).then_inc(done, 1)
                dve.drain()
                dve.tensor_tensor_scan(yT[:, c, :], a, u, 0.0, ALU.mult, ALU.add)
                dve.drain()
                dve.tensor_tensor(yT[:, c, :], yT[:, c, :], gate[:, c, :], ALU.mult)


def index_masks(env, base, qi, ki, wi, mask, pl, yT):
    ps = env.ps
    heads, chunk, top_k = 8, 64, 128
    with Stage(env, base) as st:
        r = st.sb("relu", [P, 2, LAT])
        both = st.sb("scores_and_left_to_pick", [P, 2, 2, LAT])
        sc, work = both[:, 0], both[:, 1]
        both = both.rearrange("p a b c -> p (a b c)")
        sums_v = [both[:, n * (PAD15 + LAT):(n + 1) * (PAD15 + LAT)] for n in range(2)]
        top = st.sb("top8", [P, 8])
        w8 = st.sb("weights", [P, NL, heads])
        wp = st.sb("w_pool", [P, 4, P])
        sums = [st.sb(f"window_sum{i}", [P, PAD15 + LAT]) for i in range(2)]
        pooled = st.sb("pooled", [P, 4, LAT])
        cnt = st.sb("counts", [P, 4, 16])
        w_in, counted, ready, mixed = st.sem("w_in"), st.sem("counts_ready"), st.sem("pooled_by_pool"), st.sem("mixed")
        ready_v = st.sem("pooled_by_dve")
        logit, relu, used = st.sem("logits"), st.sem("relu_done"), st.sem("relu_used")
        block = st.block()
        order = [(t, h) for t in range(NL) for h in range(heads)]

        @block.sync
        def _(sp):
            sp.dma_start(wp, env.ins["w_pool_2"][0].rearrange("g c d -> c g d")).then_inc(w_in, 16)
            env.ring_.load_to(sp, len(env.ring_.ends) + SLOTS)

        @block.tensor
        def _(pe):
            for n, (t, h) in enumerate(order):
                if n >= 4:
                    pe.wait_ge(relu, n - 3)
                b = slice((h % 2) * 64, (h % 2 + 1) * 64)
                pe.matmul(ps[:, n % 4, 0:(t + 1) * P], qi[b, h // 2, t * P:(t + 1) * P], ki[b, 0:(t + 1) * P],
                          start=True, stop=True).then_inc(logit, 1)
            pe.wait_ge(w_in, 16)
            for g in range(4):
                pe.wait_ge(*((ready, g + 1) if g < 2 else (ready_v, g - 1)))
                pe.matmul(ps[:, 4 + g, :], wp[:, g, :], pooled[:, g, :], start=True, stop=True).then_inc(mixed, 1)

        def window(eng, g, sums):
            n = PAD15 + LAT
            src, step = pl[:, g, :], 1
            for r in range(g + 1):
                dst = sums[r % 2]
                eng.drain()
                eng.tensor_copy(dst[:, 0:step], src[:, 0:step])
                eng.tensor_tensor(dst[:, step:n], src[:, step:n], src[:, 0:n - step], ALU.add)
                src, step = dst, 2 * step
            eng.drain()
            eng.tensor_tensor(pooled[:, g, 0:16], src[:, PAD15:PAD15 + 16], cnt[:, g, :], ALU.mult)
            eng.tensor_tensor(pooled[:, g, 16:LAT], src[:, PAD15 + 16:n], cnt[:, g, 15:16].broadcast_to([P, LAT - 16]), ALU.mult)
            eng.drain()
            return eng.tensor_tensor(pooled[:, g, :], pooled[:, g, :], pl[:, g, PAD15:n], ALU.subtract)

        @block.gpsimd
        def _(pool):
            pool.wait_ge(counted, 1)
            for g in (0, 1):
                window(pool, g, sums).then_inc(ready, 1)

        @block.scalar
        def _(act):
            for n, (t, h) in enumerate(order):
                act.wait_ge(logit, n + 1)
                if n >= 2:
                    act.wait_ge(used, n - 1)
                act.activation(r[:, n % 2, 0:(t + 1) * P], ps[:, n % 4, 0:(t + 1) * P], ACT.Relu, scale=64 ** -0.5).then_inc(relu, 1)
            for g in range(4):
                act.wait_ge(mixed, g + 1)
                act.activation(yT[:, g, :], ps[:, 4 + g, :], ACT.Copy, scale=col(env, "pool_scale_2", g))

        @block.vector
        def _(dve):
            for g in range(4):
                dve.tensor_scalar(cnt[:, g, :], env.iota[:, 0:16], float(2 << g), None, ALU.min)
            dve.drain()
            dve.reciprocal(cnt, cnt).then_inc(counted, 1)
            for g in (2, 3):
                window(dve, g, sums_v).then_inc(ready_v, 1)
            dve.tensor_scalar(w8, wi, heads ** -0.5, None, ALU.mult)
            n = 0
            for t in range(NL):
                keys = (t + 1) * P
                s = sc[:, t % 2, 0:keys]
                dve.drain()
                for h in range(heads):
                    dve.wait_ge(relu, n + 1)
                    if h == 0:
                        dve.tensor_scalar(s, r[:, n % 2, 0:keys], w8[:, t, h:h + 1], None, ALU.mult).then_inc(used, 1)
                    else:
                        dve.scalar_tensor_tensor(s, r[:, n % 2, 0:keys], w8[:, t, h:h + 1], s, ALU.mult, ALU.add).then_inc(used, 1)
                    dve.drain()
                    n += 1
                dve.memset(sc[0:chunk, t % 2, keys - chunk:keys], NEG)
                dve.drain()
                if t == 0:
                    dve.tensor_scalar(mask[:, t, 0:keys], s, NEG / 2, -1e30, ALU.is_lt, ALU.mult)
                    continue
                a = s
                for k in range(top_k // 8):
                    b = work[:, k % 2, 0:keys]
                    dve.max(top, a)
                    dve.drain()
                    dve.match_replace(b, top, a, NEG)
                    dve.drain()
                    a = b
                dve.tensor_tensor(mask[:, t, 0:keys], a, s, ALU.is_ge)
                dve.drain()
                dve.tensor_scalar(mask[:, t, 0:keys], mask[:, t, 0:keys], -1e30, None, ALU.mult)


def merge(env, base, h, branches, acc, merged):
    ps, ring = env.ps, env.ring_
    with Stage(env, base) as st:
        gs = st.sb("gates", [P, 4, LAT])
        tmp = st.sb("gated", [P, 2, LAT])
        sig, used = st.sem("gates_ready"), st.sem("ups_used")
        cuts, m0, b0 = ring.take_cut([[(ALL_K, tile(f), 1) for f in range(4)], 4] * 6)
        first = cuts[0][0]
        views = {first + 2 * c: ring.view(first + 2 * c, KD, HALF) for c in range(6)}
        block = st.block()

        @block.sync
        def _(sp):
            ring.load_to(sp, len(ring.ends) + SLOTS)

        @block.tensor
        def _(pe):
            for c in range(6):
                dg, n = c // 3, c % 3
                for f in range(4):
                    if c >= 1:
                        pe.wait_ge(sig, 4 * (c - 1) + f + 1)
                    m = 4 * c + f
                    pe.wait_ge(ring.low_p, b0 + m + 1)
                    hi, lo = (ring.part(x, m, ALL_K, tile(f)) for x in (ring.hi, ring.lo))
                    for k in range(KD):
                        mm = products(pe, ps[:, f, :], (hi[:, k, :], lo[:, k, :]), tuple(x[:, k, :] for x in h), k == 0, k == KD - 1)
                    mm.then_inc(ring.done, 1)
                ring.wait(pe, first + 2 * c + 1)
                w = ring.view(first + 2 * c + 1, 4, HALF)
                for f in range(4):
                    if c >= 1:
                        pe.wait_ge(used, 4 * (c - 1) + f + 1)
                    for k in range(4):
                        mm = pe.matmul(ps[:, 4 + f, :], w[:, k, tile(f)], branches[n][:, k, :], start=k == 0, stop=k == 3)
                    mm.then_inc(ring.done, 1)

        @block.gpsimd
        def _(pool):
            ring.cut_rest(pool, cuts, views)

        @block.scalar
        def _(act):
            n_ = ring.cut_after(act, cuts, views, 0, m0)
            for c in range(6):
                dg, n = c // 3, c % 3
                for f in range(4):
                    act.wait_ge(ring.done, m0 + 8 * c + f + 1)
                    if c >= 1:
                        act.wait_ge(used, 4 * (c - 1) + f + 1)
                    act.activation(gs[:, f, :], ps[:, f, :], ACT.Sigmoid, bias=col(env, "b_gate_2", n * KD + dg * 4 + f)).then_inc(sig, 1)
                    n_ = ring.cut_after(act, cuts, views, n_, m0 + 8 * c + f + 1)

        @block.vector
        def _(dve):
            for c in range(6):
                dg, n = c // 3, c % 3
                for f in range(4):
                    dve.wait_ge(ring.done, m0 + 8 * c + 4 + f + 1)
                    dve.wait_ge(sig, 4 * c + f + 1)
                    m = acc[:, f, :]
                    dst = m if n == 0 else tmp[:, f % 2, :]
                    if n == 0:
                        dve.drain()
                    dve.tensor_tensor(dst, gs[:, f, :], ps[:, 4 + f, :], ALU.mult).then_inc(used, 1)
                    if n > 0:
                        dve.drain()
                        dve.tensor_tensor(m, m, tmp[:, f % 2, :], ALU.add)
                    if n == 2:
                        hi, lo = (x[:, dg * 4 + f, :] for x in merged)
                        dve.drain()
                        dve.tensor_copy(hi, m)
                        dve.drain()
                        dve.tensor_tensor(lo, m, hi, ALU.subtract)


def ffn_hidden(env, base, h, a):
    ps, ring = env.ps, env.ring_
    tiles = FF // P
    sizes = [min(4, tiles - 4 * c) for c in range(-(-tiles // 4))]
    with Stage(env, base) as st:
        sg = st.sb("silu_gate", [P, 4, LAT])
        whole = st.sbr("hidden", [P, 2, LAT], F32)
        act_s, used = st.sem("silu_done"), st.sem("ups_used")
        cuts, m0, b0 = ring.take_cut([[(ALL_K, tile(f), 1) for f in range(m)] for m in sizes for _ in range(2)])
        views = {cuts[0][0] + n: ring.view(cuts[0][0] + n, KD, sizes[n // 2] * P) for n in range(2 * len(sizes))}
        block = st.block()

        @block.sync
        def _(sp):
            ring.load_to(sp, len(ring.ends) + SLOTS)

        @block.tensor
        def _(pe):
            for c, m in enumerate(sizes):
                for part in range(2):
                    for f in range(m):
                        if c >= 1:
                            pe.wait_ge(*((act_s, 4 * (c - 1) + f + 1) if part == 0 else (used, 4 * (c - 1) + f + 1)))
                        n = 8 * c + part * m + f
                        pe.wait_ge(ring.low_p, b0 + n + 1)
                        hi, lo = (ring.part(x, n, ALL_K, tile(f)) for x in (ring.hi, ring.lo))
                        for k in range(KD):
                            mm = products(pe, ps[:, 4 * part + f, :], (hi[:, k, :], lo[:, k, :]), tuple(x[:, k, :] for x in h),
                                          k == 0, k == KD - 1)
                        mm.then_inc(ring.done, 1)

        @block.gpsimd
        def _(pool):
            ring.cut_rest(pool, cuts, views)

        @block.scalar
        def _(act):
            n = ring.cut_after(act, cuts, views, 0, m0)
            for c, m in enumerate(sizes):
                for f in range(m):
                    act.wait_ge(ring.done, m0 + 8 * c + f + 1)
                    if c >= 1:
                        act.wait_ge(used, 4 * (c - 1) + f + 1)
                    act.activation(sg[:, f, :], ps[:, f, :], ACT.Silu).then_inc(act_s, 1)
                    n = ring.cut_after(act, cuts, views, n, m0 + 8 * c + f + 1)
                for f in range(m):
                    n = ring.cut_after(act, cuts, views, n, m0 + 8 * c + m + f + 1)

        @block.vector
        def _(dve):
            for c, m in enumerate(sizes):
                for f in range(m):
                    dve.wait_ge(ring.done, m0 + 8 * c + m + f + 1)
                    dve.wait_ge(act_s, 4 * c + f + 1)
                    w, hi, lo = whole[:, f % 2, :], a[0][:, 4 * c + f, :], a[1][:, 4 * c + f, :]
                    dve.tensor_tensor(w, sg[:, f, :], ps[:, 4 + f, :], ALU.mult).then_inc(used, 1)
                    dve.drain()
                    dve.tensor_copy(hi, w)
                    dve.drain()
                    dve.tensor_tensor(lo, w, hi, ALU.subtract)


def store(env, X, out):
    with Stage(env, X_END) as st:
        stored = st.sem("stored")
        block = st.block()

        @block.sync
        def _(sp):
            sp.dma_start(out[0].rearrange("(t p) d -> p t d", p=P), X[:, 0:NL, :]).then_inc(stored, 16)
            sp.wait_ge(stored, 16)


def build(nc, ins, out):
    env = Env()
    env.nc, env.ins, env.out, env.stage, env.col_at = nc, ins, out, 0, {}

    def dram(name, shape):
        return nc.dram_tensor(name, shape, F32).ap()

    env.mod_dram = dram("mod_rows_dram", (2, 2, 6 * D))
    env.rows_dram = dram("rows_dram", (NL, P, D))
    env.z_dram = dram("z_dram", (NT, P, DI))
    env.x_dram = dram("x_dram", (NT, P, DI))
    env.b_dram = dram("b_dram", (NT, P, G * NS))
    env.bt_dram = dram("bt_dram", (P, G, TOK))
    env.ct_dram = dram("ct_dram", (P, G, TOK))

    def kview(w, cols):
        return w[:, cols].rearrange("(k p) n -> p k n", p=P)

    with ExitStack() as es:
        sb = lambda name, shape: es.enter_context(nc.sbuf_tensor(name, shape, F32))
        env.tiles, env.area_at = 0, -(-nc.sbuf_base // 32) * 32
        env.area = sb("area", [P, AREA])
        env.ring = sb("ring", [P, SLOTS, SLOT])
        env.hi = es.enter_context(nc.sbuf_tensor("weights_high", [P, CUTS, CUT], F32R))
        env.lo = es.enter_context(nc.sbuf_tensor("weights_low", [P, CUTS, CUT], F32R))
        env.cols = sb("param_columns", [P, 3 * P])
        env.ident, env.ones, env.iota = sb("identity", [P, P]), sb("ones", [P, P]), sb("iota", [P, P])
        env.ident_b = es.enter_context(nc.sbuf_tensor("identity_bf16", [P, P], BF16))
        env.mask_b = es.enter_context(nc.sbuf_tensor("order_mask", [P, 2, P], BF16))
        env.tri = sb("triangles", [P, 4, P])
        env.cond, env.modc = sb("conditions", [P, KD, 2]), sb("modulation_columns", [P, 4, 2, KD])
        env.dtb, env.zero = sb("dt_bias", [P, 2 * H]), sb("zero", [P, 8])
        env.ps = es.enter_context(nc.psum_tensor("ps", [P, 8, HALF], F32))
        env.landed = [es.enter_context(nc.semaphore(f"slot{i}_landed")) for i in range(SLOTS)]
        env.marks = es.enter_context(nc.semaphore("matmul_marks"))
        env.cut_sems = [es.enter_context(nc.semaphore(n)) for n in ("high_parts", "low_parts_by_dve", "low_parts_by_pool", "parts_used", "high_parts_by_marks")]
        banks = []
        for b in range(2):
            held = ExitStack()
            nums = [held.enter_context(nc.semaphore(f"bank{b}_{i}")).num for i in range(32)]
            banks.append((held, nums))
        env.sem_banks = [nums for _, nums in banks]
        for held, _ in banks:
            held.close()

        chunks = []
        halves = lambda w, a, b: [kview(w, slice(c, min(c + HALF, b))) for c in range(a, b, HALF)]
        chunks += halves(ins["ada_w"][0], 0, 6 * D)
        w = ins["ssd_in_w"][0]
        nx = DI + 2 * G * NS
        chunks += halves(w, 0, DI) + halves(w, DI + nx, DI + nx + 2 * H) + halves(w, DI, DI + nx)
        w = ins["ssd_out_w"][0]
        for n in range(2):
            for c in range(2):
                chunks.append(kview(w[c * D:(c + 1) * D, :], slice(n * HALF, (n + 1) * HALF)))
        def moe_chunks(layer):
            return [kview(ins[n][layer, e], slice(h * HALF, (h + 1) * HALF))
                    for e in range(E) for n in ("moe_w1", "moe_w3", "moe_w2") for h in range(2)]

        chunks += moe_chunks(0)
        chunks += halves(ins["ada_w"][1], 0, 6 * D)
        chunks += halves(ins["attn_qkv_w"][0], 0, 1536) + halves(ins["attn_out_w"][0], 0, D)
        chunks += moe_chunks(1)
        w = ins["w_in_2"][0]
        chunks += halves(w, 0, 2048) + halves(w, 2048, 2176) + halves(w, 2176, 2688) + halves(w, 2688, 2760)
        for dg in range(2):
            for n in range(3):
                a = 2760 + n * D + dg * HALF
                chunks += halves(w, a, a + HALF) + halves(ins["w_branch_2"][0, n], dg * HALF, (dg + 1) * HALF)
        chunks += halves(ins["w_out_2"][0], 0, D)
        chunks += halves(ins["w_mem_q_2"][0], 0, HALF) + halves(ins["w_mem_kv_2"][0], 0, D) + halves(ins["w_mem_o_2"][0], 0, D)
        w = ins["w_ffn_in_2"][0]
        for a in range(0, FF, HALF):
            b = min(a + HALF, FF)
            chunks += halves(w, a, b) + halves(w, FF + a, FF + b)
        w = ins["w_ffn_out_2"][0]
        for n in range(2):
            for a in range(0, FF, D):
                chunks.append(kview(w[a:min(a + D, FF), :], slice(n * HALF, (n + 1) * HALF)))
        env.ring_ = Ring(env, chunks)

        X = carve(env, 0, [P, NT, D])
        mc = lambda q, u: (lambda k: env.modc[:, q, u, k:k + 1])
        setup(env)
        modulation(env, 0)
        t = Env()
        t.dt, t.a = carve(env, 0, [P, NT, 2 * H]), carve(env, NT * 2 * H, [P, NT, 2 * H])
        base = 2 * NT * 2 * H
        t.hh, t.hl = (carve_r(env, "h_parts", base + n * KD * TOK, [P, KD, TOK]) for n in range(2))
        xin = [(i, ins["x"][0, i * P:(i + 1) * P, :]) for i in range(NL)]
        xin += [(NL + i, ins["ctx"][0, i * P:(i + 1) * P, :]) for i in range(NC)]
        b1 = base + 2 * KD * TOK
        Xt = carve(env, b1, [P, NT, D])
        norm_turn(env, b1 + NT * D, Xt, (t.hh, t.hl), [(0, NL, mc(1, 0), mc(0, 0)), (NL, NC, mc(1, 1), mc(0, 1))], load=xin)
        ssd_project(env, t, b1)
        t.y = carve(env, base, [P, NT, DI])
        ssd_scan(env, t, base + NT * DI)
        t.yT = carve(env, base + NT * DI, [P, 2 * KD, TOK])
        nw = lambda k: col(env, "ssd_norm_w", k)
        norm_turn(env, base + 2 * NT * DI, t.y, t.yT, [(0, NL, nw, None), (NL, NC, nw, None)], width=DI, token_out=t.y, ssd=True)
        md = env.mod_dram
        project_add(env, base + 2 * NT * DI, X, t.yT, 2 * KD, list(range(NT)),
                    gate=(lambda i: int(i >= NL), [md[0, 0, 2 * D:3 * D], md[0, 1, 2 * D:3 * D]]), load=xin)
        moe(env, 0, X, NT)

        modulation(env, 1)
        q, kv = carve(env, X_END, [P, NL, D]), carve(env, X_END + NL * D, [P, NT, HALF])
        at = X_END + NL * D + NT * HALF
        hp = tuple(carve_r(env, "h_parts", at + n * KD * TOK, [P, KD, TOK]) for n in range(2))
        norm_turn(env, at + 2 * KD * TOK, X, hp, [(0, NL, mc(1, 0), mc(0, 0)), (NL, NC, mc(1, 1), mc(0, 1))])
        half = slice(0, HALF)
        jobs = [(KD, HALF, tokens(hp, half, [(t_, copy_to(q[:, t_, n * HALF:(n + 1) * HALF])) for t_ in range(NL)]))
                for n in range(2)]
        jobs.append((KD, HALF, tokens(hp, half, [(t_, copy_to(kv[:, t_, :])) for t_ in range(NT)])))
        project(env, at + 2 * KD * TOK, jobs)
        qT, kT = carve(env, at, [P, QH // 2, LAT]), carve(env, at + QH // 2 * LAT, [P, KVH, TOK])
        top = at + QH // 2 * LAT + KVH * TOK
        qk_prepare(env, top, q, kv, qT, kT)
        oT = carve_r(env, "outputs_high", X_END, [P, KD, LAT]), carve_r(env, "outputs_low", top, [P, KD, LAT])
        heads = []
        for h in range(QH):
            b, g = slice((h % 2) * HD, (h % 2 + 1) * HD), h // (QH // KVH)
            vs = [kv[:, t_, KVH * HD + g * HD:KVH * HD + (g + 1) * HD] for t_ in range(NT)]
            heads.append((qT[b, h // 2, :], kT[b, g, :], vs, tuple(x[b, h // 2, :] for x in oT)))
        attend_heads(env, top + KD * LAT, heads, TOK, HD ** -0.5, HD)
        project_add(env, at, X, oT, KD, list(range(NL)), gate=(lambda i: 0, [env.mod_dram[1, 0, 2 * D:3 * D]]))
        moe(env, 1, X, NL)
        norm_rows(env, X_END, X, NL, ins["final_norm_w"])

        NLD = NL * D
        hp = tuple(carve_r(env, "h_parts", (1 + n) * NLD, [P, KD, LAT]) for n in range(2))
        norm_turn(env, 3 * NLD, X, hp, [(0, NL, lambda k: col(env, "g_mix_pre_2", k), None)])
        spent = at = 3 * NLD
        part, place = {}, {}
        for name, shape in (("lx", [P, 4, PAD3 + LAT]), ("gate", [P, 4, LAT]), ("pool", [P, 4, PAD15 + LAT]), ("q", [P, 4, LAT]),
                            ("qi", [P, 4, LAT]), ("k", [P, LAT]), ("ki", [P, LAT]), ("v", [P, NL, HD]), ("wi", [P, NL, 8]),
                            ("ya", [P, 4, LAT]), ("yb", [P, 4, LAT]), ("yc", [P, 4, LAT])):
            part[name], place[name] = carve(env, at, shape), at
            at += int(np.prod(shape[1:]))
        all_ = slice(0, LAT)

        def wide(name, pad, func=ACT.Copy):
            def copies(f):
                dst = part[name][:, f, pad:pad + LAT]

                def go(act, s):
                    if pad:
                        act.activation(part[name][:, f, 0:pad], s[:, 0:pad], ACT.Copy, scale=0.0)
                    return act.activation(dst, s, func)
                return go
            return (KD, HALF, [features(hp, tile(f), all_, copies(f)) for f in range(4)])

        def twice(dst):
            def copies(act, s):
                act.activation(dst[0:HD, :], s, ACT.Copy)
                return act.activation(dst[HD:P, :], s, ACT.Copy)
            return features(hp, slice(0, HD), all_, copies)

        jobs = [wide("lx", PAD3), wide("gate", 0, ACT.Gelu_apprx_tanh), wide("pool", PAD15), wide("q", 0)]
        jobs.append((KD, 2 * HD, [twice(part["k"])]
                     + tokens(hp, slice(HD, 2 * HD), [(t_, copy_to(part["v"][:, t_, :])) for t_ in range(NL)])))
        jobs.append(wide("qi", 0))
        jobs.append((KD, HD + 8, [twice(part["ki"])]
                     + tokens(hp, slice(HD, HD + 8), [(t_, copy_to(part["wi"][:, t_, :])) for t_ in range(NL)])))
        project(env, at, jobs)
        recurrence(env, place["yb"], part["lx"], part["gate"], part["ya"])
        mask = carve(env, spent, [P, NL, LAT])
        index_masks(env, place["yc"], part["qi"], part["ki"], part["wi"], mask, part["pool"], part["yb"])
        o = carve(env, spent + NL * LAT, [P, NL, LAT])
        steps = []
        for t_ in range(NL):
            for h in range(8):
                b, keys = slice((h % 2) * HD, (h % 2 + 1) * HD), (t_ + 1) * P
                steps.append((part["q"][b, h // 2, t_ * P:(t_ + 1) * P], part["k"][b, :], keys, mask[:, t_, 0:keys],
                              [part["v"][:, k, :] for k in range(t_ + 1)], o[:, t_, h * HD:(h + 1) * HD]))
        attend(env, place["yc"], steps, HD ** -0.5, HD)
        turn(env, at, o, part["yc"], NL, 4)
        mT = tuple(carve_r(env, "merged_parts", spent + n * NLD, [P, KD, LAT]) for n in range(2))
        merge(env, at, hp, [part["ya"], part["yb"], part["yc"]], carve(env, spent + 2 * NLD, [P, 4, LAT]), mT)
        project_add(env, 5 * NLD, X, mT, KD, list(range(NL)), norm=ins["g_mix_post_2"][0])

        NM = 2
        mem = carve(env, 3 * NLD, [P, NM, D])
        mh = tuple(carve_r(env, "memory_parts", 3 * NLD + (1 + n) * NM * D, [P, KD, NM * P]) for n in range(2))
        at = 3 * NLD + 3 * NM * D
        norm_turn(env, at, mem, mh, [(0, NM, lambda k: col(env, "g_mem_kv_2", k), None)],
                  load=[(i, ins["mem_2"][0, i * P:(i + 1) * P, :]) for i in range(NM)])
        norm_turn(env, at, X, hp, [(0, NL, lambda k: col(env, "g_mem_pre_2", k), None)])
        qT, kT, v = carve(env, at, [P, 4, LAT]), carve(env, at + 4 * LAT, [P, 4, NM * P]), carve(env, at + 6 * LAT, [P, NM, LAT])
        oT = tuple(carve_r(env, "outputs_parts", at + (8 + 4 * n) * LAT, [P, 4, LAT]) for n in range(2))
        at += 16 * LAT
        ms = slice(0, NM * P)
        project(env, at, [(KD, HALF, [features(hp, tile(f), all_, copy_to(qT[:, f, :])) for f in range(4)]),
                          (KD, HALF, [features(mh, tile(f), ms, copy_to(kT[:, f, :])) for f in range(4)]),
                          (KD, HALF, tokens(mh, half, [(t_, copy_to(v[:, t_, :])) for t_ in range(NM)]))])
        heads = [(qT[:, h, :], kT[:, h, :], [v[:, m, h * P:(h + 1) * P] for m in range(NM)], tuple(x[:, h, :] for x in oT)) for h in range(4)]
        attend_heads(env, at, heads, NM * P, P ** -0.5, P)
        project_add(env, at, X, oT, 4, list(range(NL)), norm=ins["g_mem_post_2"][0])

        norm_turn(env, 3 * NLD, X, hp, [(0, NL, lambda k: col(env, "g_ffn_pre_2", k), None)], keep=env.rows_dram)
        ah = tuple(carve_r(env, "hidden_parts", 3 * NLD + n * FF // P * LAT, [P, FF // P, LAT]) for n in range(2))
        ffn_hidden(env, 0, hp, ah)
        project_add(env, NLD, X, ah, FF // P, list(range(NL)), norm=ins["g_ffn_post_2"][0],
                    load=[(i, env.rows_dram[i, :, :]) for i in range(NL)])
        store(env, X, out)


_INS = ["x", "c", "ctx", "c_ctx", "ada_w", "ada_b", "norm1_w", "norm2_w", "ssd_in_w", "ssd_conv_w", "ssd_conv_b",
        "ssd_dt_bias", "ssd_A_log", "ssd_D", "ssd_norm_w", "ssd_out_w", "attn_qkv_w", "attn_q_norm_w",
        "attn_k_norm_w", "attn_out_w", "moe_router_w", "moe_w1", "moe_w3", "moe_w2", "final_norm_w", "mem_2",
        "g_mix_pre_2", "w_in_2", "conv_w_2", "conv_b_2", "lru_w_a_2", "lru_b_a_2", "lru_w_x_2", "lru_b_x_2",
        "lru_a_param_2", "w_pool_2", "pool_scale_2", "w_branch_2", "b_gate_2", "w_out_2", "g_mix_post_2",
        "g_mem_pre_2", "g_mem_kv_2", "w_mem_q_2", "w_mem_kv_2", "w_mem_o_2", "g_mem_post_2", "g_ffn_pre_2",
        "w_ffn_in_2", "w_ffn_out_2", "g_ffn_post_2", "rope_cos", "rope_sin"]


def rope_tables():
    row = np.repeat(np.arange(LAT // 64), 64).astype(np.float32)
    column = np.tile(np.arange(64), LAT // 64).astype(np.float32)
    freq = np.float32(10000.0) ** (-np.arange(0, 32, 2, dtype=np.float32) / np.float32(32))
    ang = np.concatenate([row[:, None] * freq, column[:, None] * freq], axis=-1)
    return {"rope_cos": np.cos(ang).astype(np.float32), "rope_sin": np.sin(ang).astype(np.float32)}


_NAMES = _INS[:-2]


def kernel(**inputs):
    import concourse.bacc as bacc
    from concourse.bass_utils import run_bass_kernel_spmd

    nc = bacc.Bacc("TRN2", target_bir_lowering=False, num_devices=1, dynamic_dma_scratch_size=64)
    arrays, ins = {}, {}
    values = {name: np.ascontiguousarray(inputs[name]) for name in _NAMES}
    values.update(rope_tables())
    for name in _INS:
        a = values[name]
        arrays[f"in_{name}"] = a
        ins[name] = nc.dram_tensor(f"in_{name}", a.shape, mybir.dt.from_np(a.dtype), kind="ExternalInput").ap()
    out = nc.dram_tensor("out", (1, LAT, D), F32, kind="ExternalOutput").ap()
    build(nc, ins, out)
    result = run_bass_kernel_spmd(nc, [arrays], core_ids=[0])
    return result.results[0]["out"]
```
